# Optimizing a Trainium2 kernel written in Bass

```python
import math
import jax
import jax.numpy as jnp
from jax import lax
import numpy as np

D_MODEL = 1024
BATCH = 1
SEQ = 1024
DEPTH = 1
DEC_BATCH = 8
DEC_SEQ = 1
PAST_LEN = 1024
PAGE_SIZE = 128

NSA_HEADS = 8
NSA_KV_HEADS = 2
HEAD_DIM = 64
NSA_GROUP = NSA_HEADS // NSA_KV_HEADS
NSA_WIDTH = NSA_HEADS * HEAD_DIM
KV_WIDTH = NSA_KV_HEADS * HEAD_DIM
CMP_BLOCK = 32
SLC_BLOCK = 64
SLC_TOPN = 16
WINDOW = 512
QUERY_BLOCK = 128
ATTN_SCALE = HEAD_DIM ** -0.5
RET_HEADS = 8
RET_KDIM = 64
RET_VDIM = 64
RET_WIDTH = RET_HEADS * RET_VDIM
RET_CHUNK = 128
ROPE_BASE = 10000.0
REL_BUCKETS = 32
REL_MAX_DIST = 1024
EPS = 1e-6
MIX_WIDTH = NSA_WIDTH + RET_WIDTH
SPLIT_WIDTHS = (NSA_WIDTH, KV_WIDTH, KV_WIDTH, KV_WIDTH, KV_WIDTH, KV_WIDTH, KV_WIDTH,
                3 * NSA_HEADS, NSA_WIDTH, RET_HEADS * RET_KDIM, RET_HEADS * RET_KDIM, RET_WIDTH, RET_WIDTH)
IN_WIDTH = sum(SPLIT_WIDTHS)
SPLIT_POINTS = tuple(int(v) for v in np.cumsum(SPLIT_WIDTHS)[:-1])

kernel_name = 'hybrid_nsa_retention_step'

def rms_norm(x, g):
    xf = x.astype(jnp.float32)
    y = xf * lax.rsqrt(jnp.mean(xf * xf, axis=-1, keepdims=True) + EPS)
    return (y * g.astype(jnp.float32)).astype(x.dtype)

def head_group_norm(o, g):
    b, t = o.shape[:2]
    of = o.astype(jnp.float32)
    mu = jnp.mean(of, axis=-1, keepdims=True)
    var = jnp.mean(jnp.square(of - mu), axis=-1, keepdims=True)
    y = ((of - mu) * lax.rsqrt(var + EPS)).reshape(b, t, -1)
    return (y * g.astype(jnp.float32)).astype(o.dtype)

def rotary(x, pos):
    half = x.shape[-1] // 2
    inv = ROPE_BASE ** (-jnp.arange(half, dtype=jnp.float32) / half)
    ang = pos.astype(jnp.float32)[:, None] * inv[None, :]
    cos = jnp.cos(ang)[None, :, None, :]
    sin = jnp.sin(ang)[None, :, None, :]
    xf = x.astype(jnp.float32)
    x1, x2 = xf[..., :half], xf[..., half:]
    return jnp.concatenate([x1 * cos - x2 * sin, x1 * sin + x2 * cos], axis=-1).astype(x.dtype)

def t5_bucket(dist):
    n = jnp.maximum(dist, 0)
    exact = REL_BUCKETS // 2
    log_ratio = jnp.log(jnp.maximum(n, 1).astype(jnp.float32) / exact) / math.log(REL_MAX_DIST / exact)
    large = jnp.minimum(exact + (log_ratio * (REL_BUCKETS - exact)).astype(jnp.int32), REL_BUCKETS - 1)
    return jnp.where(n < exact, n, large)

def masked_softmax(logits, mask):
    logits = jnp.where(mask, logits, -jnp.inf)
    m = jnp.max(logits, axis=-2, keepdims=True)
    m = jnp.where(jnp.isfinite(m), m, 0.0)
    e = jnp.exp(logits - m)
    s = jnp.sum(e, axis=-2, keepdims=True)
    return e / jnp.where(s > 0.0, s, 1.0)

def attend_shared(q, k, v, dist, valid, rel_bias):
    b, nq = q.shape[:2]
    nk = k.shape[1]
    qg = q.reshape(b, nq, NSA_KV_HEADS, NSA_GROUP, HEAD_DIM)
    bias = rel_bias[t5_bucket(dist)].reshape(nq, nk, NSA_KV_HEADS, NSA_GROUP).transpose(0, 2, 1, 3)
    logits = jnp.einsum('bqhgd,bkhd->bqhkg', qg, k).astype(jnp.float32) * ATTN_SCALE + bias.astype(jnp.float32)[None]
    p = masked_softmax(logits, valid[None, :, None, :, None])
    o = jnp.einsum('bqhkg,bkhd->bqhgd', p.astype(v.dtype), v)
    return o.reshape(b, nq, NSA_HEADS, HEAD_DIM), p

def attend_gathered(q, k, v, dist, valid, rel_bias):
    b, nq = q.shape[:2]
    qg = q.reshape(b, nq, NSA_KV_HEADS, NSA_GROUP, HEAD_DIM)
    table = rel_bias.reshape(REL_BUCKETS, NSA_KV_HEADS, NSA_GROUP).transpose(1, 0, 2)
    h_idx = jnp.arange(NSA_KV_HEADS)[None, None, :, None]
    bias = table[h_idx, t5_bucket(dist)]
    logits = jnp.einsum('bqhgd,bqhrd->bqhrg', qg, k).astype(jnp.float32) * ATTN_SCALE + bias.astype(jnp.float32)
    p = masked_softmax(logits, valid[..., None])
    o = jnp.einsum('bqhrg,bqhrd->bqhgd', p.astype(v.dtype), v)
    return o.reshape(b, nq, NSA_HEADS, HEAD_DIM), p

def compress(rows, pe, w1, w2):
    b, l, h, d = rows.shape
    nc = l // CMP_BLOCK
    blocks = rows.reshape(b, nc, CMP_BLOCK, h, d) + pe[None, None, :, None, :]
    flat = blocks.transpose(0, 1, 3, 2, 4).reshape(b, nc, h, CMP_BLOCK * d)
    return jax.nn.silu(flat @ w1) @ w2

def select_blocks(p_cmp, qpos, n_slc):
    b, nq, h, nc, _ = p_cmp.shape
    ratio = SLC_BLOCK // CMP_BLOCK
    imp = jnp.sum(p_cmp, axis=-1)
    imp = jnp.pad(imp, ((0, 0), (0, 0), (0, 0), (0, n_slc * ratio - nc))).reshape(b, nq, h, n_slc, ratio).sum(-1)
    j = jnp.arange(n_slc)[None, :]
    cur = (qpos // SLC_BLOCK)[:, None]
    valid = j <= cur
    forced = (j == 0) | (j == cur) | (j == cur - 1)
    score = jnp.where(valid[None, :, None, :], jnp.where(forced[None, :, None, :], jnp.inf, imp), -jnp.inf)
    top, idx = lax.top_k(score, min(SLC_TOPN, n_slc))
    return idx, top > -jnp.inf

def nsa_combine(gates, o_c, o_s, o_w):
    return gates[..., 0:1] * o_c + gates[..., 1:2] * o_s + gates[..., 2:3] * o_w

def project(x, pos, norm_g, w_in, q_norm_g, k_norm_g):
    b, t = x.shape[:2]
    parts = jnp.split(rms_norm(x, norm_g) @ w_in, SPLIT_POINTS, axis=-1)
    kv = lambda a: a.reshape(b, t, NSA_KV_HEADS, HEAD_DIM)
    q = rms_norm(parts[0].reshape(b, t, NSA_HEADS, HEAD_DIM), q_norm_g)
    k_cmp, v_cmp = kv(parts[1]), kv(parts[2])
    k_slc, v_slc = rms_norm(kv(parts[3]), k_norm_g), kv(parts[4])
    k_win, v_win = rms_norm(kv(parts[5]), k_norm_g), kv(parts[6])
    gates = jax.nn.sigmoid(parts[7].reshape(b, t, NSA_HEADS, 3))
    q_r = rotary(parts[9].reshape(b, t, RET_HEADS, RET_KDIM), pos)
    k_r = rotary(parts[10].reshape(b, t, RET_HEADS, RET_KDIM), pos) * (RET_KDIM ** -0.5)
    v_r = parts[11].reshape(b, t, RET_HEADS, RET_VDIM)
    return (q, k_cmp, v_cmp, k_slc, v_slc, k_win, v_win, gates, parts[8], q_r, k_r, v_r, parts[12])

def nsa_prompt(q, k_cmp, v_cmp, k_slc, v_slc, k_win, v_win, gates, k_norm_g,
               cmp_pe_k, cmp_w1_k, cmp_w2_k, cmp_pe_v, cmp_w1_v, cmp_w2_v, rel_bias):
    b, t = q.shape[:2]
    ck = rms_norm(compress(k_cmp, cmp_pe_k, cmp_w1_k, cmp_w2_k), k_norm_g)
    cv = compress(v_cmp, cmp_pe_v, cmp_w1_v, cmp_w2_v)
    cend = jnp.arange(ck.shape[1]) * CMP_BLOCK + (CMP_BLOCK - 1)
    n_slc = t // SLC_BLOCK

    def to_blocks(a):
        return a.reshape(b, n_slc, SLC_BLOCK, NSA_KV_HEADS, HEAD_DIM).transpose(0, 3, 1, 2, 4)

    kb, vb = to_blocks(k_slc), to_blocks(v_slc)
    pad = ((0, 0), (WINDOW, 0), (0, 0), (0, 0))
    kw_pad, vw_pad = jnp.pad(k_win, pad), jnp.pad(v_win, pad)
    b_idx = jnp.arange(b)[:, None, None, None]
    h_idx = jnp.arange(NSA_KV_HEADS)[None, None, :, None]
    offs = jnp.arange(SLC_BLOCK)

    def block(qb):
        t0 = qb * QUERY_BLOCK
        qpos = t0 + jnp.arange(QUERY_BLOCK)
        qblk = lax.dynamic_slice_in_dim(q, t0, QUERY_BLOCK, axis=1)
        gblk = lax.dynamic_slice_in_dim(gates, t0, QUERY_BLOCK, axis=1)
        o_c, p_c = attend_shared(qblk, ck, cv, qpos[:, None] - cend[None, :], cend[None, :] <= qpos[:, None], rel_bias)
        idx, ok = select_blocks(p_c, qpos, n_slc)
        kpos = idx[..., None] * SLC_BLOCK + offs
        valid = (ok[..., None] & (kpos <= qpos[None, :, None, None, None])).reshape(b, QUERY_BLOCK, NSA_KV_HEADS, -1)
        kpos = kpos.reshape(b, QUERY_BLOCK, NSA_KV_HEADS, -1)
        kg = kb[b_idx, h_idx, idx].reshape(b, QUERY_BLOCK, NSA_KV_HEADS, -1, HEAD_DIM)
        vg = vb[b_idx, h_idx, idx].reshape(b, QUERY_BLOCK, NSA_KV_HEADS, -1, HEAD_DIM)
        o_s, _ = attend_gathered(qblk, kg, vg, qpos[None, :, None, None] - kpos, valid, rel_bias)
        wpos = t0 - WINDOW + jnp.arange(WINDOW + QUERY_BLOCK)
        kw = lax.dynamic_slice_in_dim(kw_pad, t0, WINDOW + QUERY_BLOCK, axis=1)
        vw = lax.dynamic_slice_in_dim(vw_pad, t0, WINDOW + QUERY_BLOCK, axis=1)
        dist = qpos[:, None] - wpos[None, :]
        wvalid = (wpos[None, :] >= 0) & (dist >= 0) & (dist < WINDOW)
        o_w, _ = attend_shared(qblk, kw, vw, dist, wvalid, rel_bias)
        return nsa_combine(gblk, o_c, o_s, o_w)

    out = lax.map(block, jnp.arange(t // QUERY_BLOCK))
    return out.transpose(1, 0, 2, 3, 4).reshape(b, t, NSA_HEADS, HEAD_DIM)

def nsa_sample(q, k_cmp, v_cmp, k_slc, v_slc, k_win, v_win, gates,
               cache_cmp_k, cache_cmp_v, cache_slc_k, cache_slc_v, cache_win_k, cache_win_v,
               page_table, k_norm_g, cmp_pe_k, cmp_w1_k, cmp_w2_k, cmp_pe_v, cmp_w1_v, cmp_w2_v, rel_bias):
    b, s = q.shape[:2]
    n_pages = page_table.shape[1]
    page = cache_cmp_k.shape[1]
    past = n_pages * page
    total = past + s
    qpos = past + jnp.arange(s)

    def past_rows(pool):
        return pool[page_table].reshape(b, past, NSA_KV_HEADS, HEAD_DIM)

    nc = total // CMP_BLOCK
    kc_all = jnp.concatenate([past_rows(cache_cmp_k), k_cmp], axis=1)[:, :nc * CMP_BLOCK]
    vc_all = jnp.concatenate([past_rows(cache_cmp_v), v_cmp], axis=1)[:, :nc * CMP_BLOCK]
    ck = rms_norm(compress(kc_all, cmp_pe_k, cmp_w1_k, cmp_w2_k), k_norm_g)
    cv = compress(vc_all, cmp_pe_v, cmp_w1_v, cmp_w2_v)
    cend = jnp.arange(nc) * CMP_BLOCK + (CMP_BLOCK - 1)
    o_c, p_c = attend_shared(q, ck, cv, qpos[:, None] - cend[None, :], cend[None, :] <= qpos[:, None], rel_bias)
    n_slc = -(-total // SLC_BLOCK)
    idx, ok = select_blocks(p_c, qpos, n_slc)
    kpos = idx[..., None] * SLC_BLOCK + jnp.arange(SLC_BLOCK)
    valid = (ok[..., None] & (kpos <= qpos[None, :, None, None, None])).reshape(b, s, NSA_KV_HEADS, -1)
    kpos = kpos.reshape(b, s, NSA_KV_HEADS, -1)
    b_idx = jnp.arange(b)[:, None, None, None]
    h_idx = jnp.arange(NSA_KV_HEADS)[None, None, :, None]
    in_past = (kpos < past)[..., None]
    phys = page_table[b_idx, jnp.minimum(kpos // page, n_pages - 1)] * page + kpos % page
    new_i = jnp.clip(kpos - past, 0, s - 1)

    def gather_rows(pool, new):
        flat = pool.reshape(-1, NSA_KV_HEADS, HEAD_DIM)
        return jnp.where(in_past, flat[phys, h_idx], new[b_idx, new_i, h_idx])

    o_s, _ = attend_gathered(q, gather_rows(cache_slc_k, k_slc), gather_rows(cache_slc_v, v_slc),
                             qpos[None, :, None, None] - kpos, valid, rel_bias)
    wb = cache_win_k.shape[1]
    kw_all = jnp.concatenate([cache_win_k, k_win], axis=1)
    vw_all = jnp.concatenate([cache_win_v, v_win], axis=1)
    wpos = past - wb + jnp.arange(wb + s)
    dist = qpos[:, None] - wpos[None, :]
    wvalid = (dist >= 0) & (dist < WINDOW)
    o_w, _ = attend_shared(q, kw_all, vw_all, dist, wvalid, rel_bias)
    keep = min(WINDOW, wb + s)
    return nsa_combine(gates, o_c, o_s, o_w), kw_all[:, -keep:], vw_all[:, -keep:]

def retention_chunk(state, q, k, v):
    c = q.shape[1]
    log_g = jnp.log1p(-jnp.exp2(-5.0 - jnp.arange(RET_HEADS, dtype=jnp.float32)))
    i = jnp.arange(c, dtype=jnp.float32)
    diff = i[:, None] - i[None, :]
    decay = jnp.where(diff >= 0, jnp.exp(jnp.maximum(diff, 0.0)[None] * log_g[:, None, None]), 0.0).astype(q.dtype)
    scores = jnp.einsum('bihd,bjhd->bhij', q, k) * decay[None]
    o = jnp.einsum('bhij,bjhv->bihv', scores, v)
    q_decay = jnp.exp((i[:, None] + 1.0) * log_g[None, :]).astype(q.dtype)
    o = o + jnp.einsum('bihd,bhdv->bihv', q, state) * q_decay[None, :, :, None]
    k_decay = jnp.exp((c - 1.0 - i)[:, None] * log_g[None, :]).astype(k.dtype)
    new_state = state * jnp.exp(c * log_g).astype(state.dtype)[None, :, None, None] \
        + jnp.einsum('bjhd,bjhv->bhdv', k * k_decay[None, :, :, None], v)
    return o, new_state

def retention_prompt(q, k, v):
    b, t = q.shape[:2]
    n = t // RET_CHUNK

    def to_chunks(a):
        return a.reshape(b, n, RET_CHUNK, RET_HEADS, a.shape[-1]).transpose(1, 0, 2, 3, 4)

    def step(state, chunk):
        o, new_state = retention_chunk(state, chunk[0], chunk[1], chunk[2])
        return new_state, o

    state0 = jnp.zeros((b, RET_HEADS, RET_KDIM, RET_VDIM), q.dtype)
    final, o = lax.scan(step, state0, (to_chunks(q), to_chunks(k), to_chunks(v)))
    return o.transpose(1, 0, 2, 3, 4).reshape(b, t, RET_HEADS, RET_VDIM), final

def mix_output(x, o_nsa, z_nsa, o_ret, z_ret, ret_gn_g, w_out):
    b, t = x.shape[:2]
    y_nsa = o_nsa.reshape(b, t, NSA_WIDTH) * jax.nn.silu(z_nsa)
    y_ret = head_group_norm(o_ret, ret_gn_g) * jax.nn.silu(z_ret)
    return x + jnp.concatenate([y_nsa, y_ret], axis=-1) @ w_out

def setup_inputs(seed: int = 0) -> dict:
    key = jax.random.key(seed)
    ks = jax.random.split(key, 24)
    n_pages = PAST_LEN // PAGE_SIZE
    n_phys = (DEC_BATCH * n_pages * 5) // 4
    win_buf = min(WINDOW, PAST_LEN)
    nrm = lambda k, shape, scale: jax.random.normal(k, shape, jnp.float32) * scale
    pool = (n_phys, PAGE_SIZE, NSA_KV_HEADS, HEAD_DIM)
    flat_in = CMP_BLOCK * HEAD_DIM
    return {
        'x_prompt': nrm(ks[0], (BATCH, SEQ, D_MODEL), 1.0),
        'x_sample': nrm(ks[1], (DEC_BATCH, DEC_SEQ, D_MODEL), 1.0),
        'cache_cmp_k': nrm(ks[2], pool, 1.0),
        'cache_cmp_v': nrm(ks[3], pool, 1.0),
        'cache_slc_k': nrm(ks[4], pool, 1.0),
        'cache_slc_v': nrm(ks[5], pool, 1.0),
        'cache_win_k': nrm(ks[6], (DEC_BATCH, win_buf, NSA_KV_HEADS, HEAD_DIM), 1.0),
        'cache_win_v': nrm(ks[7], (DEC_BATCH, win_buf, NSA_KV_HEADS, HEAD_DIM), 1.0),
        'state_ret': nrm(ks[8], (DEC_BATCH, RET_HEADS, RET_KDIM, RET_VDIM), 1.0),
        'page_table': jax.random.permutation(ks[9], n_phys)[:DEC_BATCH * n_pages].reshape(DEC_BATCH, n_pages).astype(jnp.int32),
        'norm_g': 1.0 + nrm(ks[10], (D_MODEL,), 0.02),
        'w_in': nrm(ks[11], (D_MODEL, IN_WIDTH), D_MODEL ** -0.5),
        'q_norm_g': 1.0 + nrm(ks[12], (HEAD_DIM,), 0.02),
        'k_norm_g': 1.0 + nrm(ks[13], (HEAD_DIM,), 0.02),
        'cmp_pe_k': nrm(ks[14], (CMP_BLOCK, HEAD_DIM), 0.1),
        'cmp_w1_k': nrm(ks[15], (flat_in, HEAD_DIM), flat_in ** -0.5),
        'cmp_w2_k': nrm(ks[16], (HEAD_DIM, HEAD_DIM), HEAD_DIM ** -0.5),
        'cmp_pe_v': nrm(ks[17], (CMP_BLOCK, HEAD_DIM), 0.1),
        'cmp_w1_v': nrm(ks[18], (flat_in, HEAD_DIM), flat_in ** -0.5),
        'cmp_w2_v': nrm(ks[19], (HEAD_DIM, HEAD_DIM), HEAD_DIM ** -0.5),
        'rel_bias': nrm(ks[20], (REL_BUCKETS, NSA_HEADS), 0.5),
        'ret_gn_g': 1.0 + nrm(ks[21], (RET_WIDTH,), 0.02),
        'w_out': nrm(ks[22], (MIX_WIDTH, D_MODEL), MIX_WIDTH ** -0.5),
    }

def reference(x_prompt, x_sample, cache_cmp_k, cache_cmp_v, cache_slc_k, cache_slc_v,
              cache_win_k, cache_win_v, state_ret, page_table, norm_g, w_in, q_norm_g, k_norm_g,
              cmp_pe_k, cmp_w1_k, cmp_w2_k, cmp_pe_v, cmp_w1_v, cmp_w2_v, rel_bias, ret_gn_g, w_out):
    past = page_table.shape[1] * cache_cmp_k.shape[1]
    y_prompt, y_sample = x_prompt, x_sample
    for _ in range(DEPTH):
        (q, kc, vc, ksl, vsl, kw, vw, g, zn, qr, kr, vr, zr) = project(
            y_prompt, jnp.arange(y_prompt.shape[1]), norm_g, w_in, q_norm_g, k_norm_g)
        o_nsa = nsa_prompt(q, kc, vc, ksl, vsl, kw, vw, g, k_norm_g,
                           cmp_pe_k, cmp_w1_k, cmp_w2_k, cmp_pe_v, cmp_w1_v, cmp_w2_v, rel_bias)
        o_ret, p_ret = retention_prompt(qr, kr, vr)
        keep = min(WINDOW, kw.shape[1])
        p_cmp_k, p_cmp_v, p_slc_k, p_slc_v = kc, vc, ksl, vsl
        p_win_k, p_win_v = kw[:, -keep:], vw[:, -keep:]
        y_prompt = mix_output(y_prompt, o_nsa, zn, o_ret, zr, ret_gn_g, w_out)
        (q, kc, vc, ksl, vsl, kw, vw, g, zn, qr, kr, vr, zr) = project(
            y_sample, past + jnp.arange(y_sample.shape[1]), norm_g, w_in, q_norm_g, k_norm_g)
        o_nsa, s_win_k, s_win_v = nsa_sample(
            q, kc, vc, ksl, vsl, kw, vw, g, cache_cmp_k, cache_cmp_v, cache_slc_k, cache_slc_v,
            cache_win_k, cache_win_v, page_table, k_norm_g,
            cmp_pe_k, cmp_w1_k, cmp_w2_k, cmp_pe_v, cmp_w1_v, cmp_w2_v, rel_bias)
        o_ret, s_ret = retention_chunk(state_ret, qr, kr, vr)
        s_cmp_k, s_cmp_v, s_slc_k, s_slc_v = kc, vc, ksl, vsl
        y_sample = mix_output(y_sample, o_nsa, zn, o_ret, zr, ret_gn_g, w_out)
    return (y_prompt, y_sample, p_cmp_k, p_cmp_v, p_slc_k, p_slc_v, p_win_k, p_win_v, p_ret,
            s_cmp_k, s_cmp_v, s_slc_k, s_slc_v, s_win_k, s_win_v, s_ret)


_drawn_inputs = setup_inputs


def setup_inputs(seed=0):
    import zlib

    import numpy as np

    out = dict(_drawn_inputs(seed))
    spreads = {}
    factors = {'cache_slc_k': 6.616,
     'cache_slc_v': 5.36,
     'q_norm_g': 8.0,
     'k_norm_g': 2.808,
     'cmp_pe_k': 8.0,
     'cmp_pe_v': 6.726,
     'rel_bias': 2.704,
     'ret_gn_g': 7.542}
    for name, (base, spread) in spreads.items():
        noise = np.random.default_rng([zlib.crc32(name.encode()), seed]).standard_normal(out[name].shape)
        drawn = base * np.exp(spread * noise) if base else spread * noise
        out[name] = jnp.asarray(drawn.astype(out[name].dtype))
    for name, factor in factors.items():
        out[name] = (out[name] * factor).astype(out[name].dtype)
    return out
```

```python
import math
from contextlib import ExitStack

import numpy as np
import concourse.bass as bass
from concourse import mybir
from concourse.alu_op_type import AluOpType as ALU

ACT = mybir.ActivationFunctionType
AX = mybir.AxisListType.X
F32 = mybir.dt.float32
F32R = mybir.dt.float32r
I32 = mybir.dt.int32

P = 128
D = 1024
T = 1024
TT = T // P
NT = TT + 1
B = 8
ROWS = T + B
KT = D // P
H, HKV, G, HD = 8, 2, 4, 64
KVW = HKV * HD
PAGES = 8
N_PHYS = 80
WIN = 512
EPS = 1e-6
MASK = -1e30
FLOOR = -1e29
C_Q, C_KV, C_WG, C_ZN, C_QR, C_KR, C_VR, C_ZR = 0, 512, 1024, 1304, 1816, 2328, 2840, 3352
GROUPS = [("qr", C_QR, 512), ("kr", C_KR, 512), ("vr", C_VR, 512), ("zr", C_ZR, 512),
          ("zn", C_ZN, 512), ("wg", C_WG, 280), ("kv", C_KV, 512), ("q", C_Q, 512)]
KIND = [g[0] for g in GROUPS]
NG = len(GROUPS)

CB = 32
NBP = T // CB
NBS = B * NBP

L_FULL, L_SLC, L_SWIN, L_SCMP = T + P, T, WIN, NBP
O_FULL, O_SLC = 0, L_FULL
L_SKEW = P * (L_FULL + 1) + T
O_SWIN = O_SLC + L_SLC
O_SCMP = O_SWIN + L_SWIN
O_NEW = O_SCMP + L_SCMP
L_SAMPLE = L_SLC + L_SWIN + L_SCMP + 1
L_TABLE = O_NEW + 32
N_HOT = -(-L_TABLE // 512)

S_KDEC, S_GAM128, S_GAM1, S_HALF, S_SEL = 0, 8, 16, 24, 32
S_WIDTH = 64


def rows_of(t):
    return P if t < TT else B


def view(ap, *dims):
    return bass.AP(ap.tensor, ap.offset, [list(ap.ap[0])] + [list(d) for d in dims])


def dram(ap, offset, *dims):
    return bass.AP(ap.tensor, ap.offset + offset, [list(d) for d in dims])


def f32(ap):
    return ap.bitcast(F32)


class Chain:

    def __init__(self, engine, semaphore):
        self.engine, self.semaphore, self.n = engine, semaphore, 0

    def step(self, instruction):
        self.n += 1
        instruction.then_inc(self.semaphore, 1)
        return self.n

    def sync(self, n=None):
        self.engine.wait_ge(self.semaphore, n or self.n)


class Memory:

    def __init__(self, nc, at):
        self.nc, self.at = nc, at

    def put(self, name, shape, dtype=F32):
        size = (4 * int(np.prod(shape[1:])) + 31) // 32 * 32
        tensor = self.nc.alloc_sbuf_tensor_at(name, list(shape), dtype, offset=self.at)
        self.at += size
        return tensor


class Shared:

    def __init__(self, nc):
        self.nc, self.semaphores = nc, []

    def semaphore(self, name):
        self.semaphores.append(self.nc.alloc_semaphore(name=name))
        return self.semaphores[-1]


def between(nc, s):
    nc.all_engine_barrier()
    nc.clear_and_free_semaphores(s.semaphores)
    s.semaphores = []
    nc.all_engine_barrier()


def layout(nc, s):
    m = Memory(nc, 16512)
    s.ident = m.put("ident", [P, P])
    s.small = m.put("small", [P, S_WIDTH])
    s.gates = m.put("gates", [P, NT, 24])
    s.gain = m.put("gain", [P, 4])
    s.knew = m.put("knew", [P, 2, B])
    s.vnew = m.put("vnew", [P, 2, KVW])
    s.qfull = m.put("qfull", [P, B, H])
    m.at = 16512 + 3 * 1024
    s.kh = m.put("k_high", [P, 2, HKV, T], F32R)
    s.k_region = 16512 + 3 * 1024
    s.kl = m.put("k_low", [P, 2, HKV, T], F32R)
    s.v = m.put("v_nat", [P, 2, TT, KVW])
    s.rq_region = m.at
    s.qs = m.put("q_stack", [P, H, T], F32R)
    m.at = s.rq_region
    s.qr = m.put("q_ret", [P, NT, 512])
    s.kr = m.put("k_ret", [P, NT, 512])
    s.kct_region = m.at
    s.kct = m.put("kct", [P, 2, T])
    s.x_region = m.at
    s.xh = m.put("x_high", [P, KT, ROWS], F32R)
    s.xl = m.put("x_low", [P, KT, ROWS], F32R)
    s.w_region = m.at
    s.wraw = m.put("w_raw", [P, KT, 512])
    s.wh = m.put("w_high", [P, KT, 512], F32R)
    s.wl = m.put("w_low", [P, KT, 512], F32R)
    s.st_region = m.at
    s.st = m.put("stage", [P, 2, 512])
    s.sq = m.put("squares", [P, 512])
    s.stat = m.put("stats", [P, 64])
    assert m.at <= 229368, m.at


def normalise_x(nc, s, io):
    m = Memory(nc, s.k_region)
    xt = m.put("x_tile", [P, 2, D])
    gain = m.put("norm_gain", [P, D])
    junk = m.put("x_squares", [P, D])
    relx = m.put("rel_bias_masked", [33, H])
    hot = m.put("one_hot", [33, L_TABLE])
    tab = m.put("bias_table", [H, L_TABLE])
    with ExitStack() as ctx:
        sem = s.semaphore
        x_in = [sem("x_in0"), sem("x_in1")]
        const_in, ident_ready, sum_ready, mean_ready, root_ready = (
            sem("const_in"), sem("ident_ready"), sem("sum_ready"), sem("mean_ready"), sem("root_ready"))
        norm_ready, turned, high_ready, low_ready = (
            sem("norm_ready"), sem("turned"), sem("high_ready"), sem("low_ready"))
        own_steps = sem("x_own_steps")
        hot_in, mask_set, tab_out, tab_kept, tab_stored = sem("one_hot_in"), sem("mask_set"), sem("tab_out"), sem("tab_kept"), sem("tab_stored")
        block = ctx.enter_context(nc.Block())

        @block.sync
        def _(sp):
            for t in range(NT):
                if t >= 2:
                    sp.wait_ge(turned, 2 * (t - 1))
                src = io["xp"][P * t:P * t + P, :] if t < TT else io["xs"]
                sp.dma_start(xt[0:rows_of(t), t % 2, :], src).then_inc(x_in[t % 2], 16)
                if t == 0:
                    sp.dma_start(gain[:], dram(io["norm_g"], 0, [0, P], [1, D])).then_inc(const_in, 16)
                    sp.dma_start(s.small[:], io["c_small"]).then_inc(const_in, 16)
                    for half in range(2):
                        at = slice(HD * half, HD * half + HD)
                        sp.dma_start(s.gain[at, 0:1], dram(io["q_norm_g"], 0, [1, HD], [1, 1])).then_inc(const_in, 16)
                        sp.dma_start(s.gain[at, 1:2], dram(io["k_norm_g"], 0, [1, HD], [1, 1])).then_inc(const_in, 16)

            sp.wait_ge(tab_kept, N_HOT)
            sp.dma_start(io["table"], tab[:]).then_inc(tab_stored, 16)
            sp.wait_ge(tab_stored, 16)

        @block.gpsimd
        def _(pool):
            nc.gpsimd.memset(relx[32:33, :], MASK).then_inc(mask_set, 1)
            pool.wait_ge(mask_set, 1)
            nc.gpsimd.memset(s.ident[:], 0.0).then_inc(ident_ready, 1)
            pool.wait_ge(ident_ready, 1)
            nc.gpsimd.affine_select(out=s.ident[:], in_=s.ident[:], compare_op=ALU.not_equal, fill=1.0, base=0,
                                    pattern=[[-1, P]], channel_multiplier=1).then_inc(ident_ready, 1)
            pool.wait_ge(const_in, 96)
            for t in range(NT):
                n = rows_of(t)
                pool.wait_ge(mean_ready, t + 1)
                nc.gpsimd.tensor_tensor(s.stat[0:n, 16 + t:17 + t], s.stat[0:n, 16 + t:17 + t],
                                        s.small[0:n, S_HALF:S_HALF + 1], ALU.pow).then_inc(root_ready, 1)

        @block.scalar
        def _(act):
            act.dma_start(relx[0:32, :], io["rel_bias"]).then_inc(hot_in, 16)
            act.dma_start(hot[:], io["c_hot"]).then_inc(hot_in, 16)
            for t in range(NT):
                n = rows_of(t)
                act.wait_ge(x_in[t % 2], 16 * (t // 2 + 1))
                if t >= 1:
                    act.wait_ge(sum_ready, t)
                nc.scalar.activation(junk[0:n, :], xt[0:n, t % 2, :], ACT.Square,
                                     accum_out=s.stat[0:n, t:t + 1]).then_inc(sum_ready, 1)
                for half in range(2):
                    i = 2 * t + half
                    act.wait_ge(turned, i + 1)
                    nc.scalar.activation(s.xh[:, 4 * half:4 * half + 4, P * t:P * t + n],
                                         view(s.ps[:, i % 4, 0:1], [P, 4], [1, n]), ACT.Copy).then_inc(high_ready, 1)

        @block.vector
        def _(dve):
            own = Chain(dve, own_steps)
            dve.wait_ge(const_in, 96)
            own.step(nc.vector.tensor_scalar(s.gain[:, 0:1], s.gain[:, 0:1], HD ** -0.5, None, ALU.mult))
            for t in range(NT):
                n = rows_of(t)
                dve.wait_ge(sum_ready, t + 1)
                nc.vector.tensor_scalar(s.stat[0:n, 16 + t:17 + t], s.stat[0:n, t:t + 1], 1.0 / D, EPS,
                                        ALU.mult, ALU.add).then_inc(mean_ready, 1)
                dve.wait_ge(root_ready, t + 1)
                x = xt[0:n, t % 2, :]
                nc.vector.scalar_tensor_tensor(x, x, s.stat[0:n, 16 + t:17 + t], gain[0:n, :],
                                               ALU.mult, ALU.mult).then_inc(norm_ready, 1)
                for half in range(2):
                    i = 2 * t + half
                    dve.wait_ge(high_ready, i + 1)
                    cols = (slice(None), slice(4 * half, 4 * half + 4), slice(P * t, P * t + n))
                    nc.vector.tensor_tensor(s.xl[cols], view(s.ps[:, i % 4, 0:1], [P, 4], [1, n]), f32(s.xh[cols]),
                                            ALU.subtract).then_inc(low_ready, 1)
                if t < N_HOT:
                    dve.wait_ge(tab_out, t + 1)
                    w = min(512, L_TABLE - 512 * t)
                    nc.vector.tensor_copy(tab[:, 512 * t:512 * t + w], s.ps[0:H, 6 + t % 2, 0:w]).then_inc(tab_kept, 1)
            dve.wait_ge(low_ready, 2 * NT)

        @block.tensor
        def _(pe):
            pe.wait_ge(ident_ready, 2)
            for t in range(NT):
                n = rows_of(t)
                pe.wait_ge(norm_ready, t + 1)
                for half in range(2):
                    i = 2 * t + half
                    if i >= 4:
                        pe.wait_ge(low_ready, i - 3)
                    for j in range(4):
                        k = 4 * half + j
                        last = nc.tensor.transpose(s.ps[:, i % 4, P * j:P * j + n],
                                                   xt[0:n, t % 2, P * k:P * k + P], s.ident[0:n, 0:n])
                    last.then_inc(turned, 1)
                if t < N_HOT:
                    if t == 0:
                        pe.wait_ge(hot_in, 32)
                        pe.wait_ge(mask_set, 1)
                    if t >= 2:
                        pe.wait_ge(tab_kept, t - 1)
                    w = min(512, L_TABLE - 512 * t)
                    nc.tensor.matmul(s.ps[0:H, 6 + t % 2, 0:w], relx[:], hot[:, 512 * t:512 * t + w], start=True, stop=True).then_inc(tab_out, 1)


def stores_of(kind, t):
    if kind == "zr" or kind == "zn":
        return 1
    if kind == "wg":
        return 2 if t >= TT - WIN // P else 0
    return 4 if kind == "kv" else 0


def project(nc, s, io):
    m = Memory(nc, s.k_region)
    rope = m.put("rope", [P, 2, NT, HD])
    dec = m.put("decay", [P, H, P])
    qdec = m.put("q_decay", [P, 4, P])
    gn = m.put("gn_gain", [P, 512])
    rot = m.put("rotated", [P, 2, 512])
    qt = m.put("qt", [P, 4, P])
    qdt = m.put("qt_decayed", [P, 4, P])
    ktz = m.put("kt_zeroed", [P, H, P])
    scd = m.put("scores", [P, H, P])
    kd = m.put("k_decayed", [P, 512])
    state = m.put("state", [P, H, HD])
    faded = m.put("state_faded", [P, H, HD])
    cen = m.put("centred", [P, 512])
    vr = Memory(nc, s.kct_region).put("v_ret", [P, 2, 512])
    assert m.at <= s.rq_region
    m.at = s.k_region
    last = Memory(nc, s.st_region + 4096 + 2048 + 256)
    kgain = last.put("k_gain", [P, HD])
    pet = last.put("pe_t", [P, 2, 32])
    assert last.at <= 229368
    qd = Memory(nc, s.w_region).put("q_doubled", [P, 2, D])
    n_idx = NG * NT
    G_ = {k: KIND.index(k) for k in KIND}
    kind_of = lambda i: KIND[i // NT]
    stored = [[0, 0]]
    for i in range(n_idx):
        c = list(stored[-1])
        c[i % 2] += stores_of(kind_of(i), i % NT)
        stored.append(c)
    with ExitStack() as ctx:
        sem = s.semaphore
        w_in = [sem(f"w_in{k}") for k in range(KT)]
        tables_in, w_high, w_low, w_used = sem("tables_in"), sem("w_high_ready"), sem("w_low_ready"), sem("w_used")
        projected, rows_in, = sem("projected"), sem("ret_rows_out")
        bank_free = [sem(f"bank_free{b}") for b in range(3)]
        st_stored = [sem(f"st_stored{b}") for b in range(2)]
        rot_ready, rot_added = sem("rot_ready"), sem("rot_added")
        r_turned, r_qt, r_qdt, r_scored, r_scd = (
            sem("r_turned"), sem("r_qt"), sem("r_qdt"), sem("r_scored"), sem("r_scd"))
        r_kd, r_faded, v_copied, r_out, r_grown, r_state = (
            sem("r_kd"), sem("r_faded"), sem("v_copied"), sem("r_out"), sem("r_grown"), sem("r_state"))
        cen_ready, gn_sq, gn_mean, gn_root, gn_done = (
            sem("cen_ready"), sem("gn_squared"), sem("gn_mean"), sem("gn_root"), sem("gn_done"))
        silu, y_ready, gates_raw = sem("silu_ready"), sem("y_ready"), sem("gates_raw")
        k_sq, k_mean, k_root, k_copied, k_norm = (
            sem("k_squared"), sem("k_mean"), sem("k_root"), sem("k_copied"), sem("k_normed"))
        k_turned, k_high, k_low = sem("k_turned"), sem("k_high_ready"), sem("k_low_ready")
        state_set, out_done = sem("state_set"), sem("p_stores")
        v_steps, a_steps = sem("p_v_steps"), sem("p_a_steps")
        block = ctx.enter_context(nc.Block())

        nq = rows_of
        norm_index = lambda kind, t: {"wg": 0, "kv": NT, "q": 2 * NT}[kind] + t

        @block.sync
        def _(sp):
            def load_w(g):
                for k in range(KT):
                    if g >= 1:
                        sp.wait_ge(w_low, KT * (g - 1) + k + 1)
                    _, c0, w = GROUPS[g]
                    sp.dma_start(s.wraw[:, k, 0:w], io["w_in"][P * k:P * k + P, c0:c0 + w]).then_inc(w_in[k], 16)
            load_w(0)
            sp.dma_start(rope[:], io["c_rope"].rearrange("p (a t d) -> p a t d", a=2, t=NT)).then_inc(tables_in, 16)
            sp.dma_start(dec[:], io["c_dec"].rearrange("p (h i) -> p h i", h=H)).then_inc(tables_in, 16)
            sp.dma_start(qdec[:], io["c_qdec"].rearrange("p (h i) -> p h i", h=4)).then_inc(tables_in, 16)
            sp.dma_start(gn[:], dram(io["ret_gn_g"], 0, [0, P], [1, 512])).then_inc(tables_in, 16)
            sp.dma_start(kgain[:], dram(io["k_norm_g"], 0, [0, P], [1, HD])).then_inc(tables_in, 16)
            for kv, pe_dram in enumerate((io["cmp_pe_k"], io["cmp_pe_v"])):
                for half in range(2):
                    sp.dma_start(pet[HD * half:HD * half + HD, kv, :],
                                 dram(pe_dram, 0, [1, HD], [HD, 32]),
                                 allow_slow_non_contiguous=True).then_inc(tables_in, 16)
            for g in range(NG):
                if g + 1 < NG:
                    load_w(g + 1)
                for t in range(NT):
                    i, kind, slot, n = g * NT + t, KIND[g], (g * NT + t) % 2, rows_of(t)
                    r0 = P * t
                    if g == 1 and t < H:
                        sp.dma_start(dram(io["skew"], t * L_SKEW, [L_FULL + 1, P], [1, L_FULL]),
                                     dram(io["table"], t * L_TABLE + O_FULL, [0, P], [1, L_FULL])).then_inc(out_done, 16)
                    if g == 3 and t < 2:
                        to, frm = ((io["s_win_k"], io["cache_win_k"]), (io["s_win_v"], io["cache_win_v"]))[t]
                        sp.dma_start(dram(to, 0, [WIN * KVW, B], [4088, 16], [1, 4088]),
                                     dram(frm, KVW, [WIN * KVW, B], [4088, 16], [1, 4088])).then_inc(out_done, 16)
                    if kind in ("qr", "kr") and t == TT:
                        sp.wait_ge(rot_added, i + 1)
                        src = s.qr if kind == "qr" else s.kr
                        sp.dma_start(io["ret_rows"][g], src[0:B, TT, :]).then_inc(rows_in, 16)
                    if kind == "vr" and t == TT:
                        sp.wait_ge(v_copied, NT)
                        sp.dma_start(io["ret_rows"][2], vr[0:B, t % 2, :]).then_inc(rows_in, 16)
                        sp.wait_ge(r_state, TT)
                        for e in range(2):
                            sp.dma_start(dram(io["p_ret"], e * HD * HD, [HD, HD], [2 * HD * HD, 4], [1, HD]),
                                         state[HD * e:HD * e + HD, e:H:2, :]).then_inc(out_done, 16)
                    if kind == "zr":
                        sp.wait_ge(y_ready, t + 1)
                        sp.dma_start(io["y"][r0:r0 + n, 512:1024], s.st[0:n, slot, :]).then_inc(st_stored[slot], 16)
                    if kind == "zn":
                        sp.wait_ge(silu, NT + t + 1)
                        sp.dma_start(io["zn"][r0:r0 + n, :], s.st[0:n, slot, :]).then_inc(st_stored[slot], 16)
                    if kind == "wg" and stores_of(kind, t):
                        sp.wait_ge(k_norm, norm_index(kind, t) + 1)
                        sp.wait_ge(k_copied, t + 1)
                        for j in range(2):
                            if t < TT:
                                to = (io["p_win_k"], io["p_win_v"])[j][r0 - (T - WIN):r0 - (T - WIN) + P, :]
                            else:
                                to = (io["s_win_k"], io["s_win_v"])[j][:, WIN - 1, :]
                            sp.dma_start(to, s.st[0:n, slot, KVW * j:KVW * j + KVW]).then_inc(st_stored[slot], 16)
                    if kind == "kv":
                        sp.wait_ge(k_norm, norm_index(kind, t) + 1)
                        sp.wait_ge(k_copied, NT + t + 1)
                        for j, name in enumerate(("cmp_k", "cmp_v", "slc_k", "slc_v")):
                            to = io["prompt_out"][name][r0:r0 + n, :] if t < TT else io["sample_out"][name]
                            sp.dma_start(to, s.st[0:n, slot, KVW * j:KVW * j + KVW]).then_inc(st_stored[slot], 16)
            sp.wait_ge(rows_in, 48)
            sp.wait_ge(out_done, 16 * (2 + H + 2))
            for slot in range(2):
                sp.wait_ge(st_stored[slot], 16 * stored[-1][slot])

        @block.gpsimd
        def _(pool):
            nc.gpsimd.memset(state[:], 0.0).then_inc(state_set, 1)
            nc.gpsimd.memset(ktz[:], 0.0).then_inc(state_set, 1)
            nc.gpsimd.memset(s.gates[:], 0.0).then_inc(state_set, 1)
            nc.gpsimd.memset(s.qfull[:], 0.0).then_inc(state_set, 1)

            def root(i, n, width, mean, done):
                pool.wait_ge(mean, i + 1)
                nc.gpsimd.tensor_tensor(s.stat[0:n, 8:8 + width], s.stat[0:n, 8:8 + width],
                                        view(s.small[0:n, S_HALF:S_HALF + 1], [0, width]), ALU.pow).then_inc(done, 1)

            for g in range(NG):
                for t in range(NT):
                    i, kind, n = g * NT + t, KIND[g], rows_of(t)
                    if kind in ("qr", "kr"):
                        pool.wait_ge(rot_ready, i + 1)
                        to = s.qr if kind == "qr" else s.kr
                        nc.gpsimd.tensor_tensor(to[0:n, t, :], rot[0:n, 0, :], rot[0:n, 1, :], ALU.add).then_inc(rot_added, 1)
                    if kind == "vr":
                        if t < TT:
                            if t == 0:
                                pool.wait_ge(rot_added, 2 * NT)
                                pool.wait_ge(state_set, 4)
                            else:
                                pool.wait_ge(r_grown, t)
                            nc.gpsimd.tensor_tensor(view(kd[:, 0:1], [HD, H], [1, HD]), view(s.kr[:, t, 0:1], [HD, H], [1, HD]),
                                                    view(s.small[:, S_KDEC:S_KDEC + 1], [1, H], [0, HD]), ALU.mult).then_inc(r_kd, 1)
                        if t >= 1:
                            c = t - 1
                            if c >= 1:
                                pool.wait_ge(r_state, c)
                            nc.gpsimd.tensor_tensor(faded[:], state[:],
                                                    view(s.small[:, S_GAM128:S_GAM128 + 1], [1, H], [0, HD]), ALU.mult).then_inc(r_faded, 1)
                            root(c, P, H, gn_mean, gn_root)
                            pool.wait_ge(gn_root, c + 1)
                            pool.wait_ge(r_qdt, c + 1)
                            nc.gpsimd.tensor_tensor(view(s.qr[:, c, 0:1], [HD, H], [1, HD]), view(cen[:, 0:1], [HD, H], [1, HD]),
                                                    view(s.stat[:, 8:9], [1, H], [0, HD]), ALU.mult).then_inc(gn_done, 1)
                    if kind in ("wg", "kv", "q"):
                        root(norm_index(kind, t), n, H if kind == "q" else HKV, k_mean, k_root)

        def post_evac_kind(i):
            return kind_of(i) in ("wg", "kv", "q")

        turns_before = lambda kind, t: {"wg": t, "kv": NT + 2 * t, "q": 3 * NT + 2 * t}[kind]

        @block.scalar
        def _(act):
            own = Chain(act, a_steps)

            def split_w(g):
                w = GROUPS[g][2]
                for k in range(KT):
                    act.wait_ge(w_in[k], 16 * (g + 1))
                    if g >= 1:
                        act.wait_ge(w_used, KT * (g - 1) + k + 1)
                    nc.scalar.activation(s.wh[:, k, 0:w], s.wraw[:, k, 0:w], ACT.Copy).then_inc(w_high, 1)

            def stage_free(i):
                if stored[i][i % 2]:
                    act.wait_ge(st_stored[i % 2], 16 * stored[i][i % 2])

            def evac(i):
                kind, t = kind_of(i), i % NT
                n, ps = rows_of(t), s.ps[0:rows_of(t), i % 3, :]
                if kind == "vr":
                    act.wait_ge(projected, i + 1)
                    if t >= 2:
                        act.wait_ge(r_grown, t - 1)
                    nc.scalar.activation(vr[0:n, t % 2, :], ps, ACT.Copy).then_inc(v_copied, 1)
                if kind in ("zr", "zn"):
                    act.wait_ge(projected, i + 1)
                    stage_free(i)
                    nc.scalar.activation(s.st[0:n, i % 2, :], ps, ACT.Silu).then_inc(silu, 1)
                if kind == "wg":
                    act.wait_ge(projected, i + 1)
                    if t == 0:
                        act.wait_ge(rows_in, 48)
                        act.wait_ge(out_done, 16 * (2 + H + 2))
                    stage_free(i)
                    if t >= 2:
                        act.wait_ge(k_turned, turns_before(kind, t - 1))
                    if norm_index(kind, t):
                        act.wait_ge(k_mean, norm_index(kind, t))
                    nc.scalar.activation(s.sq[0:n, 0:KVW], ps[:, 0:KVW], ACT.Square).then_inc(k_sq, 1)
                    nc.scalar.activation(s.gates[0:n, t, :], ps[:, 256:280], ACT.Copy).then_inc(gates_raw, 1)
                    v_to = s.v[:, 1, t, :] if t < TT else s.vnew[0:B, 1, :]
                    own.step(nc.scalar.activation(v_to, ps[:, KVW:2 * KVW], ACT.Copy))
                    nc.scalar.activation(s.st[0:n, i % 2, KVW:2 * KVW], ps[:, KVW:2 * KVW], ACT.Copy).then_inc(k_copied, 1)
                if kind == "kv":
                    act.wait_ge(projected, i + 1)
                    stage_free(i)
                    act.wait_ge(k_turned, turns_before(kind, t - 1) if t else NT)
                    if norm_index(kind, t):
                        act.wait_ge(k_mean, norm_index(kind, t))
                    nc.scalar.activation(s.sq[0:n, 0:KVW], ps[:, 2 * KVW:3 * KVW], ACT.Square).then_inc(k_sq, 1)
                    v_to = s.v[:, 0, t, :] if t < TT else s.vnew[0:B, 0, :]
                    own.step(nc.scalar.activation(v_to, ps[:, 3 * KVW:4 * KVW], ACT.Copy))
                    own.step(nc.scalar.activation(s.st[0:n, i % 2, 0:2 * KVW], ps[:, 0:2 * KVW], ACT.Copy))
                    own.sync()
                    nc.scalar.activation(s.st[0:n, i % 2, 3 * KVW:4 * KVW], ps[:, 3 * KVW:4 * KVW], ACT.Copy).then_inc(k_copied, 1)
                if kind == "q":
                    act.wait_ge(projected, i + 1)
                    act.wait_ge(k_mean, norm_index(kind, t))
                    if t == 0:
                        act.wait_ge(k_turned, 3 * NT - 2)
                    nc.scalar.activation(s.sq[0:n, :], ps, ACT.Square).then_inc(k_sq, 1)

            def high(bank, to, scale=1.0):
                nc.scalar.activation(to, bank, ACT.Copy, scale=scale).then_inc(k_high, 1)

            def post(i):
                kind, t = kind_of(i), i % NT
                b = turns_before(kind, t)
                cols = slice(P * t, P * t + P)
                if kind in ("wg", "kv"):
                    br = 1 if kind == "wg" else 0
                    act.wait_ge(k_turned, b + (1 if kind == "wg" else 2))
                    if t < TT:
                        bank = s.ps[:, 3 if kind == "wg" else 4, 0:2 * P]
                        high(view(bank, [P, 2], [1, P]), s.kh[:, br, :, cols])
                    else:
                        high(s.ps[:, 3 if kind == "wg" else 4, 0:B], s.knew[:, br, :])
                if kind == "q":
                    for half in range(2):
                        act.wait_ge(k_turned, b + (half + 1 if t < TT else 2))
                        if t < TT:
                            bank = view(s.ps[:, 3 + half, :], [P, 4], [1, P])
                            high(bank, s.qs[:, 4 * half:4 * half + 4, cols], s.gain[:, 0:1])
                        else:
                            at = slice(HD * half, HD * half + HD)
                            high(view(s.ps[at, 3, 0:1], [1, B], [B, G]),
                                 s.qfull[at, :, G * half:G * half + G], s.gain[at, 0:1])

            for g in range(NG):
                if g == 0:
                    split_w(0)
                for t in range(NT):
                    i = g * NT + t
                    if t == TT and g + 1 < NG:
                        split_w(g + 1)
                    if KIND[g] == "vr" and t < TT:
                        act.wait_ge(r_turned, t + 1)
                        if t >= 1:
                            act.wait_ge(r_scored, 2 * t)
                        nc.scalar.activation(qt[:], view(s.ps[:, 3, :], [P, 4], [1, P]), ACT.Copy).then_inc(r_qt, 1)
                        for e in range(2):
                            at = slice(HD * e, HD * e + HD)
                            nc.scalar.activation(ktz[at, e:H:2, :], view(s.ps[at, 4, :], [P, 4], [1, P]), ACT.Copy).then_inc(r_qt, 1)
                    evac(i)
                    if KIND[g] == "vr" and t >= 1:
                        act.wait_ge(cen_ready, t)
                        nc.scalar.activation(s.sq[:], cen[:], ACT.Square).then_inc(gn_sq, 1)
                    if i >= 1 and post_evac_kind(i - 1):
                        post(i - 1)
            post(n_idx - 1)
            act.wait_ge(gates_raw, NT)
            own.step(nc.scalar.activation(s.gates[:], s.gates[:], ACT.Sigmoid))
            own.sync()

        @block.vector
        def _(dve):
            own = Chain(dve, v_steps)

            def split_w(g):
                w = GROUPS[g][2]
                for k in range(KT):
                    dve.wait_ge(w_high, KT * g + k + 1)
                    nc.vector.tensor_tensor(s.wl[:, k, 0:w], s.wraw[:, k, 0:w], f32(s.wh[:, k, 0:w]),
                                            ALU.subtract).then_inc(w_low, 1)

            def evac(i):
                kind, t = kind_of(i), i % NT
                n, ps = rows_of(t), s.ps[0:rows_of(t), i % 3, :]
                free = bank_free[i % 3]
                if kind in ("qr", "kr"):
                    dve.wait_ge(projected, i + 1)
                    if i >= 1:
                        dve.wait_ge(rot_added, i)
                    own.step(nc.vector.tensor_tensor(view(rot[0:n, 0, :], [HD, H], [1, HD]), view(ps, [HD, H], [1, HD]),
                                                     view(rope[0:n, 0, t, :], [0, H], [1, HD]), ALU.mult))
                    for half in range(2):
                        a, o = 32 * half, 32 * (1 - half)
                        ins = nc.vector.tensor_tensor(view(rot[0:n, 1, a:a + 1], [HD, H], [1, 32]), view(ps[:, o:o + 1], [HD, H], [1, 32]),
                                                      view(rope[0:n, 1, t, a:a + 1], [0, H], [1, 32]), ALU.mult)
                        if half == 0:
                            own.step(ins)
                        else:
                            ins.then_inc(rot_ready, 1)
                    dve.wait_ge(rot_ready, i + 1)
                    dve.sem_inc(free, 1)
                if kind == "vr":
                    dve.wait_ge(v_copied, t + 1)
                    dve.sem_inc(free, 1)
                if kind == "zr":
                    dve.wait_ge(silu, t + 1)
                    dve.wait_ge(gn_done, TT)
                    st = s.st[0:n, i % 2, :]
                    if t < TT:
                        own.step(nc.vector.tensor_tensor(st, st, gn[0:n, :], ALU.mult))
                        own.sync()
                        ins = nc.vector.tensor_tensor(st, st, s.qr[:, t, :], ALU.mult)
                    else:
                        ins = nc.vector.tensor_tensor(st, st, gn[0:n, :], ALU.mult)
                    own.step(ins)
                    own.sync()
                    dve.sem_inc(y_ready, 1)
                    dve.sem_inc(free, 1)
                if kind == "zn":
                    dve.wait_ge(silu, NT + t + 1)
                    dve.sem_inc(free, 1)
                if kind in ("wg", "kv", "q"):
                    ni = norm_index(kind, t)
                    heads = H if kind == "q" else HKV
                    dve.wait_ge(k_sq, ni + 1)
                    if ni >= 1:
                        dve.wait_ge(k_root, ni)
                    own.sync()
                    own.step(nc.vector.tensor_reduce(s.stat[0:n, 0:heads], view(s.sq[0:n, 0:1], [HD, heads], [1, HD]), AX, ALU.add))
                    own.sync()
                    nc.vector.tensor_scalar(s.stat[0:n, 8:8 + heads], s.stat[0:n, 0:heads], 1.0 / HD, EPS,
                                            ALU.mult, ALU.add).then_inc(k_mean, 1)
                    dve.wait_ge(k_root, ni + 1)
                    if kind == "q":
                        if t >= 2:
                            dve.wait_ge(k_turned, turns_before(kind, t - 1))
                        if t < TT:
                            ins = nc.vector.tensor_tensor(view(qd[0:n, i % 2, :], [P, H], [HD, 2], [1, HD]), view(ps, [HD, H], [0, 2], [1, HD]),
                                                          view(s.stat[0:n, 8:9], [1, H], [0, 2], [0, HD]), ALU.mult)
                            own.step(ins)
                        else:
                            for h in range(HKV):
                                ins = nc.vector.tensor_tensor(view(qd[0:n, i % 2, HD * h:HD * h + 1], [P, G], [1, HD]),
                                                              view(ps[:, G * HD * h:G * HD * h + 1], [HD, G], [1, HD]),
                                                              view(s.stat[0:n, 8 + G * h:9 + G * h], [1, G], [0, HD]), ALU.mult)
                                own.step(ins)
                    else:
                        src, dst = (0, 0) if kind == "wg" else (2 * KVW, 2 * KVW)
                        dve.wait_ge(k_copied, t + 1 if kind == "wg" else NT + t + 1)
                        if stored[i][i % 2]:
                            dve.wait_ge(st_stored[i % 2], 16 * stored[i][i % 2])
                        if kind == "wg" and t >= 2:
                            dve.wait_ge(k_turned, turns_before(kind, t - 1))
                        if kind == "kv":
                            dve.wait_ge(k_turned, turns_before(kind, t - 1) if t else NT)
                        for h in range(HKV):
                            ins = nc.vector.scalar_tensor_tensor(
                                s.st[0:n, i % 2, dst + HD * h:dst + HD * h + HD], ps[:, src + HD * h:src + HD * h + HD],
                                s.stat[0:n, 8 + h:9 + h], kgain[0:n, :], ALU.mult, ALU.mult)
                            own.step(ins)
                            if t < TT:
                                if h == 0 and ni >= 1:
                                    dve.wait_ge(k_turned, turns_before(kind, t))
                                own.step(nc.vector.scalar_tensor_tensor(
                                    view(s.sq[0:n, 256 + P * h:257 + P * h], [HD, 2], [1, HD]), view(ps[:, src + HD * h:src + HD * h + 1], [0, 2], [1, HD]),
                                    s.stat[0:n, 8 + h:9 + h], view(kgain[0:n, :], [0, 2], [1, HD]), ALU.mult, ALU.mult))
                    own.sync()
                    dve.sem_inc(k_norm, 1)
                    dve.sem_inc(free, 1)

            def post(i):
                kind, t = kind_of(i), i % NT
                cols = slice(P * t, P * t + P)
                hi = {"wg": t, "kv": NT + t, "q": 2 * NT + 2 * t}[kind]
                if kind in ("wg", "kv"):
                    br = 1 if kind == "wg" else 0
                    if kind == "kv" and t < TT:
                        dve.wait_ge(k_turned, turns_before(kind, t) + 1)
                        for j in range(2):
                            own.step(nc.vector.tensor_tensor(
                                view(s.kct[:, j, 4 * t:4 * t + 1], [1, 4], [32, 32]), view(s.ps[:, 3, P * j:P * j + 1], [32, 4], [1, 32]),
                                view(pet[:, j, :], [0, 4], [1, 32]), ALU.add))
                        own.sync()
                    dve.wait_ge(k_high, hi + 1)
                    if t < TT:
                        bank = view(s.ps[:, 3 if kind == "wg" else 4, :], [P, 2], [1, P])
                        nc.vector.tensor_tensor(s.kl[:, br, :, cols], bank, f32(s.kh[:, br, :, cols]),
                                                ALU.subtract).then_inc(k_low, 1)
                    else:
                        dve.sem_inc(k_low, 1)
                if kind == "q":
                    for half in range(2):
                        dve.wait_ge(k_high, hi + half + 1)
                        if t < TT:
                            to = s.qs[HD:P, 4 * half:4 * half + 4, cols]
                            nc.vector.scalar_tensor_tensor(to, view(s.ps[HD:P, 3 + half, :], [P, 4], [1, P]), s.gain[HD:P, 0:1],
                                                           f32(to), ALU.mult, ALU.subtract).then_inc(k_low, 1)
                        else:
                            dve.sem_inc(k_low, 1)

            own.step(nc.vector.memset(s.stat[:], 0.0))
            own.sync()
            dve.wait_ge(tables_in, 144)
            for g in range(NG):
                if g == 0:
                    split_w(0)
                for t in range(NT):
                    i = g * NT + t
                    if t == TT and g + 1 < NG:
                        split_w(g + 1)
                    if KIND[g] == "vr" and t < TT:
                        dve.wait_ge(r_turned, t + 1)
                        if t >= 1:
                            dve.wait_ge(r_out, t)
                        dve.wait_ge(r_qt, 3 * t + 1)
                        nc.vector.tensor_tensor(qdt[:], view(s.ps[:, 3, :], [P, 4], [1, P]), qdec[:], ALU.mult).then_inc(r_qdt, 1)
                    evac(i)
                    if KIND[g] == "vr":
                        if t < TT:
                            for e in range(2):
                                dve.wait_ge(r_scored, 2 * t + e + 1)
                                nc.vector.tensor_tensor(scd[:, e:H:2, :], view(s.ps[:, 5 + e, :], [P, 4], [1, P]),
                                                        dec[:, e:H:2, :], ALU.mult).then_inc(r_scd, 1)
                        if t >= 1:
                            retention_norm(nc, s, dve, own, cen, P, s.ps[:, 7, :], r_out, t, gn_done, t - 1, cen_ready, gn_sq, gn_mean)
                            dve.wait_ge(r_grown, t)
                            dve.wait_ge(r_faded, t)
                            for e in range(2):
                                at = slice(HD * e, HD * e + HD)
                                ins = nc.vector.tensor_tensor(state[at, e:H:2, :], faded[at, e:H:2, :],
                                                              view(s.ps[at, 3, HD * e:HD * e + 1], [P, 4], [1, HD]), ALU.add)
                                own.step(ins)
                            own.sync()
                            dve.sem_inc(r_state, 1)
                    if i >= 1 and post_evac_kind(i - 1):
                        post(i - 1)
            post(n_idx - 1)
            own.sync()
            dve.wait_ge(k_low, 4 * NT)

        @block.tensor
        def _(pe):
            def proj(i):
                g, t = i // NT, i % NT
                n, w = rows_of(t), GROUPS[g][2]
                if i >= 3:
                    pe.wait_ge(bank_free[i % 3], (i - 3) // 3 + 1)
                for k in range(KT):
                    if t == 0:
                        pe.wait_ge(w_low, KT * g + k + 1)
                    rows = slice(P * t, P * t + n)
                    out = s.ps[0:n, i % 3, 0:w]
                    nc.tensor.matmul(out, s.xh[:, k, rows], s.wh[:, k, 0:w], start=(k == 0), stop=False)
                    nc.tensor.matmul(out, s.xh[:, k, rows], s.wl[:, k, 0:w], start=False, stop=False)
                    ins = nc.tensor.matmul(out, s.xl[:, k, rows], s.wh[:, k, 0:w], start=False, stop=(k == KT - 1))
                    if t == TT and k < KT - 1:
                        ins.then_inc(w_used, 1)
                if t == TT:
                    ins.then_inc(w_used, 1)
                    pe.wait_ge(w_used, KT * (g + 1))
                    pe.sem_inc(projected, 1)
                else:
                    ins.then_inc(projected, 1)

            def turn_ret(t):
                pe.wait_ge(rot_added, 2 * NT)
                if t >= 1:
                    pe.wait_ge(r_state, t - 1) if t >= 2 else None
                    pe.wait_ge(r_qdt, t)
                    pe.wait_ge(r_qt, 3 * t)
                for bank, src in ((3, s.qr), (4, s.kr)):
                    for j in range(4):
                        last = nc.tensor.transpose(s.ps[:, bank, P * j:P * j + P], src[:, t, P * j:P * j + P], s.ident[:])
                last.then_inc(r_turned, 1)

            def score(t):
                pe.wait_ge(r_qt, 3 * (t + 1))
                if t >= 1:
                    pe.wait_ge(r_scd, 2 * t)
                else:
                    pe.wait_ge(state_set, 4)
                for e in range(2):
                    for j in range(4):
                        last = nc.tensor.matmul(s.ps[:, 5 + e, P * j:P * j + P], ktz[:, 2 * j + e, :], qt[:, j, :], start=True, stop=True)
                    last.then_inc(r_scored, 1)

            def out_ret(c):
                pe.wait_ge(v_copied, c + 1)
                pe.wait_ge(r_scd, 2 * (c + 1))
                pe.wait_ge(r_qdt, c + 1)
                if c >= 1:
                    pe.wait_ge(r_state, c)
                    pe.wait_ge(cen_ready, c)
                for h in range(H):
                    out = s.ps[:, 7, HD * h:HD * h + HD]
                    nc.tensor.matmul(out, scd[:, h, :], vr[:, c % 2, HD * h:HD * h + HD], start=True, stop=False)
                    last = nc.tensor.matmul(out, qdt[:, h // 2, :], state[:, h, :], start=False, stop=True)
                last.then_inc(r_out, 1)
                pe.wait_ge(r_kd, c + 1)
                if c + 1 < TT:
                    pe.wait_ge(r_qdt, c + 2)
                for j in range(4):
                    last = nc.tensor.matmul(s.ps[:, 3, P * j:P * j + P], kd[:, P * j:P * j + P], vr[:, c % 2, P * j:P * j + P],
                                            start=True, stop=True)
                last.then_inc(r_grown, 1)

            def post(i):
                kind, t = kind_of(i), i % NT
                n = rows_of(t)
                st = s.st[0:n, i % 2, :]
                one = s.ident[0:n, 0:n]
                pe.wait_ge(k_norm, norm_index(kind, t) + 1)
                low_before = {"wg": t, "kv": NT + t, "q": 2 * NT + 2 * t}[kind]
                if low_before:
                    pe.wait_ge(k_low, low_before)
                def doubled(bank, at, src):
                    return nc.tensor.transpose(s.ps[:, bank, at:at + P], src, one)
                if kind == "wg":
                    if t < TT:
                        for h in range(HKV):
                            last = doubled(3, P * h, s.sq[:, 256 + P * h:256 + P * h + P])
                    else:
                        last = nc.tensor.transpose(s.ps[:, 3, 0:B], st[:, 0:KVW], one)
                    last.then_inc(k_turned, 1)
                if kind == "kv":
                    for j in range(2):
                        last = nc.tensor.transpose(s.ps[:, 3, P * j:P * j + n], st[:, KVW * j:KVW * j + KVW], one)
                    last.then_inc(k_turned, 1)
                    if t < TT:
                        for h in range(HKV):
                            last = doubled(4, P * h, s.sq[:, 256 + P * h:256 + P * h + P])
                    else:
                        last = nc.tensor.transpose(s.ps[:, 4, 0:B], st[:, 2 * KVW:3 * KVW], one)
                    last.then_inc(k_turned, 1)
                if kind == "q":
                    if t < TT:
                        for half in range(2):
                            for j in range(4):
                                last = doubled(3 + half, P * j, qd[:, i % 2, P * (4 * half + j):P * (4 * half + j) + P])
                            last.then_inc(k_turned, 1)
                    else:
                        for j in range(G):
                            last = nc.tensor.transpose(s.ps[:, 3, B * j:B * j + B], qd[0:n, i % 2, P * j:P * j + P], one)
                            if j % 2:
                                last.then_inc(k_turned, 1)

            for i in range(n_idx):
                kind, t = kind_of(i), i % NT
                if kind == "vr" and t < TT:
                    turn_ret(t)
                proj(i)
                if kind == "vr":
                    if t < TT:
                        score(t)
                    if t >= 1:
                        out_ret(t - 1)
                if i >= 1 and post_evac_kind(i - 1):
                    post(i - 1)
            post(n_idx - 1)


def retention_norm(nc, s, dve, own, cen, n, bank, out_sem, out_value, free_sem, free_value, cen_ready, gn_sq, gn_mean):
    heads = lambda ap: view(ap, [HD, H], [1, HD])
    dve.wait_ge(out_sem, out_value)
    if free_value >= 1:
        dve.wait_ge(free_sem, free_value)
    own.step(nc.vector.tensor_reduce(s.stat[0:n, 0:H], heads(bank[0:n]), AX, ALU.add))
    own.sync()
    own.step(nc.vector.tensor_scalar(s.stat[0:n, 16:24], s.stat[0:n, 0:H], 1.0 / HD, None, ALU.mult))
    own.sync()
    nc.vector.tensor_tensor(heads(cen[0:n, 0:1]), heads(bank[0:n]), view(s.stat[0:n, 16:17], [1, H], [0, HD]),
                            ALU.subtract).then_inc(cen_ready, 1)
    dve.wait_ge(gn_sq, out_value)
    own.step(nc.vector.tensor_reduce(s.stat[0:n, 0:H], heads(s.sq[0:n, 0:1]), AX, ALU.add))
    own.sync()
    nc.vector.tensor_scalar(s.stat[0:n, 8:16], s.stat[0:n, 0:H], 1.0 / HD, EPS, ALU.mult, ALU.add).then_inc(gn_mean, 1)


SLOTS = 6


def persistent_compressed(nc, s):
    m = Memory(nc, s.kct_region)
    s.ck_h = m.put("ck_high", [P, HKV, NBP], F32R)
    s.ck_l = m.put("ck_low", [P, HKV, NBP], F32R)
    s.cv_bd = m.put("cv_blocks", [P, HKV, G, HD])
    s.cks = m.put("ck_sample", [P, NBS])
    s.cvs = m.put("cv_sample", [P, 2, KVW])
    s.d_region = m.at


def compress(nc, s, io):
    m = Memory(nc, s.x_region)
    w1 = m.put("w1_blocks", [P, 2, CB, P])
    w2 = m.put("w2_blocks", [P, 2, P])
    kcs = m.put("kcs", [P, CB, NBS])
    raw = m.put("raw_pages", [P, SLOTS, PAGES, P])
    hid = m.put("hidden", [P, 2, NBS + NBP])
    pet = m.put("pe_t2", [P, 2, CB])
    kgain = m.put("k_gain2", [P, HD])
    pages = m.put("page_row", [1, B * PAGES], I32)
    sq = m.put("c_squares", [P, KVW])
    nat = m.put("ck_natural", [P, KVW])
    dup = m.put("ck_doubled", [P, HKV, 2, HD])
    stat = m.put("c_stats", [P, 16])
    cvd = m.put("cv_blocks_first", [P, HKV, G, HD])
    ckh = m.put("ck_high_first", [P, HKV, NBP], F32R)
    cks0 = m.put("ck_sample_first", [P, NBS])
    cvs0 = m.put("cv_sample_first", [P, 2, KVW])
    assert m.at <= 229368, m.at
    pool_dram = [c.rearrange("n t h d -> n t (h d)") for c in (io["cache_cmp_k"], io["cache_cmp_v"])]
    with ExitStack() as ctx:
        sem = s.semaphore
        consts_in, table_in, zeroed = sem("c_consts_in"), sem("page_table_in"), sem("c_zeroed")
        raw_in = [sem(f"c_raw_in{b}") for b in range(SLOTS)]
        turned, evacuated, first_out, silu_out = sem("c_turned"), sem("c_evacuated"), sem("c_first_out"), sem("c_silu")
        second_out, squared, meaned, rooted = sem("c_second_out"), sem("c_squared"), sem("c_meaned"), sem("c_rooted")
        normed, key_turned, key_kept, value_kept = sem("c_normed"), sem("c_key_turned"), sem("c_key_kept"), sem("c_value_kept")
        key_high = sem("c_key_high")
        v_steps, a_steps = sem("c_v_steps"), sem("c_a_steps")
        block = ctx.enter_context(nc.Block())
        OUT_BANK = [6, 7, 5]
        tiles = [(P * j, P) for j in range(2)] + [(NBS, NBP)]

        def load_pages(engine, u, half):
            kv, b = u // B, u % B
            if u == 0:
                engine.wait_ge(table_in, 16)
            if u >= SLOTS:
                engine.wait_ge(turned, 2 * (u - SLOTS + 1))
            for p in range(4 * half, 4 * half + 4):
                page = engine.value_load(pages[0:1, PAGES * b + p:PAGES * b + p + 1], min_val=0, max_val=N_PHYS - 1)
                engine.dma_start(raw[:, u % SLOTS, p, :],
                                 pool_dram[kv][bass.ds(page, 1), :, :].rearrange("a t c -> (a t) c")).then_inc(raw_in[u % SLOTS], 16)

        @block.sync
        def _(sp):
            sp.dma_start(pages[:], io["page_table"].rearrange("(a b) p -> a (b p)", a=1)).then_inc(table_in, 16)
            sp.wait_ge(zeroed, 2)
            for kv, (w1d, w2d, pe_dram) in enumerate(((io["cmp_w1_k"], io["cmp_w2_k"], io["cmp_pe_k"]), (io["cmp_w1_v"], io["cmp_w2_v"], io["cmp_pe_v"]))):
                for half in range(2):
                    at = slice(HD * half, HD * half + HD)
                    sp.dma_start(w1[at, kv, :, HD * half:HD * half + HD],
                                 dram(w1d, 0, [HD, HD], [HD * HD, CB], [1, HD])).then_inc(consts_in, 16)
                    sp.dma_start(w2[at, kv, HD * half:HD * half + HD], w2d).then_inc(consts_in, 16)
                    sp.dma_start(pet[at, kv, :], dram(pe_dram, 0, [1, HD], [HD, CB]), allow_slow_non_contiguous=True).then_inc(consts_in, 16)
            sp.dma_start(kgain[:], dram(io["k_norm_g"], 0, [0, P], [1, HD])).then_inc(consts_in, 16)
            for u in range(2 * B):
                load_pages(sp, u, 0)

        @block.gpsimd
        def _(pool):
            nc.gpsimd.memset(cvd[:], 0.0).then_inc(zeroed, 1)
            for j, (_, n) in enumerate(tiles):
                pool.wait_ge(meaned, j + 1)
                nc.gpsimd.tensor_tensor(stat[0:n, 4:6], stat[0:n, 4:6], view(s.small[0:n, S_HALF:S_HALF + 1], [0, 2]),
                                        ALU.pow).then_inc(rooted, 1)

        @block.scalar
        def _(act):
            own = Chain(act, a_steps)
            for kv in range(2):
                for u in range(B + SLOTS - 2) if kv == 0 else range(B + SLOTS - 2, 2 * B):
                    load_pages(act, u, 1)
                act.wait_ge(first_out, 2 * kv + 2)
                nc.scalar.activation(hid[:, kv, 0:NBS], s.ps[:, 4, 0:NBS], ACT.Silu).then_inc(silu_out, 1)
                nc.scalar.activation(hid[:, kv, NBS:NBS + NBP], s.ps[:, 5, 0:NBP], ACT.Silu).then_inc(silu_out, 1)
                for j, (_, n) in enumerate(tiles):
                    act.wait_ge(second_out, 3 * kv + j + 1)
                    if kv == 0:
                        if j:
                            act.wait_ge(meaned, j)
                        nc.scalar.activation(sq[0:n, :], s.ps[0:n, OUT_BANK[j], 0:KVW], ACT.Square).then_inc(squared, 1)
                    elif j < 2:
                        nc.scalar.activation(cvs0[:, j, :], s.ps[:, OUT_BANK[j], 0:KVW], ACT.Copy).then_inc(value_kept, 1)
                    else:
                        act.wait_ge(zeroed, 2)
                        for g in range(G):
                            for h in range(HKV):
                                ins = nc.scalar.activation(cvd[NBP * g:NBP * g + NBP, h, g, :], s.ps[0:NBP, OUT_BANK[2], HD * h:HD * h + HD], ACT.Copy)
                                own.step(ins)
                        own.sync()
                        act.sem_inc(value_kept, 1)
                if kv == 0:
                    act.wait_ge(key_turned, 3)
                    nc.scalar.activation(ckh[:], view(s.ps[:, 3, 0:1], [P, HKV], [1, NBP]), ACT.Copy).then_inc(key_high, 1)
            act.wait_ge(first_out, 4)
            own.step(nc.scalar.activation(s.cvs[:], cvs0[:], ACT.Copy))
            own.step(nc.scalar.activation(s.cv_bd[:], cvd[:], ACT.Copy))
            own.sync()

        @block.vector
        def _(dve):
            own = Chain(dve, v_steps)
            own.step(nc.vector.memset(w1[:], 0.0))
            own.step(nc.vector.memset(w2[:], 0.0))
            own.sync()
            dve.sem_inc(zeroed, 1)
            dve.wait_ge(consts_in, 16 * 13)

            def norm_keys():
                for j, (_, n) in enumerate(tiles):
                    bank = s.ps[0:n, OUT_BANK[j], :]
                    dve.wait_ge(squared, j + 1)
                    if j:
                        dve.wait_ge(rooted, j)
                    own.sync()
                    own.step(nc.vector.tensor_reduce(stat[0:n, 0:2], view(sq[0:n, 0:1], [HD, 2], [1, HD]), AX, ALU.add))
                    own.sync()
                    nc.vector.tensor_scalar(stat[0:n, 4:6], stat[0:n, 0:2], 1.0 / HD, EPS, ALU.mult, ALU.add).then_inc(meaned, 1)
                    dve.wait_ge(rooted, j + 1)
                    if j == 1:
                        dve.wait_ge(key_turned, 1)
                    for h in range(HKV):
                        src = bank[:, HD * h:HD * h + HD]
                        if j < 2:
                            own.step(nc.vector.scalar_tensor_tensor(nat[0:n, HD * h:HD * h + HD], src, stat[0:n, 4 + h:5 + h],
                                                                    kgain[0:n, :], ALU.mult, ALU.mult))
                        else:
                            own.step(nc.vector.scalar_tensor_tensor(dup[0:n, h, :, :], view(src, [0, 2], [1, HD]), stat[0:n, 4 + h:5 + h],
                                                                    view(kgain[0:n, :], [0, 2], [1, HD]), ALU.mult, ALU.mult))
                    own.sync()
                    dve.sem_inc(normed, 1)
                    if j < 2:
                        dve.wait_ge(key_turned, j + 1)
                        nc.vector.tensor_copy(cks0[:, P * j:P * j + P], s.ps[:, 3, 0:P]).then_inc(key_kept, 1)

            for kv in range(2):
                for b in range(B):
                    u = B * kv + b
                    if kv == 1 and b == 0:
                        dve.wait_ge(first_out, 2)
                    for half in range(2):
                        i = 2 * u + half
                        dve.wait_ge(turned, i + 1)
                        nc.vector.tensor_tensor(view(kcs[:, 0, NBP * b + 16 * half:NBP * b + 16 * half + 1], [1, 16], [NBS, CB]),
                                                view(s.ps[:, i % 3, 0:1], [CB, 16], [1, CB]),
                                                view(pet[:, kv, 0:1], [0, 16], [1, CB]), ALU.add).then_inc(evacuated, 1)
                    if kv == 1 and b == 1:
                        norm_keys()
            dve.wait_ge(first_out, 4)
            dve.wait_ge(key_high, 1)
            own.step(nc.vector.tensor_tensor(s.ck_l[:], view(s.ps[:, 3, 0:1], [P, HKV], [1, NBP]), f32(ckh[:]), ALU.subtract))
            own.step(nc.vector.tensor_copy(s.ck_h[:], f32(ckh[:])))
            dve.wait_ge(key_kept, 2)
            own.step(nc.vector.tensor_copy(s.cks[:], cks0[:]))
            own.sync()

        @block.tensor
        def _(pe):
            def turn(u):
                pe.wait_ge(raw_in[u % SLOTS], 16 * PAGES * (u // SLOTS + 1))
                for half in range(2):
                    i = 2 * u + half
                    if i >= 3:
                        pe.wait_ge(evacuated, i - 2)
                    for j in range(4):
                        last = nc.tensor.transpose(s.ps[:, i % 3, P * j:P * j + P], raw[:, u % SLOTS, 4 * half + j, :], s.ident[:])
                    last.then_inc(turned, 1)

            def second(kv):
                for j, (c0, n) in enumerate(tiles):
                    pe.wait_ge(silu_out, 2 * kv + (1 if j < 2 else 2))
                    nc.tensor.matmul(s.ps[0:n, OUT_BANK[j], 0:KVW], hid[:, kv, c0:c0 + n], w2[:, kv, :], start=True, stop=True).then_inc(second_out, 1)

            def turn_keys(j):
                pe.wait_ge(normed, j + 1)
                if j == 1:
                    pe.wait_ge(key_kept, 1)
                if j < 2:
                    nc.tensor.transpose(s.ps[:, 3, 0:P], nat[:], s.ident[:]).then_inc(key_turned, 1)
                else:
                    pe.wait_ge(key_kept, 2)
                    for h in range(HKV):
                        last = nc.tensor.transpose(s.ps[:, 3, P * h:P * h + NBP], dup[0:NBP, h, :, :].rearrange("p a d -> p (a d)"), s.ident[0:NBP, 0:NBP])
                    last.then_inc(key_turned, 1)

            pe.wait_ge(consts_in, 16 * 13)
            for kv in range(2):
                for b in range(B):
                    turn(B * kv + b)
                    if kv == 1 and b == 1:
                        for j in range(2):
                            turn_keys(j)
                        turn_keys(2)
                pe.wait_ge(evacuated, 2 * B * (kv + 1))
                if kv == 1:
                    pe.wait_ge(silu_out, 2)
                    pe.wait_ge(normed, 3)
                for i in range(CB):
                    last = nc.tensor.matmul(s.ps[:, 4, 0:NBS], w1[:, kv, i, :], kcs[:, i, :], start=(i == 0), stop=(i == CB - 1))
                last.then_inc(first_out, 1)
                for i in range(CB):
                    last = nc.tensor.matmul(s.ps[:, 5, 0:NBP], w1[:, kv, i, :], s.kct[:, kv, CB * i:CB * i + NBP], start=(i == 0), stop=(i == CB - 1))
                last.then_inc(first_out, 1)
                second(kv)


R_ = B * H


def attend_sample(nc, s, io):
    m = Memory(nc, s.x_region)
    qb = m.put("q_by_row", [P, B, R_])
    kraw = m.put("keys_raw", [P, 2, PAGES + 4, P])
    ktr = m.put("keys_turned", [P, 2, T + WIN])
    vs = m.put("values", [P, B, PAGES + 4, KVW])
    bias = m.put("bias_sample", [R_, L_SAMPLE])
    sc = m.put("logits", [R_, T + B + WIN + B])
    pc = m.put("p_compressed", [R_, 4, NBP])
    own_mask = m.put("own_mask", [R_, B])
    newb = m.put("bias_new", [R_, B])
    sel = m.put("selection", [R_, 4, 16])
    groups = m.put("group_sum", [R_, R_])
    order = m.put("block_order", [R_, 16])
    stat = m.put("d_stats", [R_, 24])
    pts = m.put("pt_selected", [P, PAGES, R_])
    ptw = m.put("pt_window", [P, 4, R_])
    ptn = m.put("pt_new", [B, 2, R_])
    ptc = m.put("pt_compressed", [P, 2, G, H])
    ot = m.put("o_turned", [P, R_])
    on = m.put("o_natural", [R_, 2, HD])
    ys = m.put("y_rows", [B, 4, 512])
    pages = m.put("page_row2", [1, B * PAGES], I32)
    assert m.at <= 229368, m.at
    pools = [c.rearrange("n t h d -> n t (h d)") for c in (io["cache_slc_k"], io["cache_slc_v"])]
    wins = [io["cache_win_k"], io["cache_win_v"]]
    with ExitStack() as ctx:
        sem = s.semaphore
        small_in, page_in = sem("d_small_in"), sem("page_table_in2")
        k_in = [sem(f"d_keys_in{b}") for b in range(2)]
        v_in, v_in_w = [sem(f"d_values_in{b}") for b in range(B)], sem("d_values_w")
        bias_in = sem("bias_in")
        gates_out, gates_in, qb_ready = sem("gates_out"), sem("gates_in"), sem("qb_ready")
        turned, evac_v, evac_a, scored = sem("d_turned"), sem("d_evac_v"), sem("d_evac_a"), sem("d_scored")
        c_scored, c_max, c_exp, c_norm, c_grouped = sem("c_scored"), sem("c_max"), sem("c_exp"), sem("c_norm"), sem("c_grouped")
        s_max, s_exp, s_scaled, p_turned, p_kept, zero_c = (
            sem("s_max"), sem("s_exp"), sem("s_scaled"), sem("p_turned"), sem("p_kept"), sem("zero_c"))
        o_out, o_kept, o_turned, o_sel, o_stored, y_in, y_done, y_stored = (
            sem("o_out"), sem("o_kept"), sem("o_turned"), sem("o_sel"), sem("o_stored"), sem("y_in"), sem("y_done"), sem("y_stored"))
        v_steps = sem("d_v_steps")
        block = ctx.enter_context(nc.Block())
        N1, W0 = T, T + B

        @block.sync
        def _(sp):
            sp.dma_start(pages[:], io["page_table"].rearrange("(a b) p -> a (b p)", a=1)).then_inc(page_in, 16)
            sp.dma_start(own_mask[:], io["c_own"]).then_inc(small_in, 16)
            sp.dma_start(groups[:], io["c_group"]).then_inc(small_in, 16)
            sp.dma_start(order[:], io["c_order"]).then_inc(small_in, 16)
            sp.dma_start(dram(io["scratch"], 0, [24, B], [1, 24]), s.gates[0:B, TT, :]).then_inc(gates_out, 16)
            for b in range(B):
                sp.dma_start(bias[H * b:H * b + H, :], io["table"][:, O_SLC:O_SLC + L_SAMPLE]).then_inc(bias_in, 16)
            sp.wait_ge(gates_out, 16)
            sp.dma_start(stat[:, 0:3], dram(io["scratch"], 0, [3, R_], [1, 3])).then_inc(gates_in, 16)
            sp.wait_ge(page_in, 16)
            for b in range(B):
                if b >= 2:
                    sp.wait_ge(turned, 3 * (b - 1))
                for p in range(PAGES):
                    page = sp.value_load(pages[0:1, PAGES * b + p:PAGES * b + p + 1], min_val=0, max_val=N_PHYS - 1)
                    sp.dma_start(kraw[:, b % 2, p, :], pools[0][bass.ds(page, 1), :, :].rearrange("a t c -> (a t) c")).then_inc(k_in[b % 2], 16)
                sp.dma_start(kraw[:, b % 2, PAGES:PAGES + 4, :], wins[0][b].rearrange("(a t) c -> t a c", t=P)).then_inc(k_in[b % 2], 16)
            sp.dma_start(ys[:, 1, :], io["zn"][T:ROWS, :]).then_inc(y_in, 16)
            sp.wait_ge(o_sel, 1)
            sp.dma_start(dram(io["scratch"], 65536, [HD, R_], [1, HD]), on[:, 0, :]).then_inc(o_stored, 16)
            sp.wait_ge(o_stored, 16)
            sp.dma_start(ys[:, 0, :], dram(io["scratch"], 65536, [512, B], [1, 512])).then_inc(y_in, 16)
            sp.wait_ge(y_done, 1)
            sp.dma_start(io["y"][T:ROWS, 0:512], ys[:, 0, :]).then_inc(y_stored, 16)
            sp.wait_ge(y_stored, 16)

        @block.gpsimd
        def _(pool):
            nc.gpsimd.memset(qb[:], 0.0).then_inc(zero_c, 1)
            nc.gpsimd.memset(ptc[:], 0.0).then_inc(zero_c, 1)
            pool.wait_ge(zero_c, 2)

        @block.scalar
        def _(act):
            act.wait_ge(page_in, 16)
            for b in range(B):
                for p in range(PAGES):
                    page = act.value_load(pages[0:1, PAGES * b + p:PAGES * b + p + 1], min_val=0, max_val=N_PHYS - 1)
                    act.dma_start(vs[:, b, p, :], pools[1][bass.ds(page, 1), :, :].rearrange("a t c -> (a t) c")).then_inc(v_in[b], 16)
                act.dma_start(vs[:, b, PAGES:PAGES + 4, :], wins[1][b].rearrange("(a t) c -> t a c", t=P)).then_inc(v_in[b], 16)
                act.wait_ge(turned, 3 * b + 2)
                if b >= 2:
                    act.wait_ge(scored, b - 1)
                nc.scalar.activation(ktr[:, b % 2, 512:1024], s.ps[:, 5, :], ACT.Copy).then_inc(evac_a, 1)
            act.wait_ge(c_max, 1)
            nc.scalar.activation(pc[:, 0, :], pc[:, 0, :], ACT.Exp, bias=stat[:, 4:5], accum_out=stat[:, 5:6]).then_inc(c_exp, 1)
            for j, (a, z) in enumerate(((0, W0), (W0, W0 + WIN + B))):
                act.wait_ge(s_max, j + 1)
                nc.scalar.activation(sc[:, a:z], sc[:, a:z], ACT.Exp, bias=stat[:, 6 + j:7 + j], accum_out=stat[:, 8 + j:9 + j]).then_inc(s_exp, 1)

        @block.vector
        def _(dve):
            own = Chain(dve, v_steps)
            step, sync, tt, ts = own.step, own.sync, nc.vector.tensor_tensor, nc.vector.tensor_scalar
            dve.wait_ge(zero_c, 2)
            nc.vector.tensor_copy(view(qb[:, 0, 0:1], [R_ + H, B], [1, H]), s.qfull[:]).then_inc(qb_ready, 1)
            for b in range(B):
                dve.wait_ge(turned, 3 * b + 1)
                if b >= 2:
                    dve.wait_ge(scored, b - 1)
                nc.vector.tensor_copy(ktr[:, b % 2, 0:512], s.ps[:, 4, :]).then_inc(evac_v, 1)
                dve.wait_ge(turned, 3 * b + 3)
                nc.vector.tensor_copy(ktr[:, b % 2, 1024:1536], s.ps[:, 6, :]).then_inc(evac_v, 1)
            dve.wait_ge(bias_in, 128)
            dve.wait_ge(small_in, 48)
            dve.wait_ge(gates_in, 16)
            dve.wait_ge(c_scored, 1)
            step(tt(pc[:, 0, :], s.ps[0:R_, 3, 16:16 + NBP], bias[:, L_SLC + L_SWIN:L_SLC + L_SWIN + NBP], ALU.add))
            sync()
            step(nc.vector.tensor_reduce(stat[:, 3:4], pc[:, 0, :], AX, ALU.max))
            sync()
            ts(stat[:, 4:5], stat[:, 3:4], -1.0, None, ALU.mult).then_inc(c_max, 1)
            dve.wait_ge(c_exp, 1)
            step(nc.vector.reciprocal(stat[:, 10:11], stat[:, 5:6]))
            sync()
            step(ts(pc[:, 1, :], pc[:, 0, :], stat[:, 10:11], None, ALU.mult))
            sync()
            dve.sem_inc(c_norm, 1)
            step(ts(pc[:, 2, :], pc[:, 1, :], stat[:, 0:1], None, ALU.mult))
            sync()
            step(nc.vector.tensor_copy(pc[:, 0, :], pc[:, 2, :]))
            step(nc.vector.tensor_copy(pc[:, 3, :], pc[:, 2, :]))
            dve.wait_ge(c_grouped, 1)
            step(nc.vector.tensor_reduce(sel[:, 0, :], view(s.ps[0:R_, 3, 64:65], [2, 16], [1, 2]), AX, ALU.add))
            sync()
            step(nc.vector.tensor_copy(pc[:, 1, :], pc[:, 2, :]))
            step(nc.vector.tensor_reduce(stat[:, 11:12], sel[:, 0, 1:15], AX, ALU.min))
            sync()
            step(ts(sel[:, 1, 1:15], sel[:, 0, 1:15], stat[:, 11:12], None, ALU.is_equal))
            sync()
            step(tt(sel[:, 2, 1:15], sel[:, 1, 1:15], order[:, 1:15], ALU.mult))
            sync()
            step(nc.vector.tensor_reduce(stat[:, 12:13], sel[:, 2, 1:15], AX, ALU.max))
            sync()
            step(ts(sel[:, 3, :], order[:], stat[:, 12:13], MASK, ALU.is_equal, ALU.mult))
            step(ts(newb[:], own_mask[:], bias[:, L_SAMPLE - 1:L_SAMPLE], None, ALU.add))
            sync()
            dve.wait_ge(scored, B)
            for j in range(2):
                step(tt(sc[:, 512 * j:512 * j + 512], s.ps[0:R_, j, :], bias[:, 512 * j:512 * j + 512], ALU.add))
            step(tt(sc[:, W0:W0 + WIN], s.ps[0:R_, 2, :], bias[:, L_SLC:L_SLC + WIN], ALU.add))
            dve.wait_ge(c_scored, 2)
            step(tt(sc[:, N1:N1 + B], s.ps[0:R_, 3, 0:B], newb[:], ALU.add))
            step(tt(sc[:, W0 + WIN:W0 + WIN + B], s.ps[0:R_, 3, B:2 * B], newb[:], ALU.add))
            sync()
            step(tt(view(sc[:, 0:1], [64, 16], [1, 64]), view(sc[:, 0:1], [64, 16], [1, 64]), view(sel[:, 3, 0:1], [1, 16], [0, 64]), ALU.add))
            sync()
            for j, (a, z) in enumerate(((0, W0), (W0, W0 + WIN + B))):
                step(nc.vector.tensor_reduce(stat[:, 13 + j:14 + j], sc[:, a:z], AX, ALU.max))
                sync()
                ts(stat[:, 6 + j:7 + j], stat[:, 13 + j:14 + j], -1.0, None, ALU.mult).then_inc(s_max, 1)
            for j, (a, z) in enumerate(((0, W0), (W0, W0 + WIN + B))):
                dve.wait_ge(s_exp, j + 1)
                step(nc.vector.reciprocal(stat[:, 15 + j:16 + j], stat[:, 8 + j:9 + j]))
                sync()
                ts(sc[:, a:z], sc[:, a:z], stat[:, 15 + j:16 + j], stat[:, 1 + j:2 + j], ALU.mult, ALU.mult).then_inc(s_scaled, 1)
            dve.wait_ge(p_turned, 1)
            step(nc.vector.tensor_copy(pts[:], view(s.ps[:, 4, 0:1], [R_, PAGES], [1, R_])))
            dve.wait_ge(p_turned, 2)
            step(nc.vector.tensor_copy(ptw[:], view(s.ps[:, 5, 0:1], [R_, 4], [1, R_])))
            step(nc.vector.tensor_copy(ptn[:], view(s.ps[0:B, 5, 256:257], [R_, 2], [1, R_])))
            for r in range(G):
                at = slice(NBP * r, NBP * r + NBP)
                step(nc.vector.tensor_copy(ptc[at, :, r, :], view(s.ps[at, 5, 384 + H * r:385 + H * r], [32, 2], [1, H])))
            sync()
            dve.sem_inc(p_kept, 1)
            dve.wait_ge(o_out, 1)
            nc.vector.tensor_copy(ot[:], s.ps[:, 7, 0:R_]).then_inc(o_kept, 1)
            dve.wait_ge(o_turned, 1)
            step(ts(on[:, 1, :], s.ps[0:R_, 6, 0:HD], s.small[0:R_, S_SEL + 2:S_SEL + 3], None, ALU.mult))
            sync()
            nc.vector.scalar_tensor_tensor(on[:, 0, :], s.ps[0:R_, 6, HD:2 * HD], s.small[0:R_, S_SEL + 3:S_SEL + 4], on[:, 1, :],
                                           ALU.mult, ALU.add).then_inc(o_sel, 1)
            dve.wait_ge(y_in, 32)
            tt(ys[:, 0, :], ys[:, 0, :], ys[:, 1, :], ALU.mult).then_inc(y_done, 1)
            dve.wait_ge(y_done, 1)

        @block.tensor
        def _(pe):
            pe.wait_ge(small_in, 48)
            pe.wait_ge(zero_c, 2)
            pe.wait_ge(qb_ready, 1)
            for b in range(B):
                last = nc.tensor.matmul(s.ps[0:R_, 3, 16:16 + NBP], qb[:, b, :], s.cks[:, NBP * b:NBP * b + NBP], start=(b == 0), stop=(b == B - 1))
            last.then_inc(c_scored, 1)
            for j in range(2):
                last = nc.tensor.matmul(s.ps[0:R_, 3, B * j:B * j + B], s.qfull[:].rearrange("p b h -> p (b h)"), s.knew[:, j, :], start=True, stop=True)
            last.then_inc(c_scored, 1)

            def turn(b):
                pe.wait_ge(k_in[b % 2], 16 * (PAGES + 1) * (b // 2 + 1))
                for part in range(3):
                    if b:
                        pe.wait_ge(evac_a if part == 1 else evac_v, b if part == 1 else 2 * b - (1 if part == 0 else 0))
                    for j in range(4):
                        last = nc.tensor.transpose(s.ps[:, 4 + part, P * j:P * j + P], kraw[:, b % 2, 4 * part + j, :], s.ident[:])
                    last.then_inc(turned, 1)

            def score(b):
                pe.wait_ge(evac_a, b + 1)
                pe.wait_ge(evac_v, 2 * b + 2)
                for part in range(3):
                    last = nc.tensor.matmul(s.ps[0:R_, part, :], qb[:, b, :], ktr[:, b % 2, 512 * part:512 * part + 512],
                                            start=(b == 0), stop=(b == B - 1))
                last.then_inc(scored, 1)

            turn(0)
            for b in range(B):
                if b + 1 < B:
                    turn(b + 1)
                score(b)
            pe.wait_ge(c_norm, 1)
            nc.tensor.matmul(s.ps[0:R_, 3, 64:64 + NBP], groups[:], pc[:, 1, :], start=True, stop=True).then_inc(c_grouped, 1)
            pe.wait_ge(s_scaled, 1)
            for j in range(PAGES):
                last = nc.tensor.transpose(s.ps[:, 4, R_ * j:R_ * j + R_], sc[:, P * j:P * j + P], s.ident[0:R_, 0:R_])
            last.then_inc(p_turned, 1)
            pe.wait_ge(s_scaled, 2)
            for j in range(4):
                nc.tensor.transpose(s.ps[:, 5, R_ * j:R_ * j + R_], sc[:, W0 + P * j:W0 + P * j + P], s.ident[0:R_, 0:R_])
            for j, a in enumerate((N1, W0 + WIN)):
                nc.tensor.transpose(s.ps[0:B, 5, 256 + R_ * j:256 + R_ * j + R_], sc[:, a:a + B], s.ident[0:R_, 0:R_])
            nc.tensor.transpose(s.ps[:, 5, 384:384 + R_], pc[:].rearrange("p a c -> p (a c)"), s.ident[0:R_, 0:R_]).then_inc(p_turned, 1)
            pe.wait_ge(p_kept, 1)
            for b in range(B):
                pe.wait_ge(v_in[b], 16 * (PAGES + 1))
                cols = slice(H * b, H * b + H)
                out = s.ps[:, 7, cols]
                for j in range(PAGES):
                    nc.tensor.matmul(out, vs[:, b, j, :], pts[:, j, cols], start=(j == 0), stop=False)
                for j in range(4):
                    nc.tensor.matmul(out, vs[:, b, PAGES + j, :], ptw[:, j, cols], start=False, stop=False)
                for j in range(2):
                    nc.tensor.matmul(out, s.vnew[0:B, j, :], ptn[:, j, cols], start=False, stop=False)
                last = nc.tensor.matmul(out, s.cvs[:, b // G, :], ptc[:, b // G, b % G, :], start=False, stop=True)
            last.then_inc(o_out, 1)
            pe.wait_ge(o_kept, 1)
            nc.tensor.transpose(s.ps[0:R_, 6, 0:P], ot[:], s.ident[:]).then_inc(o_turned, 1)

def retain_sample(nc, s, io):
    m = Memory(nc, s.x_region)
    st = m.put("s_state", [P, B, 4, HD])
    vb = m.put("s_v_spread", [P, B, 4, HD])
    pq = m.put("s_pq", [P, B, 4, HD])
    qk = m.put("s_qk", [P, 2, B * 4])
    so = m.put("s_out", [2, B * 4 * HD])
    y = m.put("s_y", [B, 3, 512])
    stat = m.put("s_stats", [B, 32])
    with ExitStack() as ctx:
        sem = s.semaphore
        r_in, st_ready, st_out, pq_ready, summed, so_kept, so_out, o_in, mean, root, y_ready, y_out = (
            sem("e_in"), sem("e_state"), sem("e_state_out"), sem("e_pq"), sem("e_summed"), sem("e_kept"), sem("e_stored"),
            sem("e_o_in"), sem("e_mean"), sem("e_root"), sem("e_y"), sem("e_y_out"))
        v_steps = sem("e_v_steps")
        block = ctx.enter_context(nc.Block())

        @block.sync
        def _(sp):
            for e in range(2):
                at = slice(HD * e, HD * e + HD)
                for b in range(B):
                    sp.dma_start(st[at, b, :, :], dram(io["state_ret"], (H * b + e) * HD * HD, [HD, HD], [2 * HD * HD, 4], [1, HD])).then_inc(r_in, 16)
                    sp.dma_start(vb[at, b, :, :], dram(io["ret_rows"], (2 * B + b) * 512 + HD * e, [0, HD], [P, 4], [1, HD])).then_inc(r_in, 16)
            for j in range(2):
                sp.dma_start(qk[:, j, :], dram(io["ret_rows"], j * B * 512, [1, P], [P, B * 4]), allow_slow_non_contiguous=True).then_inc(r_in, 16)
            sp.dma_start(y[:, 1, :], io["y"][T:ROWS, 512:1024]).then_inc(r_in, 16)
            sp.wait_ge(st_ready, 1)
            for e in range(2):
                at = slice(HD * e, HD * e + HD)
                for b in range(B):
                    sp.dma_start(dram(io["s_ret"], (H * b + e) * HD * HD, [HD, HD], [2 * HD * HD, 4], [1, HD]), st[at, b, :, :]).then_inc(st_out, 16)
            sp.wait_ge(so_kept, 4)
            sp.dma_start(dram(io["scratch"], 2 * 65536, [2048, 2], [1, 2048]), so[:]).then_inc(so_out, 16)
            sp.wait_ge(so_out, 16)
            for e in range(2):
                sp.dma_start(view(y[:, 0, HD * e:HD * e + 1], [P, 4], [1, HD]), dram(io["scratch"], 2 * 65536 + 2048 * e, [256, B], [HD, 4], [1, HD])).then_inc(o_in, 16)
            sp.wait_ge(y_ready, 1)
            sp.dma_start(io["y"][T:ROWS, 512:1024], y[:, 0, :]).then_inc(y_out, 16)
            sp.wait_ge(y_out, 16)
            sp.wait_ge(st_out, 256)

        @block.gpsimd
        def _(pool):
            pool.wait_ge(mean, 1)
            nc.gpsimd.tensor_tensor(stat[:, 16:24], stat[:, 16:24], view(s.small[0:B, S_HALF:S_HALF + 1], [0, H]), ALU.pow).then_inc(root, 1)

        @block.vector
        def _(dve):
            own = Chain(dve, v_steps)
            step, sync, tt, ts = own.step, own.sync, nc.vector.tensor_tensor, nc.vector.tensor_scalar
            every = lambda ap: view(ap, [256, B], [HD, 4], [1, HD])
            of_row = lambda j: view(qk[:, j, 0:1], [1, 32], [0, HD])
            rows = lambda ap: view(ap, [HD, 32], [1, HD])
            heads = lambda ap: view(ap, [HD, H], [1, HD])
            dve.wait_ge(r_in, 16 * 35)
            step(ts(qk[:, 1, :], qk[:, 1, :], HD ** -0.5, None, ALU.mult))
            step(tt(every(st[:, 0, 0, 0:1]), every(st[:, 0, 0, 0:1]), view(s.small[:, S_GAM1:S_GAM1 + 1], [0, B], [1, 4], [0, HD]), ALU.mult))
            sync()
            step(tt(rows(vb[:, 0, 0, 0:1]), rows(vb[:, 0, 0, 0:1]), of_row(1), ALU.mult))
            sync()
            tt(rows(st[:, 0, 0, 0:1]), rows(st[:, 0, 0, 0:1]), rows(vb[:, 0, 0, 0:1]), ALU.add).then_inc(st_ready, 1)
            dve.wait_ge(st_ready, 1)
            tt(rows(pq[:, 0, 0, 0:1]), rows(st[:, 0, 0, 0:1]), of_row(0), ALU.mult).then_inc(pq_ready, 1)
            for j in range(4):
                dve.wait_ge(summed, j + 1)
                nc.vector.tensor_copy(so[:, 512 * j:512 * j + 512], s.ps[0:2, j, :]).then_inc(so_kept, 1)
            dve.wait_ge(o_in, 32)
            step(nc.vector.tensor_reduce(stat[:, 0:8], heads(y[:, 0, 0:1]), AX, ALU.add))
            sync()
            step(ts(stat[:, 8:16], stat[:, 0:8], 1.0 / HD, None, ALU.mult))
            sync()
            step(tt(heads(y[:, 0, 0:1]), heads(y[:, 0, 0:1]), view(stat[:, 8:9], [1, H], [0, HD]), ALU.subtract))
            sync()
            step(tt(y[:, 2, :], y[:, 0, :], y[:, 0, :], ALU.mult))
            sync()
            step(nc.vector.tensor_reduce(stat[:, 0:8], heads(y[:, 2, 0:1]), AX, ALU.add))
            sync()
            ts(stat[:, 16:24], stat[:, 0:8], 1.0 / HD, EPS, ALU.mult, ALU.add).then_inc(mean, 1)
            dve.wait_ge(root, 1)
            step(tt(heads(y[:, 0, 0:1]), heads(y[:, 0, 0:1]), view(stat[:, 16:17], [1, H], [0, HD]), ALU.mult))
            sync()
            tt(y[:, 0, :], y[:, 0, :], y[:, 1, :], ALU.mult).then_inc(y_ready, 1)
            dve.wait_ge(y_ready, 1)

        @block.tensor
        def _(pe):
            pe.wait_ge(pq_ready, 1)
            flat = pq[:].rearrange("p b j d -> p (b j d)")
            for j in range(4):
                nc.tensor.matmul(s.ps[0:2, j, :], s.small[:, S_SEL:S_SEL + 2], flat[:, 512 * j:512 * j + 512], start=True, stop=True).then_inc(summed, 1)


def attend_prompt(nc, s, io):
    RL, RP = 5, 3
    m = Memory(nc, s.x_region)
    full = m.put("bias_full", [P, H, T])
    wide = m.put("bias_window", [P, H, WIN + P])
    short = m.put("bias_short", [P, H, 2 * NBP])
    lg = m.put("unit_logits", [P, RL, T])
    pt = m.put("unit_pt", [P, RP, T])
    yt = m.put("y_tile", [P, 2, 512])
    zt = m.put("z_tile", [P, 2, 512])
    tmp = m.put("branch_tile", [P, 512])
    st = m.put("a_stats", [P, 128])
    relx = m.put("rel_bias_masked2", [33, H])
    assert m.at <= 229368, m.at
    hot = Memory(nc, s.x_region + 4 * H * T + 4 * H * (WIN + P) + 4 * H * 2 * NBP).put("one_hot2", [33, NBP * P])
    units = []
    for t in range(TT):
        units.append((t, "c", 0, 2))
        for h in range(H):
            units += [(t, "f", h, t + 1), (t, "w", h, min(t, WIN // P) + 1)]
    n_u = len(units)
    per_tile = 1 + 2 * H
    chunks = []
    first_chunk = []
    for u, (_, _, _, n) in enumerate(units):
        first_chunk.append(len(chunks))
        chunks += [(u, b0, min(4, n - b0)) for b0 in range(0, n, 4)]
    first_chunk.append(len(chunks))
    by_act = [k % 2 == 0 for k in range(len(chunks))]
    n_by = lambda k, act: sum(1 for j in range(k) if by_act[j] == act)
    fulls = lambda u: u // per_tile
    HALF = T // 2
    LB, LE, LC, LT, LP = 1, 2, 3, 3, 5
    in_turn = lambda u: 0 <= u < n_u

    with ExitStack() as ctx:
        sem = s.semaphore
        small_in, near_in, short_out, short_kept = sem("a_small_in"), sem("near_in"), sem("short_out"), sem("short_kept")
        far_in, wide_ready = sem("far_in"), sem("wide_ready")
        z_in = [sem(f"z_in{b}") for b in range(2)]
        scored, biased, exped, c_ready = sem("scored"), sem("biased"), sem("exped"), sem("c_ready")
        turned, kept_v, kept_a = sem("a_turned"), sem("kept_v"), sem("kept_a")
        weighed, c_used, tile_used = sem("weighed"), sem("c_used"), sem("tile_used")
        y_ready = sem("a_y_ready")
        y_out = [sem(f"a_y_out{b}") for b in range(2)]
        v_steps = sem("a_v_steps")
        block = ctx.enter_context(nc.Block())
        S_MIN, S_SUM = 0, 3
        S_F, S_W, S_C = 8, 24, 40

        @block.sync
        def _(sp):
            sp.dma_start(relx[0:32, :], io["rel_bias"]).then_inc(small_in, 16)
            sp.dma_start(hot[:], io["c_hot_cmp"]).then_inc(small_in, 16)
            rows = lambda h, first: io["skew"][bass.ds(h, 1), first:first + P * L_FULL].rearrange("a (p c) -> (a p) c", c=L_FULL)
            with sp.Fori(0, H) as h:
                sp.dma_start(full[:, bass.ds(h, 1), HALF:T].rearrange("p a c -> p (a c)"), rows(h, P - 1 + HALF)[:, 0:HALF]).then_inc(near_in, 16)
            with sp.Fori(0, H) as h:
                sp.dma_start(full[:, bass.ds(h, 1), 0:HALF].rearrange("p a c -> p (a c)"), rows(h, P - 1)[:, 0:HALF]).then_inc(far_in, 16)
            for t in range(TT):
                if t >= 2:
                    sp.wait_ge(y_ready, t - 1)
                sp.dma_start(zt[:, t % 2, :], io["zn"][P * t:P * t + P, :]).then_inc(z_in[t % 2], 16)
                if t >= 1:
                    sp.wait_ge(y_ready, t)
                    sp.dma_start(io["y"][P * (t - 1):P * t, 0:512], yt[:, (t - 1) % 2, :]).then_inc(y_out[(t - 1) % 2], 16)
            sp.wait_ge(y_ready, TT)
            sp.dma_start(io["y"][T - P:T, 0:512], yt[:, (TT - 1) % 2, :]).then_inc(y_out[(TT - 1) % 2], 16)
            for b in range(2):
                sp.wait_ge(y_out[b], 16 * TT // 2)

        @block.gpsimd
        def _(pool):
            nc.gpsimd.memset(relx[32:33, :], MASK).then_inc(short_kept, 1)
            pool.wait_ge(short_kept, 1)
            nc.gpsimd.memset(short[:], MASK).then_inc(short_kept, 1)
            pool.wait_ge(short_kept, 2)
            pool.wait_ge(near_in, 16 * H)
            pool.wait_ge(far_in, 16 * H)
            nc.gpsimd.tensor_copy(wide[:], full[:, :, T - WIN - P:T]).then_inc(wide_ready, 1)
            pool.wait_ge(wide_ready, 1)
            nc.gpsimd.affine_select(out=wide[:, :, 0:P], in_=wide[:, :, 0:P], compare_op=ALU.is_gt, fill=MASK, base=0,
                                    pattern=[[0, H], [1, P]], channel_multiplier=-1).then_inc(wide_ready, 1)
            pool.wait_ge(wide_ready, 2)

        def keep(k, engine_wait, copy, done):
            u, b0, n = chunks[k]
            engine_wait(turned, k + 1)
            if u >= RP:
                engine_wait(weighed, u - RP + 1)
            copy(pt[:, u % RP, P * b0:P * b0 + P * n], s.ps[:, 4 + k % 2, 0:P * n]).then_inc(done, 1)

        @block.scalar
        def _(act):
            def exp(u):
                t, br, h, n = units[u]
                if br == "c":
                    act.wait_ge(c_ready, fulls(u) + 1)
                    nc.scalar.activation(lg[:, u % RL, 0:H * NBP], lg[:, u % RL, 0:H * NBP], ACT.Exp, scale=-1.0).then_inc(exped, 1)
                else:
                    at = (S_F if br == "f" else S_W) + H * (t % 2) + h
                    act.wait_ge(biased, u + 1)
                    if t >= 2 and h == 0:
                        act.wait_ge(tile_used, t - 1)
                    nc.scalar.activation(lg[:, u % RL, 0:P * n], lg[:, u % RL, 0:P * n], ACT.Exp, scale=-1.0,
                                         bias=st[:, S_MIN + u % RL:S_MIN + u % RL + 1], accum_out=st[:, at:at + 1]).then_inc(exped, 1)

            for i in range(n_u + LP):
                if in_turn(i - LE):
                    exp(i - LE)
                if in_turn(i - LT):
                    for k in range(first_chunk[i - LT], first_chunk[i - LT + 1]):
                        if by_act[k]:
                            keep(k, act.wait_ge, lambda out, in_: nc.scalar.activation(out, in_, ACT.Copy), kept_a)

        @block.vector
        def _(dve):
            own = Chain(dve, v_steps)
            step, sync, tt, ts = own.step, own.sync, nc.vector.tensor_tensor, nc.vector.tensor_scalar
            blocks = lambda ap: view(ap, [NBP, H], [1, NBP])
            heads = lambda ap: view(ap, [HD, H], [1, HD])
            per_head = lambda c: view(st[:, c:c + 1], [1, H], [0, HD])
            gate = lambda t, j: view(s.gates[:, t, j:j + 1], [3, H])

            def bias(u):
                t, br, h, n = units[u]
                dve.wait_ge(scored, u + 1)
                if u >= RL:
                    dve.wait_ge(turned, first_chunk[u - RL + 1])
                pair = s.ps[:, 2 * (u % 2):2 * (u % 2) + 2, :].rearrange("p a c -> p (a c)")
                if br == "c":
                    v0 = 4 * (TT - 1 - t)
                    l = lg[:, u % RL, 0:H * NBP]
                    step(nc.vector.scalar_tensor_tensor(blocks(l), blocks(pair), -1.0, view(short[:, 0, v0:v0 + 1], [2 * NBP, H], [1, NBP]),
                                                        ALU.mult, ALU.subtract))
                    sync()
                    dve.sem_inc(biased, 1)
                    step(nc.vector.tensor_reduce(st[:, 48:56], blocks(l), AX, ALU.min))
                    sync()
                    step(ts(st[:, 56:64], st[:, 48:56], -FLOOR, None, ALU.min))
                    sync()
                    tt(blocks(l), blocks(l), view(st[:, 56:57], [1, H], [0, NBP]), ALU.subtract).then_inc(c_ready, 1)
                else:
                    if P * t == HALF and h == 0:
                        if br == "f":
                            dve.wait_ge(far_in, 16 * H)
                        else:
                            dve.wait_ge(wide_ready, 2)
                    strip = full[:, h, T - P * n:T] if br == "f" or P * n <= WIN else wide[:, h, :]
                    nc.vector.tensor_tensor_reduce(out=lg[:, u % RL, 0:P * n], in0=pair[:, 0:P * n], in1=strip, scale=-1.0, scalar=-FLOOR,
                                                   op0=ALU.add, op1=ALU.min, accum_out=st[:, S_MIN + u % RL:S_MIN + u % RL + 1]).then_inc(biased, 1)

            def c_sums(u):
                dve.wait_ge(exped, u + 1)
                step(nc.vector.tensor_reduce(st[:, 64:72], blocks(lg[:, u % RL, 0:H * NBP]), AX, ALU.add))
                sync()
                step(ts(st[:, 64:72], st[:, 64:72], 1e-30, None, ALU.max))
                sync()
                step(nc.vector.reciprocal(st[:, 72:80], st[:, 64:72]))
                sync()
                step(tt(st[:, 72:80], st[:, 72:80], gate(units[u][0], 0), ALU.mult))
                sync()

            def c_out(u):
                t = units[u][0]
                dve.wait_ge(weighed, u + 1)
                if t >= 2:
                    dve.wait_ge(y_out[t % 2], 16 * (t // 2))
                tt(heads(yt[:, t % 2, :]), heads(s.ps[:, 7, :]), per_head(72), ALU.mult).then_inc(c_used, 1)

            def tile_end(t):
                u_last = per_tile * (t + 1) - 1
                y = yt[:, t % 2, :]
                dve.wait_ge(weighed, u_last + 1)
                dve.wait_ge(c_used, t + 1)
                for j, (c, bank) in enumerate(((S_F, 6), (S_W, 7))):
                    a = c + H * (t % 2)
                    step(nc.vector.reciprocal(st[:, 80 + 8 * j:88 + 8 * j], st[:, a:a + H]))
                    sync()
                    step(tt(st[:, 80 + 8 * j:88 + 8 * j], st[:, 80 + 8 * j:88 + 8 * j], gate(t, 1 + j), ALU.mult))
                    sync()
                    step(tt(heads(tmp[:]), heads(s.ps[:, bank, :]), per_head(80 + 8 * j), ALU.mult))
                    sync()
                    step(tt(y, y, tmp[:], ALU.add))
                    sync()
                dve.sem_inc(tile_used, 1)
                dve.wait_ge(z_in[t % 2], 16 * (t // 2 + 1))
                tt(y, y, zt[:, t % 2, :], ALU.mult).then_inc(y_ready, 1)

            dve.wait_ge(short_kept, 2)
            dve.wait_ge(short_out, 1)
            step(nc.vector.tensor_copy(short[:, :, 0:NBP], view(s.ps[:, 0, 0:1], [1, H], [H, NBP])))
            sync()
            dve.sem_inc(short_kept, 1)
            dve.wait_ge(near_in, 16 * H)
            for i in range(n_u + LP + 1):
                if in_turn(i - LB):
                    bias(i - LB)
                if in_turn(i - LC) and units[i - LC][1] == "c":
                    c_sums(i - LC)
                if in_turn(i - LT):
                    for k in range(first_chunk[i - LT], first_chunk[i - LT + 1]):
                        if not by_act[k]:
                            keep(k, dve.wait_ge, nc.vector.tensor_copy, kept_v)
                v = i - LP
                if in_turn(v) and units[v][1] == "c":
                    c_out(v)
                if in_turn(v) and v % per_tile == per_tile - 1:
                    tile_end(units[v][0])
            dve.wait_ge(y_ready, TT)

        @block.tensor
        def _(pe):
            def score(u):
                t, br, h, n = units[u]
                if u >= 2:
                    pe.wait_ge(biased, u - 1)
                q = lambda h: s.qs[:, h, P * t:P * t + P]
                b0 = 2 * (u % 2)
                if br == "c":
                    for h in range(H):
                        out = s.ps[:, b0, NBP * h:NBP * h + NBP]
                        nc.tensor.matmul(out, q(h), s.ck_h[:, h // G, :], start=True, stop=False)
                        last = nc.tensor.matmul(out, q(h), s.ck_l[:, h // G, :], start=False, stop=True)
                    last.then_inc(scored, 1)
                    return
                j, k0 = (0, 0) if br == "f" else (1, P * (t + 1 - n))
                for c in range(0, P * n, 512):
                    w = min(512, P * n - c)
                    out = s.ps[:, b0 + c // 512, 0:w]
                    nc.tensor.matmul(out, q(h), s.kh[:, j, h // G, k0 + c:k0 + c + w], start=True, stop=False)
                    last = nc.tensor.matmul(out, q(h), s.kl[:, j, h // G, k0 + c:k0 + c + w], start=False, stop=True)
                last.then_inc(scored, 1)

            def turn(u):
                pe.wait_ge(exped, u + 1)
                for k in range(first_chunk[u], first_chunk[u + 1]):
                    if k >= 2:
                        j = k - 2
                        pe.wait_ge(kept_a if by_act[j] else kept_v, n_by(j, by_act[j]) + 1)
                    _, b0, n = chunks[k]
                    for b in range(n):
                        last = nc.tensor.transpose(s.ps[:, 4 + k % 2, P * b:P * b + P], lg[:, u % RL, P * (b0 + b):P * (b0 + b) + P], s.ident[:])
                    last.then_inc(turned, 1)

            def weigh(u):
                t, br, h, n = units[u]
                k = first_chunk[u + 1]
                pe.wait_ge(kept_a, n_by(k, True))
                if n_by(k, False):
                    pe.wait_ge(kept_v, n_by(k, False))
                if br == "c":
                    if t >= 1:
                        pe.wait_ge(tile_used, t)
                    for kv in range(HKV):
                        last = nc.tensor.matmul(s.ps[:, 7, 256 * kv:256 * kv + 256], pt[:, u % RP, P * kv:P * kv + P],
                                                s.cv_bd[:, kv, :, :].rearrange("p g d -> p (g d)"), start=True, stop=True)
                    last.then_inc(weighed, 1)
                    return
                if br == "w" and h == 0:
                    pe.wait_ge(c_used, t + 1)
                j = 0 if br == "f" else 1
                for b in range(n):
                    last = nc.tensor.matmul(s.ps[:, 6 + j, HD * h:HD * h + HD], pt[:, u % RP, P * b:P * b + P],
                                            s.v[:, j, t + 1 - n + b, HD * (h // G):HD * (h // G) + HD], start=(b == 0), stop=(b == n - 1))
                last.then_inc(weighed, 1)

            pe.wait_ge(small_in, 32)
            pe.wait_ge(short_kept, 2)
            for v in range(NBP):
                last = nc.tensor.matmul(s.ps[:, 0, H * v:H * v + H], hot[:, P * v:P * v + P], relx[:], start=True, stop=True)
            last.then_inc(short_out, 1)
            pe.wait_ge(short_kept, 3)
            for i in range(n_u + LP):
                if in_turn(i):
                    score(i)
                if in_turn(i - LT):
                    turn(i - LT)
                if in_turn(i - LP):
                    weigh(i - LP)


def project_out(nc, s, io):
    m = Memory(nc, s.k_region)
    yt = m.put("y_rows_in", [P, 2, D])
    xr = m.put("x_rows", [P, 2, 512])
    out = m.put("out_rows", [P, 2, 512])
    n_idx = 2 * NT
    with ExitStack() as ctx:
        sem = s.semaphore
        y_in = [sem(f"o_y_in{b}") for b in range(2)]
        x_in = [sem(f"o_x_in{b}") for b in range(2)]
        w_in = [sem(f"o_w_in{k}") for k in range(KT)]
        turned, y_high, y_low, w_high, w_low, w_used = sem("y_turned"), sem("o_y_high"), sem("o_y_low"), sem("o_w_high"), sem("o_w_low"), sem("o_w_used")
        projected, added = sem("o_projected"), sem("o_added")
        stored = [sem(f"o_stored{b}") for b in range(2)]
        block = ctx.enter_context(nc.Block())
        yh, yl = s.xh, s.xl

        @block.sync
        def _(sp):
            def load_w(g):
                for k in range(KT):
                    if g:
                        sp.wait_ge(w_low, k + 1)
                    sp.dma_start(s.wraw[:, k, :], io["w_out"][P * k:P * k + P, 512 * g:512 * g + 512]).then_inc(w_in[k], 16)
            load_w(0)
            def load_y(t):
                if t >= 2:
                    sp.wait_ge(turned, 2 * (t - 1))
                sp.dma_start(yt[0:rows_of(t), t % 2, :], io["y"][P * t:P * t + rows_of(t), :]).then_inc(y_in[t % 2], 16)

            load_y(0)
            load_y(1)
            for i in range(n_idx + 1):
                if i + 2 < NT:
                    load_y(i + 2)
                if i == 1:
                    load_w(1)
                if i < n_idx:
                    g, t = i // NT, i % NT
                    if i >= 2:
                        sp.wait_ge(added, i - 1)
                    src = io["xp"][P * t:P * t + P, :] if t < TT else io["xs"]
                    sp.dma_start(xr[0:rows_of(t), i % 2, :], src[:, 512 * g:512 * g + 512]).then_inc(x_in[i % 2], 16)
                if i >= 1:
                    g, t = (i - 1) // NT, (i - 1) % NT
                    sp.wait_ge(added, i)
                    to = io["yp"][P * t:P * t + P, :] if t < TT else io["ys"]
                    sp.dma_start(to[:, 512 * g:512 * g + 512], out[0:rows_of(t), (i - 1) % 2, :]).then_inc(stored[(i - 1) % 2], 16)
            for b in range(2):
                sp.wait_ge(stored[b], 16 * NT)

        @block.scalar
        def _(act):
            def split_w(g):
                for k in range(KT):
                    act.wait_ge(w_in[k], 16 * (g + 1))
                    if g:
                        act.wait_ge(w_used, k + 1)
                    nc.scalar.activation(s.wh[:, k, :], s.wraw[:, k, :], ACT.Copy).then_inc(w_high, 1)
            split_w(0)
            for t in range(NT):
                n = rows_of(t)
                for half in range(2):
                    i = 2 * t + half
                    act.wait_ge(turned, i + 1)
                    nc.scalar.activation(yh[:, 4 * half:4 * half + 4, P * t:P * t + n],
                                         view(s.ps[:, 4 + i % 4, 0:1], [P, 4], [1, n]), ACT.Copy).then_inc(y_high, 1)
            split_w(1)

        @block.vector
        def _(dve):
            def split_w(g):
                for k in range(KT):
                    dve.wait_ge(w_high, KT * g + k + 1)
                    nc.vector.tensor_tensor(s.wl[:, k, :], s.wraw[:, k, :], f32(s.wh[:, k, :]), ALU.subtract).then_inc(w_low, 1)

            def add(i):
                n = rows_of(i % NT)
                dve.wait_ge(projected, i + 1)
                dve.wait_ge(x_in[i % 2], 16 * (i // 2 + 1))
                if i >= 2:
                    dve.wait_ge(stored[i % 2], 16 * (i // 2))
                nc.vector.tensor_tensor(out[0:n, i % 2, :], s.ps[0:n, i % 4, :], xr[0:n, i % 2, :], ALU.add).then_inc(added, 1)

            split_w(0)
            for t in range(NT):
                n = rows_of(t)
                for half in range(2):
                    i = 2 * t + half
                    dve.wait_ge(y_high, i + 1)
                    cols = (slice(None), slice(4 * half, 4 * half + 4), slice(P * t, P * t + n))
                    nc.vector.tensor_tensor(yl[cols], view(s.ps[:, 4 + i % 4, 0:1], [P, 4], [1, n]), f32(yh[cols]),
                                            ALU.subtract).then_inc(y_low, 1)
                if t >= 2:
                    add(t - 2)
            split_w(1)
            for i in range(NT - 2, n_idx):
                add(i)
            dve.wait_ge(added, n_idx)

        @block.tensor
        def _(pe):
            def turn(t):
                n = rows_of(t)
                pe.wait_ge(y_in[t % 2], 16 * (t // 2 + 1))
                for half in range(2):
                    i = 2 * t + half
                    if i >= 4:
                        pe.wait_ge(y_low, i - 3)
                    for j in range(4):
                        k = 4 * half + j
                        last = nc.tensor.transpose(s.ps[:, 4 + i % 4, P * j:P * j + n], yt[0:n, t % 2, P * k:P * k + P], s.ident[0:n, 0:n])
                    last.then_inc(turned, 1)

            def proj(i):
                g, t = i // NT, i % NT
                n = rows_of(t)
                if i >= 4:
                    pe.wait_ge(added, i - 3)
                if g == 0:
                    pe.wait_ge(y_low, 2 * (t + 1))
                for k in range(KT):
                    if t == 0:
                        pe.wait_ge(w_low, KT * g + k + 1)
                    rows = slice(P * t, P * t + n)
                    to = s.ps[0:n, i % 4, :]
                    nc.tensor.matmul(to, yh[:, k, rows], s.wh[:, k, :], start=(k == 0), stop=False)
                    nc.tensor.matmul(to, yh[:, k, rows], s.wl[:, k, :], start=False, stop=False)
                    ins = nc.tensor.matmul(to, yl[:, k, rows], s.wh[:, k, :], start=False, stop=(k == KT - 1))
                    if t == TT and g == 0:
                        ins.then_inc(w_used, 1)
                if t == TT and g == 0:
                    pe.wait_ge(w_used, KT)
                    pe.sem_inc(projected, 1)
                else:
                    ins.then_inc(projected, 1)

            turn(0)
            turn(1)
            for i in range(n_idx):
                if i + 2 < NT:
                    turn(i + 2)
                proj(i)


def build(nc, io):
    s = Shared(nc)
    layout(nc, s)
    persistent_compressed(nc, s)
    with nc.psum_tensor("ps", [P, 8, 512], F32) as ps:
        s.ps = ps
        normalise_x(nc, s, io)
        between(nc, s)
        project(nc, s, io)
        between(nc, s)
        compress(nc, s, io)
        between(nc, s)
        attend_sample(nc, s, io)
        between(nc, s)
        retain_sample(nc, s, io)
        between(nc, s)
        attend_prompt(nc, s, io)
        between(nc, s)
        project_out(nc, s, io)


def bucket_one_hot(dist, masked):
    n = np.maximum(dist, 0)
    ratio = np.log(np.maximum(n, 1).astype(np.float32) / np.float32(16)) / np.float32(math.log(64))
    large = np.minimum(16 + (ratio * np.float32(16)).astype(np.int32), 31)
    bucket = np.where(masked, 32, np.where(n < 16, n, large))
    return (np.arange(33)[:, None] == bucket.reshape(1, -1)).astype(np.float32)


def constants():
    c = {}
    half = HD // 2
    inv = np.float32(10000.0) ** (-np.arange(half, dtype=np.float32) / np.float32(half))
    pos = np.minimum(np.arange(NT * P).reshape(NT, P).T, T).astype(np.float32)
    ang = pos[:, :, None] * inv.astype(np.float32)
    cos, sin = np.cos(ang), np.sin(ang)
    c["c_rope"] = np.stack([np.concatenate([cos, cos], -1), np.concatenate([-sin, sin], -1)], 1).reshape(P, -1)
    log_g = np.log1p(-np.exp2(-5.0 - np.arange(H)))
    i = np.arange(P)
    diff = i[None, :] - i[:, None]
    scale = HD ** -0.5
    dec = np.where(diff >= 0, np.exp(np.maximum(diff, 0)[None] * log_g[:, None, None]), 0.0) * scale
    c["c_dec"] = dec.transpose(1, 0, 2).reshape(P, -1)
    part_head = 2 * np.arange(4)[None, :] + (i[:, None] // HD)
    c["c_qdec"] = np.exp((i[None, None, :] + 1.0) * log_g[part_head][:, :, None]).reshape(P, -1)
    small = np.zeros((P, S_WIDTH))
    small[:, S_KDEC:S_KDEC + 8] = np.exp((P - 1.0 - i)[:, None] * log_g[None, :]) * scale
    small[:, S_GAM128:S_GAM128 + 8] = np.exp(P * log_g)[None, :]
    small[:, S_GAM1:S_GAM1 + 4] = np.exp(log_g)[part_head]
    small[:, S_HALF] = -0.5
    small[:, S_SEL] = i < HD
    small[:, S_SEL + 1] = i >= HD
    small[:, S_SEL + 2] = (i % 8) < G
    small[:, S_SEL + 3] = (i % 8) >= G
    c["c_small"] = small
    k = np.arange
    dist = np.concatenate([1023 - k(L_FULL), T - k(L_SLC), WIN - k(L_SWIN), T - (CB - 1) - CB * k(L_SCMP), 0 * k(32)])
    masked = dist < 0
    masked[O_SWIN:O_SWIN + L_SWIN] |= dist[O_SWIN:O_SWIN + L_SWIN] >= WIN
    c["c_hot"] = bucket_one_hot(dist, masked)
    dist = k(P)[None, :] - (CB - 1) + CB * (28 - k(NBP)[:, None])
    c["c_hot_cmp"] = bucket_one_hot(dist, dist < 0)
    row = k(R_) // H
    c["c_own"] = np.where(row[:, None] == k(B)[None, :], 0.0, MASK)
    c["c_group"] = (k(R_)[:, None] // G == k(R_)[None, :] // G)
    c["c_order"] = np.broadcast_to(k(16) + 1.0, (R_, 16))
    return {k: np.ascontiguousarray(v, dtype=np.float32) for k, v in c.items()}


_INS = ["x_prompt", "x_sample", "cache_cmp_k", "cache_cmp_v", "cache_slc_k", "cache_slc_v", "cache_win_k", "cache_win_v",
        "state_ret", "page_table", "norm_g", "w_in", "q_norm_g", "k_norm_g", "cmp_pe_k", "cmp_w1_k", "cmp_w2_k",
        "cmp_pe_v", "cmp_w1_v", "cmp_w2_v", "rel_bias", "ret_gn_g", "w_out"]
_KV1, _KVS = (1, T, HKV, HD), (B, 1, HKV, HD)
_OUTS = [("y_prompt", (1, T, D)), ("y_sample", (B, 1, D)),
         ("p_cmp_k", _KV1), ("p_cmp_v", _KV1), ("p_slc_k", _KV1), ("p_slc_v", _KV1),
         ("p_win_k", (1, WIN, HKV, HD)), ("p_win_v", (1, WIN, HKV, HD)), ("p_ret", (1, H, HD, HD)),
         ("s_cmp_k", _KVS), ("s_cmp_v", _KVS), ("s_slc_k", _KVS), ("s_slc_v", _KVS),
         ("s_win_k", (B, WIN, HKV, HD)), ("s_win_v", (B, WIN, HKV, HD)), ("s_ret", (B, H, HD, HD))]


def flat_rows(io):
    io["xp"] = io["x_prompt"].rearrange("a t d -> (a t) d")
    io["xs"] = io["x_sample"].rearrange("b s d -> (b s) d")
    prompt = lambda a: a.rearrange("a t h d -> (a t) (h d)")
    sample = lambda a: a.rearrange("b s h d -> (b s) (h d)")
    io["yp"], io["ys"] = io["y_prompt"].rearrange("a t d -> (a t) d"), io["y_sample"].rearrange("b s d -> (b s) d")
    parts = ("cmp_k", "cmp_v", "slc_k", "slc_v")
    io["prompt_out"] = {n: prompt(io["p_" + n]) for n in parts}
    io["sample_out"] = {n: sample(io["s_" + n]) for n in parts}
    io["p_win_k"], io["p_win_v"] = prompt(io["p_win_k"]), prompt(io["p_win_v"])
    window = lambda a: a.rearrange("b t h d -> b t (h d)")
    io["s_win_k"], io["s_win_v"] = window(io["s_win_k"]), window(io["s_win_v"])
    io["cache_win_k"], io["cache_win_v"] = window(io["cache_win_k"]), window(io["cache_win_v"])


def kernel(**inputs):
    import numpy as _np
    import concourse.bacc as _bacc
    from concourse import mybir as _mybir
    from concourse.bass_utils import run_bass_kernel_spmd as _run

    nc = _bacc.Bacc("TRN2", target_bir_lowering=False, num_devices=1)
    arrays, io = {}, {}
    for name, a in [(n, inputs[n]) for n in _INS] + list(constants().items()):
        a = _np.ascontiguousarray(a)
        arrays[f"in_{name}"] = a
        io[name] = (nc.dram_tensor(f"in_{name}", a.shape, _mybir.dt.from_np(a.dtype), kind="ExternalInput").ap())
    for name, shape in _OUTS:
        io[name] = (nc.dram_tensor(f"out_{name}", list(shape), F32, kind="ExternalOutput").ap())
    for name, shape in (("y", (ROWS, D)), ("zn", (ROWS, 512)), ("ret_rows", (3, B, 512)), ("scratch", (8, 65536)), ("table", (H, L_TABLE)), ("skew", (H, L_SKEW))):
        io[name] = (nc.dram_tensor(f"tmp_{name}", list(shape), F32).ap())
    flat_rows(io)
    build(nc, io)
    r = _run(nc, [arrays], core_ids=[0])
    return tuple(r.results[0][f"out_{name}"] for name, _ in _OUTS)
```

```python
import math
from contextlib import ExitStack

import numpy as np
import concourse.bass as bass
from concourse import mybir
from concourse.alu_op_type import AluOpType as ALU

ACT = mybir.ActivationFunctionType
AX = mybir.AxisListType.X
F32 = mybir.dt.float32
F32R = mybir.dt.float32r
I32 = mybir.dt.int32

P = 128
D = 1024
T = 1024
TT = T // P
NT = TT + 1
B = 8
ROWS = T + B
KT = D // P
H, HKV, G, HD = 8, 2, 4, 64
KVW = HKV * HD
PAGES = 8
N_PHYS = 80
WIN = 512
EPS = 1e-6
MASK = -1e30
FLOOR = -1e29
C_Q, C_KV, C_WG, C_ZN, C_QR, C_KR, C_VR, C_ZR = 0, 512, 1024, 1304, 1816, 2328, 2840, 3352
GROUPS = [("qr", C_QR, 512), ("kr", C_KR, 512), ("vr", C_VR, 512), ("zr", C_ZR, 512),
          ("zn", C_ZN, 512), ("wg", C_WG, 280), ("kv", C_KV, 512), ("q", C_Q, 512)]
KIND = [g[0] for g in GROUPS]
NG = len(GROUPS)

CB = 32
NBP = T // CB
NBS = B * NBP

L_FULL, L_SLC, L_SWIN, L_SCMP = T + P, T, WIN, NBP
O_FULL, O_SLC = 0, L_FULL
L_SKEW = P * (L_FULL + 1) + T
O_SWIN = O_SLC + L_SLC
O_SCMP = O_SWIN + L_SWIN
O_NEW = O_SCMP + L_SCMP
L_SAMPLE = L_SLC + L_SWIN + L_SCMP + 1
L_TABLE = O_NEW + 32
N_HOT = -(-L_TABLE // 512)

S_KDEC, S_GAM128, S_GAM1, S_HALF, S_SEL = 0, 8, 16, 24, 32
S_WIDTH = 64


def rows_of(t):
    return P if t < TT else B


def view(ap, *dims):
    return bass.AP(ap.tensor, ap.offset, [list(ap.ap[0])] + [list(d) for d in dims])


def dram(ap, offset, *dims):
    return bass.AP(ap.tensor, ap.offset + offset, [list(d) for d in dims])


def f32(ap):
    return ap.bitcast(F32)


class Chain:

    def __init__(self, engine, semaphore):
        self.engine, self.semaphore, self.n = engine, semaphore, 0

    def step(self, instruction):
        self.n += 1
        instruction.then_inc(self.semaphore, 1)
        return self.n

    def sync(self, n=None):
        self.engine.wait_ge(self.semaphore, n or self.n)


class Memory:

    def __init__(self, nc, at):
        self.nc, self.at = nc, at

    def put(self, name, shape, dtype=F32):
        size = (4 * int(np.prod(shape[1:])) + 31) // 32 * 32
        tensor = self.nc.alloc_sbuf_tensor_at(name, list(shape), dtype, offset=self.at)
        self.at += size
        return tensor


class Shared:

    def __init__(self, nc):
        self.nc, self.semaphores = nc, []

    def semaphore(self, name):
        self.semaphores.append(self.nc.alloc_semaphore(name=name))
        return self.semaphores[-1]


def between(nc, s):
    nc.all_engine_barrier()
    nc.clear_and_free_semaphores(s.semaphores)
    s.semaphores = []
    nc.all_engine_barrier()


def layout(nc, s):
    m = Memory(nc, 16512)
    s.ident = m.put("ident", [P, P])
    s.small = m.put("small", [P, S_WIDTH])
    s.gates = m.put("gates", [P, NT, 24])
    s.gain = m.put("gain", [P, 4])
    s.knew = m.put("knew", [P, 2, B])
    s.vnew = m.put("vnew", [P, 2, KVW])
    s.qfull = m.put("qfull", [P, B, H])
    m.at = 16512 + 3 * 1024
    s.kh = m.put("k_high", [P, 2, HKV, T], F32R)
    s.k_region = 16512 + 3 * 1024
    s.kl = m.put("k_low", [P, 2, HKV, T], F32R)
    s.v = m.put("v_nat", [P, 2, TT, KVW])
    s.rq_region = m.at
    s.qs = m.put("q_stack", [P, H, T], F32R)
    m.at = s.rq_region
    s.qr = m.put("q_ret", [P, NT, 512])
    s.kr = m.put("k_ret", [P, NT, 512])
    s.kct_region = m.at
    s.kct = m.put("kct", [P, 2, T])
    s.x_region = m.at
    s.xh = m.put("x_high", [P, KT, ROWS], F32R)
    s.xl = m.put("x_low", [P, KT, ROWS], F32R)
    s.w_region = m.at
    s.wraw = m.put("w_raw", [P, KT, 512])
    s.wh = m.put("w_high", [P, KT, 512], F32R)
    s.wl = m.put("w_low", [P, KT, 512], F32R)
    s.st_region = m.at
    s.st = m.put("stage", [P, 2, 512])
    s.sq = m.put("squares", [P, 512])
    s.stat = m.put("stats", [P, 64])
    assert m.at <= 229368, m.at


def normalise_x(nc, s, io):
    XS = 4
    m = Memory(nc, s.k_region)
    xt = m.put("x_tile", [P, XS, D])
    gain = m.put("norm_gain", [P, D])
    junk = m.put("x_squares", [P, D])
    relx = m.put("rel_bias_masked", [33, H])
    hot = m.put("one_hot", [33, L_TABLE])
    tab = m.put("bias_table", [H, L_TABLE])
    with ExitStack() as ctx:
        sem = s.semaphore
        x_in = [sem(f"x_in{b}") for b in range(XS)]
        const_in, ident_ready, sum_ready, mean_ready, root_ready = (
            sem("const_in"), sem("ident_ready"), sem("sum_ready"), sem("mean_ready"), sem("root_ready"))
        norm_ready, turned, high_ready, low_ready = (
            sem("norm_ready"), sem("turned"), sem("high_ready"), sem("low_ready"))
        own_steps = sem("x_own_steps")
        w_first, w_first_high = sem("w_first_in"), sem("w_first_high")
        hot_in, mask_set, tab_out, tab_kept, tab_stored = sem("one_hot_in"), sem("mask_set"), sem("tab_out"), sem("tab_kept"), sem("tab_stored")
        block = ctx.enter_context(nc.Block())

        @block.sync
        def _(sp):
            for t in range(NT):
                if t >= XS:
                    sp.wait_ge(turned, 2 * (t - XS + 1))
                src = io["xp"][P * t:P * t + P, :] if t < TT else io["xs"]
                sp.dma_start(xt[0:rows_of(t), t % XS, :], src).then_inc(x_in[t % XS], 16)
                if t == 0:
                    sp.dma_start(gain[:], dram(io["norm_g"], 0, [0, P], [1, D])).then_inc(const_in, 16)
                    sp.dma_start(s.small[:], io["c_small"]).then_inc(const_in, 16)
                    for half in range(2):
                        at = slice(HD * half, HD * half + HD)
                        sp.dma_start(s.gain[at, 0:1], dram(io["q_norm_g"], 0, [1, HD], [1, 1])).then_inc(const_in, 16)
                        sp.dma_start(s.gain[at, 1:2], dram(io["k_norm_g"], 0, [1, HD], [1, 1])).then_inc(const_in, 16)

            for k in range(KT):
                sp.dma_start(s.wraw[:, k, :], io["w_in"][P * k:P * k + P, C_QR:C_QR + 512]).then_inc(w_first, 16)
            sp.wait_ge(tab_kept, N_HOT)
            sp.dma_start(io["table"], tab[:]).then_inc(tab_stored, 16)
            sp.wait_ge(tab_stored, 16)
            sp.wait_ge(w_first, 16 * KT)

        @block.gpsimd
        def _(pool):
            nc.gpsimd.memset(relx[32:33, :], MASK).then_inc(mask_set, 1)
            pool.wait_ge(mask_set, 1)
            nc.gpsimd.memset(s.ident[:], 0.0).then_inc(ident_ready, 1)
            pool.wait_ge(ident_ready, 1)
            nc.gpsimd.affine_select(out=s.ident[:], in_=s.ident[:], compare_op=ALU.not_equal, fill=1.0, base=0,
                                    pattern=[[-1, P]], channel_multiplier=1).then_inc(ident_ready, 1)
            pool.wait_ge(const_in, 96)
            for t in range(NT):
                n = rows_of(t)
                pool.wait_ge(mean_ready, t + 1)
                nc.gpsimd.tensor_tensor(s.stat[0:n, 16 + t:17 + t], s.stat[0:n, 16 + t:17 + t],
                                        s.small[0:n, S_HALF:S_HALF + 1], ALU.pow).then_inc(root_ready, 1)

        @block.scalar
        def _(act):
            act.dma_start(relx[0:32, :], io["rel_bias"]).then_inc(hot_in, 16)
            act.dma_start(hot[:], io["c_hot"]).then_inc(hot_in, 16)
            def square(t):
                n = rows_of(t)
                act.wait_ge(x_in[t % XS], 16 * (t // XS + 1))
                if t >= 1:
                    act.wait_ge(sum_ready, t)
                nc.scalar.activation(junk[0:n, :], xt[0:n, t % XS, :], ACT.Square,
                                     accum_out=s.stat[0:n, t:t + 1]).then_inc(sum_ready, 1)

            def high(t):
                n = rows_of(t)
                for half in range(2):
                    i = 2 * t + half
                    act.wait_ge(turned, i + 1)
                    nc.scalar.activation(s.xh[:, 4 * half:4 * half + 4, P * t:P * t + n],
                                         view(s.ps[:, i % 4, 0:1], [P, 4], [1, n]), ACT.Copy).then_inc(high_ready, 1)

            for i in range(NT + 2):
                if i < NT:
                    square(i)
                if i >= 2:
                    high(i - 2)
            act.wait_ge(w_first, 16 * KT)
            for k in range(KT):
                nc.scalar.activation(s.wh[:, k, :], s.wraw[:, k, :], ACT.Copy).then_inc(w_first_high, 1)

        @block.vector
        def _(dve):
            own = Chain(dve, own_steps)
            dve.wait_ge(const_in, 96)
            own.step(nc.vector.tensor_scalar(s.gain[:, 0:1], s.gain[:, 0:1], HD ** -0.5, None, ALU.mult))
            def mean(t):
                n = rows_of(t)
                dve.wait_ge(sum_ready, t + 1)
                nc.vector.tensor_scalar(s.stat[0:n, 16 + t:17 + t], s.stat[0:n, t:t + 1], 1.0 / D, EPS,
                                        ALU.mult, ALU.add).then_inc(mean_ready, 1)

            def norm(t):
                n = rows_of(t)
                dve.wait_ge(root_ready, t + 1)
                x = xt[0:n, t % XS, :]
                nc.vector.scalar_tensor_tensor(x, x, s.stat[0:n, 16 + t:17 + t], gain[0:n, :],
                                               ALU.mult, ALU.mult).then_inc(norm_ready, 1)

            def low(t):
                n = rows_of(t)
                for half in range(2):
                    i = 2 * t + half
                    dve.wait_ge(high_ready, i + 1)
                    cols = (slice(None), slice(4 * half, 4 * half + 4), slice(P * t, P * t + n))
                    nc.vector.tensor_tensor(s.xl[cols], view(s.ps[:, i % 4, 0:1], [P, 4], [1, n]), f32(s.xh[cols]),
                                            ALU.subtract).then_inc(low_ready, 1)
                if t < N_HOT:
                    dve.wait_ge(tab_out, t + 1)
                    w = min(512, L_TABLE - 512 * t)
                    nc.vector.tensor_copy(tab[:, 512 * t:512 * t + w], s.ps[0:H, 6 + t % 2, 0:w]).then_inc(tab_kept, 1)

            for i in range(NT + 2):
                if i < NT:
                    mean(i)
                if 1 <= i <= NT:
                    norm(i - 1)
                if i >= 2:
                    low(i - 2)
            for k in range(KT):
                dve.wait_ge(w_first_high, k + 1)
                own.step(nc.vector.tensor_tensor(s.wl[:, k, :], s.wraw[:, k, :], f32(s.wh[:, k, :]), ALU.subtract))
            own.sync()
            dve.wait_ge(low_ready, 2 * NT)

        @block.tensor
        def _(pe):
            pe.wait_ge(ident_ready, 2)
            for t in range(NT):
                n = rows_of(t)
                pe.wait_ge(norm_ready, t + 1)
                for half in range(2):
                    i = 2 * t + half
                    if i >= 4:
                        pe.wait_ge(low_ready, i - 3)
                    for j in range(4):
                        k = 4 * half + j
                        last = nc.tensor.transpose(s.ps[:, i % 4, P * j:P * j + n],
                                                   xt[0:n, t % XS, P * k:P * k + P], s.ident[0:n, 0:n])
                    last.then_inc(turned, 1)
                if t < N_HOT:
                    if t == 0:
                        pe.wait_ge(hot_in, 32)
                        pe.wait_ge(mask_set, 1)
                    if t >= 2:
                        pe.wait_ge(tab_kept, t - 1)
                    w = min(512, L_TABLE - 512 * t)
                    nc.tensor.matmul(s.ps[0:H, 6 + t % 2, 0:w], relx[:], hot[:, 512 * t:512 * t + w], start=True, stop=True).then_inc(tab_out, 1)


def stores_of(kind, t):
    if kind == "zr" or kind == "zn":
        return 1
    if kind == "wg":
        return 2 if t >= TT - WIN // P else 0
    return 4 if kind == "kv" else 0


def project(nc, s, io):
    m = Memory(nc, s.k_region)
    rope = m.put("rope", [P, 2, NT, HD])
    dec = m.put("decay", [P, H, P])
    qdec = m.put("q_decay", [P, 4, P])
    gn = m.put("gn_gain", [P, 512])
    rot = m.put("rotated", [P, 2, 512])
    qt = m.put("qt", [P, 4, P])
    qdt = m.put("qt_decayed", [P, 4, P])
    ktz = m.put("kt_zeroed", [P, H, P])
    scd = m.put("scores", [P, H, P])
    kd = m.put("k_decayed", [P, 512])
    state = m.put("state", [P, H, HD])
    faded = m.put("state_faded", [P, H, HD])
    cen = m.put("centred", [P, 512])
    vr = Memory(nc, s.kct_region).put("v_ret", [P, 2, 512])
    assert m.at <= s.rq_region
    m.at = s.k_region
    last = Memory(nc, s.st_region + 4096 + 2048 + 256)
    kgain = last.put("k_gain", [P, HD])
    pet = last.put("pe_t", [P, 2, 32])
    assert last.at <= 229368
    qd = Memory(nc, s.w_region).put("q_doubled", [P, 2, D])
    n_idx = NG * NT
    G_ = {k: KIND.index(k) for k in KIND}
    kind_of = lambda i: KIND[i // NT]
    stored = [[0, 0]]
    for i in range(n_idx):
        c = list(stored[-1])
        c[i % 2] += stores_of(kind_of(i), i % NT)
        stored.append(c)
    with ExitStack() as ctx:
        sem = s.semaphore
        w_in = [sem(f"w_in{k}") for k in range(KT)]
        tables_in, w_high, w_low, w_used = sem("tables_in"), sem("w_high_ready"), sem("w_low_ready"), sem("w_used")
        projected, rows_in, = sem("projected"), sem("ret_rows_out")
        bank_free = [sem(f"bank_free{b}") for b in range(3)]
        st_stored = [sem(f"st_stored{b}") for b in range(2)]
        rot_ready, rot_added = sem("rot_ready"), sem("rot_added")
        r_turned, r_qt, r_qdt, r_scored, r_scd = (
            sem("r_turned"), sem("r_qt"), sem("r_qdt"), sem("r_scored"), sem("r_scd"))
        r_kd, r_faded, v_copied, r_out, r_grown, r_state = (
            sem("r_kd"), sem("r_faded"), sem("v_copied"), sem("r_out"), sem("r_grown"), sem("r_state"))
        cen_ready, gn_sq, gn_mean, gn_root, gn_done = (
            sem("cen_ready"), sem("gn_squared"), sem("gn_mean"), sem("gn_root"), sem("gn_done"))
        silu, y_ready, gates_raw = sem("silu_ready"), sem("y_ready"), sem("gates_raw")
        k_sq, k_mean, k_root, k_copied, k_norm = (
            sem("k_squared"), sem("k_mean"), sem("k_root"), sem("k_copied"), sem("k_normed"))
        k_turned, k_high, k_low = sem("k_turned"), sem("k_high_ready"), sem("k_low_ready")
        state_set, out_done = sem("state_set"), sem("p_stores")
        v_steps, a_steps = sem("p_v_steps"), sem("p_a_steps")
        block = ctx.enter_context(nc.Block())

        nq = rows_of
        norm_index = lambda kind, t: {"wg": 0, "kv": NT, "q": 2 * NT}[kind] + t

        @block.sync
        def _(sp):
            def load_w(g):
                for k in range(KT):
                    if g >= 2:
                        sp.wait_ge(w_low, KT * (g - 2) + k + 1)
                    _, c0, w = GROUPS[g]
                    sp.dma_start(s.wraw[:, k, 0:w], io["w_in"][P * k:P * k + P, c0:c0 + w]).then_inc(w_in[k], 16)
            sp.dma_start(rope[:], io["c_rope"].rearrange("p (a t d) -> p a t d", a=2, t=NT)).then_inc(tables_in, 16)
            sp.dma_start(dec[:], io["c_dec"].rearrange("p (h i) -> p h i", h=H)).then_inc(tables_in, 16)
            sp.dma_start(qdec[:], io["c_qdec"].rearrange("p (h i) -> p h i", h=4)).then_inc(tables_in, 16)
            sp.dma_start(gn[:], dram(io["ret_gn_g"], 0, [0, P], [1, 512])).then_inc(tables_in, 16)
            sp.dma_start(kgain[:], dram(io["k_norm_g"], 0, [0, P], [1, HD])).then_inc(tables_in, 16)
            for kv, pe_dram in enumerate((io["cmp_pe_k"], io["cmp_pe_v"])):
                for half in range(2):
                    sp.dma_start(pet[HD * half:HD * half + HD, kv, :],
                                 dram(pe_dram, 0, [1, HD], [HD, 32]),
                                 allow_slow_non_contiguous=True).then_inc(tables_in, 16)
            for g in range(NG):
                if g + 1 < NG:
                    load_w(g + 1)
                for t in range(NT):
                    i, kind, slot, n = g * NT + t, KIND[g], (g * NT + t) % 2, rows_of(t)
                    r0 = P * t
                    if g == 1 and t < H:
                        sp.dma_start(dram(io["skew"], t * L_SKEW, [L_FULL + 1, P], [1, L_FULL]),
                                     dram(io["table"], t * L_TABLE + O_FULL, [0, P], [1, L_FULL])).then_inc(out_done, 16)
                    if g == 3 and t < 2:
                        to, frm = ((io["s_win_k"], io["cache_win_k"]), (io["s_win_v"], io["cache_win_v"]))[t]
                        sp.dma_start(dram(to, 0, [WIN * KVW, B], [4088, 16], [1, 4088]),
                                     dram(frm, KVW, [WIN * KVW, B], [4088, 16], [1, 4088])).then_inc(out_done, 16)
                    if kind in ("qr", "kr") and t == TT:
                        sp.wait_ge(rot_added, i + 1)
                        src = s.qr if kind == "qr" else s.kr
                        sp.dma_start(io["ret_rows"][g], src[0:B, TT, :]).then_inc(rows_in, 16)
                    if kind == "vr" and t == TT:
                        sp.wait_ge(v_copied, NT)
                        sp.dma_start(io["ret_rows"][2], vr[0:B, t % 2, :]).then_inc(rows_in, 16)
                        sp.wait_ge(r_state, TT)
                        for e in range(2):
                            sp.dma_start(dram(io["p_ret"], e * HD * HD, [HD, HD], [2 * HD * HD, 4], [1, HD]),
                                         state[HD * e:HD * e + HD, e:H:2, :]).then_inc(out_done, 16)
                    if kind == "zr":
                        sp.wait_ge(y_ready, t + 1)
                        sp.dma_start(io["y"][r0:r0 + n, 512:1024], s.st[0:n, slot, :]).then_inc(st_stored[slot], 16)
                    if kind == "zn":
                        sp.wait_ge(silu, NT + t + 1)
                        sp.dma_start(io["zn"][r0:r0 + n, :], s.st[0:n, slot, :]).then_inc(st_stored[slot], 16)
                    if kind == "wg" and stores_of(kind, t):
                        sp.wait_ge(k_norm, norm_index(kind, t) + 1)
                        sp.wait_ge(k_copied, t + 1)
                        for j in range(2):
                            if t < TT:
                                to = (io["p_win_k"], io["p_win_v"])[j][r0 - (T - WIN):r0 - (T - WIN) + P, :]
                            else:
                                to = (io["s_win_k"], io["s_win_v"])[j][:, WIN - 1, :]
                            sp.dma_start(to, s.st[0:n, slot, KVW * j:KVW * j + KVW]).then_inc(st_stored[slot], 16)
                    if kind == "kv":
                        sp.wait_ge(k_norm, norm_index(kind, t) + 1)
                        sp.wait_ge(k_copied, NT + t + 1)
                        for j, name in enumerate(("cmp_k", "cmp_v", "slc_k", "slc_v")):
                            to = io["prompt_out"][name][r0:r0 + n, :] if t < TT else io["sample_out"][name]
                            sp.dma_start(to, s.st[0:n, slot, KVW * j:KVW * j + KVW]).then_inc(st_stored[slot], 16)
            sp.wait_ge(rows_in, 48)
            sp.wait_ge(out_done, 16 * (2 + H + 2))
            for slot in range(2):
                sp.wait_ge(st_stored[slot], 16 * stored[-1][slot])

        @block.gpsimd
        def _(pool):
            nc.gpsimd.memset(state[:], 0.0).then_inc(state_set, 1)
            nc.gpsimd.memset(ktz[:], 0.0).then_inc(state_set, 1)
            nc.gpsimd.memset(s.gates[:], 0.0).then_inc(state_set, 1)
            nc.gpsimd.memset(s.qfull[:], 0.0).then_inc(state_set, 1)

            def root(i, n, width, mean, done):
                pool.wait_ge(mean, i + 1)
                nc.gpsimd.tensor_tensor(s.stat[0:n, 8:8 + width], s.stat[0:n, 8:8 + width],
                                        view(s.small[0:n, S_HALF:S_HALF + 1], [0, width]), ALU.pow).then_inc(done, 1)

            for g in range(NG):
                for t in range(NT):
                    i, kind, n = g * NT + t, KIND[g], rows_of(t)
                    if kind in ("qr", "kr"):
                        pool.wait_ge(rot_ready, i + 1)
                        to = s.qr if kind == "qr" else s.kr
                        nc.gpsimd.tensor_tensor(to[0:n, t, :], rot[0:n, 0, :], rot[0:n, 1, :], ALU.add).then_inc(rot_added, 1)
                    if kind == "vr":
                        if t < TT:
                            if t == 0:
                                pool.wait_ge(rot_added, 2 * NT)
                                pool.wait_ge(state_set, 4)
                            else:
                                pool.wait_ge(r_grown, t)
                            nc.gpsimd.tensor_tensor(view(kd[:, 0:1], [HD, H], [1, HD]), view(s.kr[:, t, 0:1], [HD, H], [1, HD]),
                                                    view(s.small[:, S_KDEC:S_KDEC + 1], [1, H], [0, HD]), ALU.mult).then_inc(r_kd, 1)
                        if t >= 1:
                            c = t - 1
                            if c >= 1:
                                pool.wait_ge(r_state, c)
                            nc.gpsimd.tensor_tensor(faded[:], state[:],
                                                    view(s.small[:, S_GAM128:S_GAM128 + 1], [1, H], [0, HD]), ALU.mult).then_inc(r_faded, 1)
                            root(c, P, H, gn_mean, gn_root)
                            pool.wait_ge(gn_root, c + 1)
                            pool.wait_ge(r_qdt, c + 1)
                            nc.gpsimd.tensor_tensor(view(s.qr[:, c, 0:1], [HD, H], [1, HD]), view(cen[:, 0:1], [HD, H], [1, HD]),
                                                    view(s.stat[:, 8:9], [1, H], [0, HD]), ALU.mult).then_inc(gn_done, 1)
                    if kind in ("wg", "kv", "q"):
                        root(norm_index(kind, t), n, H if kind == "q" else HKV, k_mean, k_root)

        def post_evac_kind(i):
            return kind_of(i) in ("wg", "kv", "q")

        turns_before = lambda kind, t: {"wg": t, "kv": NT + 2 * t, "q": 3 * NT + 2 * t}[kind]

        @block.scalar
        def _(act):
            own = Chain(act, a_steps)

            def split_w(g):
                w = GROUPS[g][2]
                for k in range(KT):
                    act.wait_ge(w_in[k], 16 * g)
                    act.wait_ge(w_used, KT * (g - 1) + k + 1)
                    nc.scalar.activation(s.wh[:, k, 0:w], s.wraw[:, k, 0:w], ACT.Copy).then_inc(w_high, 1)

            def stage_free(i):
                if stored[i][i % 2]:
                    act.wait_ge(st_stored[i % 2], 16 * stored[i][i % 2])

            def evac(i):
                kind, t = kind_of(i), i % NT
                n, ps = rows_of(t), s.ps[0:rows_of(t), i % 3, :]
                if kind == "vr":
                    act.wait_ge(projected, i + 1)
                    if t >= 2:
                        act.wait_ge(r_grown, t - 1)
                    nc.scalar.activation(vr[0:n, t % 2, :], ps, ACT.Copy).then_inc(v_copied, 1)
                if kind in ("zr", "zn"):
                    act.wait_ge(projected, i + 1)
                    stage_free(i)
                    nc.scalar.activation(s.st[0:n, i % 2, :], ps, ACT.Silu).then_inc(silu, 1)
                if kind == "wg":
                    act.wait_ge(projected, i + 1)
                    if t == 0:
                        act.wait_ge(rows_in, 48)
                        act.wait_ge(out_done, 16 * (2 + H + 2))
                    stage_free(i)
                    if t >= 2:
                        act.wait_ge(k_turned, turns_before(kind, t - 1))
                    if norm_index(kind, t):
                        act.wait_ge(k_mean, norm_index(kind, t))
                    nc.scalar.activation(s.sq[0:n, 0:KVW], ps[:, 0:KVW], ACT.Square).then_inc(k_sq, 1)
                    nc.scalar.activation(s.gates[0:n, t, :], ps[:, 256:280], ACT.Copy).then_inc(gates_raw, 1)
                    v_to = s.v[:, 1, t, :] if t < TT else s.vnew[0:B, 1, :]
                    own.step(nc.scalar.activation(v_to, ps[:, KVW:2 * KVW], ACT.Copy))
                    nc.scalar.activation(s.st[0:n, i % 2, KVW:2 * KVW], ps[:, KVW:2 * KVW], ACT.Copy).then_inc(k_copied, 1)
                if kind == "kv":
                    act.wait_ge(projected, i + 1)
                    stage_free(i)
                    act.wait_ge(k_turned, turns_before(kind, t - 1) if t else NT)
                    if norm_index(kind, t):
                        act.wait_ge(k_mean, norm_index(kind, t))
                    nc.scalar.activation(s.sq[0:n, 0:KVW], ps[:, 2 * KVW:3 * KVW], ACT.Square).then_inc(k_sq, 1)
                    v_to = s.v[:, 0, t, :] if t < TT else s.vnew[0:B, 0, :]
                    own.step(nc.scalar.activation(v_to, ps[:, 3 * KVW:4 * KVW], ACT.Copy))
                    own.step(nc.scalar.activation(s.st[0:n, i % 2, 0:2 * KVW], ps[:, 0:2 * KVW], ACT.Copy))
                    own.sync()
                    nc.scalar.activation(s.st[0:n, i % 2, 3 * KVW:4 * KVW], ps[:, 3 * KVW:4 * KVW], ACT.Copy).then_inc(k_copied, 1)
                if kind == "q":
                    act.wait_ge(projected, i + 1)
                    act.wait_ge(k_mean, norm_index(kind, t))
                    if t == 0:
                        act.wait_ge(k_turned, 3 * NT - 2)
                    nc.scalar.activation(s.sq[0:n, :], ps, ACT.Square).then_inc(k_sq, 1)

            def high(bank, to, scale=1.0):
                nc.scalar.activation(to, bank, ACT.Copy, scale=scale).then_inc(k_high, 1)

            def post(i):
                kind, t = kind_of(i), i % NT
                b = turns_before(kind, t)
                cols = slice(P * t, P * t + P)
                if kind in ("wg", "kv"):
                    br = 1 if kind == "wg" else 0
                    act.wait_ge(k_turned, b + (1 if kind == "wg" else 2))
                    if t < TT:
                        bank = s.ps[:, 3 if kind == "wg" else 4, 0:2 * P]
                        high(view(bank, [P, 2], [1, P]), s.kh[:, br, :, cols])
                    else:
                        high(s.ps[:, 3 if kind == "wg" else 4, 0:B], s.knew[:, br, :])
                if kind == "q":
                    for half in range(2):
                        act.wait_ge(k_turned, b + (half + 1 if t < TT else 2))
                        if t < TT:
                            bank = view(s.ps[:, 3 + half, :], [P, 4], [1, P])
                            high(bank, s.qs[:, 4 * half:4 * half + 4, cols], s.gain[:, 0:1])
                        else:
                            at = slice(HD * half, HD * half + HD)
                            high(view(s.ps[at, 3, 0:1], [1, B], [B, G]),
                                 s.qfull[at, :, G * half:G * half + G], s.gain[at, 0:1])

            for g in range(NG):
                for t in range(NT):
                    i = g * NT + t
                    if t == TT and g + 1 < NG:
                        split_w(g + 1)
                    if KIND[g] == "vr" and t < TT:
                        act.wait_ge(r_turned, t + 1)
                        if t >= 1:
                            act.wait_ge(r_scored, 2 * t)
                        nc.scalar.activation(qt[:], view(s.ps[:, 3, :], [P, 4], [1, P]), ACT.Copy).then_inc(r_qt, 1)
                        for e in range(2):
                            at = slice(HD * e, HD * e + HD)
                            nc.scalar.activation(ktz[at, e:H:2, :], view(s.ps[at, 4, :], [P, 4], [1, P]), ACT.Copy).then_inc(r_qt, 1)
                    evac(i)
                    if KIND[g] == "vr" and t >= 1:
                        act.wait_ge(cen_ready, t)
                        nc.scalar.activation(s.sq[:], cen[:], ACT.Square).then_inc(gn_sq, 1)
                    if i >= 1 and post_evac_kind(i - 1):
                        post(i - 1)
            post(n_idx - 1)
            act.wait_ge(gates_raw, NT)
            own.step(nc.scalar.activation(s.gates[:], s.gates[:], ACT.Sigmoid))
            own.sync()

        @block.vector
        def _(dve):
            own = Chain(dve, v_steps)

            def split_w(g):
                w = GROUPS[g][2]
                for k in range(KT):
                    dve.wait_ge(w_high, KT * (g - 1) + k + 1)
                    nc.vector.tensor_tensor(s.wl[:, k, 0:w], s.wraw[:, k, 0:w], f32(s.wh[:, k, 0:w]),
                                            ALU.subtract).then_inc(w_low, 1)

            def evac(i):
                kind, t = kind_of(i), i % NT
                n, ps = rows_of(t), s.ps[0:rows_of(t), i % 3, :]
                free = bank_free[i % 3]
                if kind in ("qr", "kr"):
                    dve.wait_ge(projected, i + 1)
                    if i >= 1:
                        dve.wait_ge(rot_added, i)
                    own.step(nc.vector.tensor_tensor(view(rot[0:n, 0, :], [HD, H], [1, HD]), view(ps, [HD, H], [1, HD]),
                                                     view(rope[0:n, 0, t, :], [0, H], [1, HD]), ALU.mult))
                    for half in range(2):
                        a, o = 32 * half, 32 * (1 - half)
                        ins = nc.vector.tensor_tensor(view(rot[0:n, 1, a:a + 1], [HD, H], [1, 32]), view(ps[:, o:o + 1], [HD, H], [1, 32]),
                                                      view(rope[0:n, 1, t, a:a + 1], [0, H], [1, 32]), ALU.mult)
                        if half == 0:
                            own.step(ins)
                        else:
                            ins.then_inc(rot_ready, 1)
                    dve.wait_ge(rot_ready, i + 1)
                    dve.sem_inc(free, 1)
                if kind == "vr":
                    dve.wait_ge(v_copied, t + 1)
                    dve.sem_inc(free, 1)
                if kind == "zr":
                    dve.wait_ge(silu, t + 1)
                    dve.wait_ge(gn_done, TT)
                    st = s.st[0:n, i % 2, :]
                    if t < TT:
                        own.step(nc.vector.tensor_tensor(st, st, gn[0:n, :], ALU.mult))
                        own.sync()
                        ins = nc.vector.tensor_tensor(st, st, s.qr[:, t, :], ALU.mult)
                    else:
                        ins = nc.vector.tensor_tensor(st, st, gn[0:n, :], ALU.mult)
                    own.step(ins)
                    own.sync()
                    dve.sem_inc(y_ready, 1)
                    dve.sem_inc(free, 1)
                if kind == "zn":
                    dve.wait_ge(silu, NT + t + 1)
                    dve.sem_inc(free, 1)
                if kind in ("wg", "kv", "q"):
                    ni = norm_index(kind, t)
                    heads = H if kind == "q" else HKV
                    dve.wait_ge(k_sq, ni + 1)
                    if ni >= 1:
                        dve.wait_ge(k_root, ni)
                    own.sync()
                    own.step(nc.vector.tensor_reduce(s.stat[0:n, 0:heads], view(s.sq[0:n, 0:1], [HD, heads], [1, HD]), AX, ALU.add))
                    own.sync()
                    nc.vector.tensor_scalar(s.stat[0:n, 8:8 + heads], s.stat[0:n, 0:heads], 1.0 / HD, EPS,
                                            ALU.mult, ALU.add).then_inc(k_mean, 1)
                    dve.wait_ge(k_root, ni + 1)
                    if kind == "q":
                        if t >= 2:
                            dve.wait_ge(k_turned, turns_before(kind, t - 1))
                        if t < TT:
                            ins = nc.vector.tensor_tensor(view(qd[0:n, i % 2, :], [P, H], [HD, 2], [1, HD]), view(ps, [HD, H], [0, 2], [1, HD]),
                                                          view(s.stat[0:n, 8:9], [1, H], [0, 2], [0, HD]), ALU.mult)
                            own.step(ins)
                        else:
                            for h in range(HKV):
                                ins = nc.vector.tensor_tensor(view(qd[0:n, i % 2, HD * h:HD * h + 1], [P, G], [1, HD]),
                                                              view(ps[:, G * HD * h:G * HD * h + 1], [HD, G], [1, HD]),
                                                              view(s.stat[0:n, 8 + G * h:9 + G * h], [1, G], [0, HD]), ALU.mult)
                                own.step(ins)
                    else:
                        src, dst = (0, 0) if kind == "wg" else (2 * KVW, 2 * KVW)
                        dve.wait_ge(k_copied, t + 1 if kind == "wg" else NT + t + 1)
                        if stored[i][i % 2]:
                            dve.wait_ge(st_stored[i % 2], 16 * stored[i][i % 2])
                        if kind == "wg" and t >= 2:
                            dve.wait_ge(k_turned, turns_before(kind, t - 1))
                        if kind == "kv":
                            dve.wait_ge(k_turned, turns_before(kind, t - 1) if t else NT)
                        for h in range(HKV):
                            ins = nc.vector.scalar_tensor_tensor(
                                s.st[0:n, i % 2, dst + HD * h:dst + HD * h + HD], ps[:, src + HD * h:src + HD * h + HD],
                                s.stat[0:n, 8 + h:9 + h], kgain[0:n, :], ALU.mult, ALU.mult)
                            own.step(ins)
                            if t < TT:
                                if h == 0 and ni >= 1:
                                    dve.wait_ge(k_turned, turns_before(kind, t))
                                own.step(nc.vector.scalar_tensor_tensor(
                                    view(s.sq[0:n, 256 + P * h:257 + P * h], [HD, 2], [1, HD]), view(ps[:, src + HD * h:src + HD * h + 1], [0, 2], [1, HD]),
                                    s.stat[0:n, 8 + h:9 + h], view(kgain[0:n, :], [0, 2], [1, HD]), ALU.mult, ALU.mult))
                    own.sync()
                    dve.sem_inc(k_norm, 1)
                    dve.sem_inc(free, 1)

            def post(i):
                kind, t = kind_of(i), i % NT
                cols = slice(P * t, P * t + P)
                hi = {"wg": t, "kv": NT + t, "q": 2 * NT + 2 * t}[kind]
                if kind in ("wg", "kv"):
                    br = 1 if kind == "wg" else 0
                    if kind == "kv" and t < TT:
                        dve.wait_ge(k_turned, turns_before(kind, t) + 1)
                        for j in range(2):
                            own.step(nc.vector.tensor_tensor(
                                view(s.kct[:, j, 4 * t:4 * t + 1], [1, 4], [32, 32]), view(s.ps[:, 3, P * j:P * j + 1], [32, 4], [1, 32]),
                                view(pet[:, j, :], [0, 4], [1, 32]), ALU.add))
                        own.sync()
                    dve.wait_ge(k_high, hi + 1)
                    if t < TT:
                        bank = view(s.ps[:, 3 if kind == "wg" else 4, :], [P, 2], [1, P])
                        nc.vector.tensor_tensor(s.kl[:, br, :, cols], bank, f32(s.kh[:, br, :, cols]),
                                                ALU.subtract).then_inc(k_low, 1)
                    else:
                        dve.sem_inc(k_low, 1)
                if kind == "q":
                    for half in range(2):
                        dve.wait_ge(k_high, hi + half + 1)
                        if t < TT:
                            to = s.qs[HD:P, 4 * half:4 * half + 4, cols]
                            nc.vector.scalar_tensor_tensor(to, view(s.ps[HD:P, 3 + half, :], [P, 4], [1, P]), s.gain[HD:P, 0:1],
                                                           f32(to), ALU.mult, ALU.subtract).then_inc(k_low, 1)
                        else:
                            dve.sem_inc(k_low, 1)

            own.step(nc.vector.memset(s.stat[:], 0.0))
            own.sync()
            dve.wait_ge(tables_in, 144)
            for g in range(NG):
                for t in range(NT):
                    i = g * NT + t
                    if t == TT and g + 1 < NG:
                        split_w(g + 1)
                    if KIND[g] == "vr" and t < TT:
                        dve.wait_ge(r_turned, t + 1)
                        if t >= 1:
                            dve.wait_ge(r_out, t)
                        dve.wait_ge(r_qt, 3 * t + 1)
                        nc.vector.tensor_tensor(qdt[:], view(s.ps[:, 3, :], [P, 4], [1, P]), qdec[:], ALU.mult).then_inc(r_qdt, 1)
                    evac(i)
                    if KIND[g] == "vr":
                        if t < TT:
                            for e in range(2):
                                dve.wait_ge(r_scored, 2 * t + e + 1)
                                nc.vector.tensor_tensor(scd[:, e:H:2, :], view(s.ps[:, 5 + e, :], [P, 4], [1, P]),
                                                        dec[:, e:H:2, :], ALU.mult).then_inc(r_scd, 1)
                        if t >= 1:
                            retention_norm(nc, s, dve, own, cen, P, s.ps[:, 7, :], r_out, t, gn_done, t - 1, cen_ready, gn_sq, gn_mean)
                            dve.wait_ge(r_grown, t)
                            dve.wait_ge(r_faded, t)
                            for e in range(2):
                                at = slice(HD * e, HD * e + HD)
                                ins = nc.vector.tensor_tensor(state[at, e:H:2, :], faded[at, e:H:2, :],
                                                              view(s.ps[at, 3, HD * e:HD * e + 1], [P, 4], [1, HD]), ALU.add)
                                own.step(ins)
                            own.sync()
                            dve.sem_inc(r_state, 1)
                    if i >= 1 and post_evac_kind(i - 1):
                        post(i - 1)
            post(n_idx - 1)
            own.sync()
            dve.wait_ge(k_low, 4 * NT)

        @block.tensor
        def _(pe):
            def proj(i):
                g, t = i // NT, i % NT
                n, w = rows_of(t), GROUPS[g][2]
                if i >= 3:
                    pe.wait_ge(bank_free[i % 3], (i - 3) // 3 + 1)
                for k in range(KT):
                    if t == 0 and g >= 1:
                        pe.wait_ge(w_low, KT * (g - 1) + k + 1)
                    rows = slice(P * t, P * t + n)
                    out = s.ps[0:n, i % 3, 0:w]
                    nc.tensor.matmul(out, s.xh[:, k, rows], s.wh[:, k, 0:w], start=(k == 0), stop=False)
                    nc.tensor.matmul(out, s.xh[:, k, rows], s.wl[:, k, 0:w], start=False, stop=False)
                    ins = nc.tensor.matmul(out, s.xl[:, k, rows], s.wh[:, k, 0:w], start=False, stop=(k == KT - 1))
                    if t == TT and k < KT - 1:
                        ins.then_inc(w_used, 1)
                if t == TT:
                    ins.then_inc(w_used, 1)
                    pe.wait_ge(w_used, KT * (g + 1))
                    pe.sem_inc(projected, 1)
                else:
                    ins.then_inc(projected, 1)

            def turn_ret(t):
                pe.wait_ge(rot_added, 2 * NT)
                if t >= 1:
                    pe.wait_ge(r_state, t - 1) if t >= 2 else None
                    pe.wait_ge(r_qdt, t)
                    pe.wait_ge(r_qt, 3 * t)
                for bank, src in ((3, s.qr), (4, s.kr)):
                    for j in range(4):
                        last = nc.tensor.transpose(s.ps[:, bank, P * j:P * j + P], src[:, t, P * j:P * j + P], s.ident[:])
                last.then_inc(r_turned, 1)

            def score(t):
                pe.wait_ge(r_qt, 3 * (t + 1))
                if t >= 1:
                    pe.wait_ge(r_scd, 2 * t)
                else:
                    pe.wait_ge(state_set, 4)
                for e in range(2):
                    for j in range(4):
                        last = nc.tensor.matmul(s.ps[:, 5 + e, P * j:P * j + P], ktz[:, 2 * j + e, :], qt[:, j, :], start=True, stop=True)
                    last.then_inc(r_scored, 1)

            def out_ret(c):
                pe.wait_ge(v_copied, c + 1)
                pe.wait_ge(r_scd, 2 * (c + 1))
                pe.wait_ge(r_qdt, c + 1)
                if c >= 1:
                    pe.wait_ge(r_state, c)
                    pe.wait_ge(cen_ready, c)
                for h in range(H):
                    out = s.ps[:, 7, HD * h:HD * h + HD]
                    nc.tensor.matmul(out, scd[:, h, :], vr[:, c % 2, HD * h:HD * h + HD], start=True, stop=False)
                    last = nc.tensor.matmul(out, qdt[:, h // 2, :], state[:, h, :], start=False, stop=True)
                last.then_inc(r_out, 1)
                pe.wait_ge(r_kd, c + 1)
                if c + 1 < TT:
                    pe.wait_ge(r_qdt, c + 2)
                for j in range(4):
                    last = nc.tensor.matmul(s.ps[:, 3, P * j:P * j + P], kd[:, P * j:P * j + P], vr[:, c % 2, P * j:P * j + P],
                                            start=True, stop=True)
                last.then_inc(r_grown, 1)

            def post(i):
                kind, t = kind_of(i), i % NT
                n = rows_of(t)
                st = s.st[0:n, i % 2, :]
                one = s.ident[0:n, 0:n]
                pe.wait_ge(k_norm, norm_index(kind, t) + 1)
                low_before = {"wg": t, "kv": NT + t, "q": 2 * NT + 2 * t}[kind]
                if low_before:
                    pe.wait_ge(k_low, low_before)
                def doubled(bank, at, src):
                    return nc.tensor.transpose(s.ps[:, bank, at:at + P], src, one)
                if kind == "wg":
                    if t < TT:
                        for h in range(HKV):
                            last = doubled(3, P * h, s.sq[:, 256 + P * h:256 + P * h + P])
                    else:
                        last = nc.tensor.transpose(s.ps[:, 3, 0:B], st[:, 0:KVW], one)
                    last.then_inc(k_turned, 1)
                if kind == "kv":
                    for j in range(2):
                        last = nc.tensor.transpose(s.ps[:, 3, P * j:P * j + n], st[:, KVW * j:KVW * j + KVW], one)
                    last.then_inc(k_turned, 1)
                    if t < TT:
                        for h in range(HKV):
                            last = doubled(4, P * h, s.sq[:, 256 + P * h:256 + P * h + P])
                    else:
                        last = nc.tensor.transpose(s.ps[:, 4, 0:B], st[:, 2 * KVW:3 * KVW], one)
                    last.then_inc(k_turned, 1)
                if kind == "q":
                    if t < TT:
                        for half in range(2):
                            for j in range(4):
                                last = doubled(3 + half, P * j, qd[:, i % 2, P * (4 * half + j):P * (4 * half + j) + P])
                            last.then_inc(k_turned, 1)
                    else:
                        for j in range(G):
                            last = nc.tensor.transpose(s.ps[:, 3, B * j:B * j + B], qd[0:n, i % 2, P * j:P * j + P], one)
                            if j % 2:
                                last.then_inc(k_turned, 1)

            for i in range(n_idx):
                kind, t = kind_of(i), i % NT
                if kind == "vr" and t < TT:
                    turn_ret(t)
                proj(i)
                if kind == "vr":
                    if t < TT:
                        score(t)
                    if t >= 1:
                        out_ret(t - 1)
                if i >= 1 and post_evac_kind(i - 1):
                    post(i - 1)
            post(n_idx - 1)


def retention_norm(nc, s, dve, own, cen, n, bank, out_sem, out_value, free_sem, free_value, cen_ready, gn_sq, gn_mean):
    heads = lambda ap: view(ap, [HD, H], [1, HD])
    dve.wait_ge(out_sem, out_value)
    if free_value >= 1:
        dve.wait_ge(free_sem, free_value)
    own.step(nc.vector.tensor_reduce(s.stat[0:n, 0:H], heads(bank[0:n]), AX, ALU.add))
    own.sync()
    own.step(nc.vector.tensor_scalar(s.stat[0:n, 16:24], s.stat[0:n, 0:H], 1.0 / HD, None, ALU.mult))
    own.sync()
    nc.vector.tensor_tensor(heads(cen[0:n, 0:1]), heads(bank[0:n]), view(s.stat[0:n, 16:17], [1, H], [0, HD]),
                            ALU.subtract).then_inc(cen_ready, 1)
    dve.wait_ge(gn_sq, out_value)
    own.step(nc.vector.tensor_reduce(s.stat[0:n, 0:H], heads(s.sq[0:n, 0:1]), AX, ALU.add))
    own.sync()
    nc.vector.tensor_scalar(s.stat[0:n, 8:16], s.stat[0:n, 0:H], 1.0 / HD, EPS, ALU.mult, ALU.add).then_inc(gn_mean, 1)


SLOTS = 5
SP_PAGES, ACT_PAGES, POOL_PAGES = range(0, 3), range(3, 6), range(6, 8)


def persistent_compressed(nc, s):
    m = Memory(nc, s.kct_region)
    s.ck_h = m.put("ck_high", [P, HKV, NBP], F32R)
    s.ck_l = m.put("ck_low", [P, HKV, NBP], F32R)
    s.cv_bd = m.put("cv_blocks", [P, HKV, G, HD])
    s.cks = m.put("ck_sample", [P, NBS])
    s.cvs = m.put("cv_sample", [P, 2, KVW])
    s.d_region = m.at
    m.at = 229368 // 32 * 32 - 4 * P * (PAGES + 4) * (B + 2)
    s.vs_region = m.at
    s.vs = m.put("values", [P, B, PAGES + 4, KVW])
    s.kraw = m.put("keys_raw", [P, 2, PAGES + 4, P])


def compress(nc, s, io):
    m = Memory(nc, s.x_region)
    w1 = m.put("w1_blocks", [P, 2, CB, P])
    w2 = m.put("w2_blocks", [P, 2, P])
    kcs = m.put("kcs", [P, CB, NBS])
    raw = m.put("raw_pages", [P, SLOTS, PAGES, P])
    hid = m.put("hidden", [P, 2, NBS + NBP])
    pet = m.put("pe_t2", [P, 2, CB])
    kgain = m.put("k_gain2", [P, HD])
    pages = m.put("page_row", [1, B * PAGES], I32)
    sq = m.put("c_squares", [P, KVW])
    nat = m.put("ck_natural", [P, KVW])
    dup = m.put("ck_doubled", [P, HKV, 2, HD])
    stat = m.put("c_stats", [P, 16])
    cvd = m.put("cv_blocks_first", [P, HKV, G, HD])
    ckh = m.put("ck_high_first", [P, HKV, NBP], F32R)
    cks0 = m.put("ck_sample_first", [P, NBS])
    cvs0 = m.put("cv_sample_first", [P, 2, KVW])
    assert m.at <= s.vs_region + 4 * P * (PAGES + 4) * (B - 2), m.at
    pool_dram = [c.rearrange("n t h d -> n t (h d)") for c in (io["cache_cmp_k"], io["cache_cmp_v"])]
    with ExitStack() as ctx:
        sem = s.semaphore
        next_in, next_in_pool = sem("c_next_in"), sem("c_next_in_pool")
        raw_in_pool = [sem(f"c_raw_in_pool{b}") for b in range(SLOTS)]
        consts_in, codes_in, table_in, zeroed = sem("c_consts_in"), sem("c_codes_in"), sem("page_table_in"), sem("c_zeroed")
        raw_in = [sem(f"c_raw_in{b}") for b in range(SLOTS)]
        turned, evacuated, first_out, prompt_out, silu_out = sem("c_turned"), sem("c_evacuated"), sem("c_first_out"), sem("c_prompt_out"), sem("c_silu")
        second_out, squared, meaned, rooted = sem("c_second_out"), sem("c_squared"), sem("c_meaned"), sem("c_rooted")
        normed, key_turned, key_kept, value_kept = sem("c_normed"), sem("c_key_turned"), sem("c_key_kept"), sem("c_value_kept")
        key_high = sem("c_key_high")
        v_steps, a_steps = sem("c_v_steps"), sem("c_a_steps")
        block = ctx.enter_context(nc.Block())
        OUT_BANK = [6, 7, 5]
        tiles = [(P * j, P) for j in range(2)] + [(NBS, NBP)]

        def load_pages(engine, u, some, loaded=raw_in):
            kv, b = u // B, u % B
            if u == 0:
                engine.wait_ge(table_in, 16)
            if u >= SLOTS:
                engine.wait_ge(turned, 2 * (u - SLOTS + 1))
            for p in some:
                page = engine.value_load(pages[0:1, PAGES * b + p:PAGES * b + p + 1], min_val=0, max_val=N_PHYS - 1)
                engine.dma_start(raw[:, u % SLOTS, p, :],
                                 pool_dram[kv][bass.ds(page, 1), :, :].rearrange("a t c -> (a t) c")).then_inc(loaded[u % SLOTS], 16)

        def load_next(engine, tile, slot, b, cache, window, loaded=next_in):
            for p in range(PAGES):
                page = engine.value_load(pages[0:1, PAGES * b + p:PAGES * b + p + 1], min_val=0, max_val=N_PHYS - 1)
                engine.dma_start(tile[:, slot, p, :], cache.rearrange("n t h d -> n t (h d)")[bass.ds(page, 1), :, :]
                                 .rearrange("a t c -> (a t) c")).then_inc(loaded, 16)
            engine.dma_start(tile[:, slot, PAGES:PAGES + 4, :], window[b].rearrange("(a t) c -> t a c", t=P)).then_inc(loaded, 16)

        @block.sync
        def _(sp):
            sp.dma_start(pages[:], io["page_table"].rearrange("(a b) p -> a (b p)", a=1)).then_inc(table_in, 16)
            for kv, pe_dram in enumerate((io["cmp_pe_k"], io["cmp_pe_v"])):
                for half in range(2):
                    sp.dma_start(pet[HD * half:HD * half + HD, kv, :], dram(pe_dram, 0, [1, HD], [HD, CB]),
                                 allow_slow_non_contiguous=True).then_inc(codes_in, 16)
            sp.dma_start(kgain[:], dram(io["k_norm_g"], 0, [0, P], [1, HD])).then_inc(codes_in, 16)
            load_pages(sp, 0, SP_PAGES)
            load_pages(sp, 1, SP_PAGES)
            sp.wait_ge(zeroed, 3)
            for kv, (w1d, w2d) in enumerate(((io["cmp_w1_k"], io["cmp_w2_k"]), (io["cmp_w1_v"], io["cmp_w2_v"]))):
                for half in range(2):
                    at = slice(HD * half, HD * half + HD)
                    sp.dma_start(w1[at, kv, :, HD * half:HD * half + HD],
                                 dram(w1d, 0, [HD, HD], [HD * HD, CB], [1, HD])).then_inc(consts_in, 16)
                    sp.dma_start(w2[at, kv, HD * half:HD * half + HD], w2d).then_inc(consts_in, 16)
            for u in range(2, 2 * B):
                load_pages(sp, u, SP_PAGES)
            for b in range(2):
                load_next(sp, s.kraw, b, b, io["cache_slc_k"], io["cache_win_k"])
            sp.wait_ge(next_in, 16 * 3 * (PAGES + 1))

        @block.gpsimd
        def _(pool):
            for i, tile in enumerate((w1, w2, cvd)):
                if i:
                    pool.wait_ge(zeroed, i)
                nc.gpsimd.memset(tile[:], 0.0).then_inc(zeroed, 1)
            for u in range(B + SLOTS - 2):
                load_pages(pool, u, POOL_PAGES, raw_in_pool)
            for j, (_, n) in enumerate(tiles):
                pool.wait_ge(meaned, j + 1)
                nc.gpsimd.tensor_tensor(stat[0:n, 4:6], stat[0:n, 4:6], view(s.small[0:n, S_HALF:S_HALF + 1], [0, 2]),
                                        ALU.pow).then_inc(rooted, 1)
            for u in range(B + SLOTS - 2, 2 * B):
                load_pages(pool, u, POOL_PAGES, raw_in_pool)
            load_next(pool, s.vs, B - 1, B - 1, io["cache_slc_v"], io["cache_win_v"], next_in_pool)
            pool.wait_ge(next_in_pool, 16 * (PAGES + 1))

        @block.scalar
        def _(act):
            own = Chain(act, a_steps)
            for kv in range(2):
                for u in range(B + SLOTS - 2) if kv == 0 else range(B + SLOTS - 2, 2 * B):
                    load_pages(act, u, ACT_PAGES)
                if kv == 1:
                    load_next(act, s.vs, B - 2, B - 2, io["cache_slc_v"], io["cache_win_v"])
                act.wait_ge(prompt_out, 1)
                act.wait_ge(first_out, 2 * kv + 2)
                nc.scalar.activation(hid[:, kv, 0:NBS], s.ps[:, 4, 0:NBS], ACT.Silu).then_inc(silu_out, 1)
                if kv == 0:
                    nc.scalar.activation(hid[:, :, NBS:NBS + NBP], view(s.ps[:, 5, 0:1], [NBP, 2], [1, NBP]), ACT.Silu).then_inc(silu_out, 1)
                for j, (_, n) in enumerate(tiles):
                    act.wait_ge(second_out, 3 * kv + j + 1)
                    if kv == 0:
                        if j:
                            act.wait_ge(meaned, j)
                        nc.scalar.activation(sq[0:n, :], s.ps[0:n, OUT_BANK[j], 0:KVW], ACT.Square).then_inc(squared, 1)
                    elif j < 2:
                        nc.scalar.activation(cvs0[:, j, :], s.ps[:, OUT_BANK[j], 0:KVW], ACT.Copy).then_inc(value_kept, 1)
                    else:
                        act.wait_ge(zeroed, 3)
                        for g in range(G):
                            for h in range(HKV):
                                ins = nc.scalar.activation(cvd[NBP * g:NBP * g + NBP, h, g, :], s.ps[0:NBP, OUT_BANK[2], HD * h:HD * h + HD], ACT.Copy)
                                own.step(ins)
                        own.sync()
                        act.sem_inc(value_kept, 1)
                if kv == 0:
                    act.wait_ge(key_turned, 3)
                    nc.scalar.activation(ckh[:], view(s.ps[:, 3, 0:1], [P, HKV], [1, NBP]), ACT.Copy).then_inc(key_high, 1)
            act.wait_ge(first_out, 4)
            own.step(nc.scalar.activation(s.cvs[:], cvs0[:], ACT.Copy))
            own.step(nc.scalar.activation(s.cv_bd[:], cvd[:], ACT.Copy))
            own.sync()

        @block.vector
        def _(dve):
            own = Chain(dve, v_steps)
            dve.wait_ge(codes_in, 16 * 5)

            def norm_keys():
                for j, (_, n) in enumerate(tiles):
                    bank = s.ps[0:n, OUT_BANK[j], :]
                    dve.wait_ge(squared, j + 1)
                    if j:
                        dve.wait_ge(rooted, j)
                    own.sync()
                    own.step(nc.vector.tensor_reduce(stat[0:n, 0:2], view(sq[0:n, 0:1], [HD, 2], [1, HD]), AX, ALU.add))
                    own.sync()
                    nc.vector.tensor_scalar(stat[0:n, 4:6], stat[0:n, 0:2], 1.0 / HD, EPS, ALU.mult, ALU.add).then_inc(meaned, 1)
                    dve.wait_ge(rooted, j + 1)
                    if j == 1:
                        dve.wait_ge(key_turned, 1)
                    for h in range(HKV):
                        src = bank[:, HD * h:HD * h + HD]
                        if j < 2:
                            own.step(nc.vector.scalar_tensor_tensor(nat[0:n, HD * h:HD * h + HD], src, stat[0:n, 4 + h:5 + h],
                                                                    kgain[0:n, :], ALU.mult, ALU.mult))
                        else:
                            own.step(nc.vector.scalar_tensor_tensor(dup[0:n, h, :, :], view(src, [0, 2], [1, HD]), stat[0:n, 4 + h:5 + h],
                                                                    view(kgain[0:n, :], [0, 2], [1, HD]), ALU.mult, ALU.mult))
                    own.sync()
                    dve.sem_inc(normed, 1)
                    if j < 2:
                        dve.wait_ge(key_turned, j + 1)
                        nc.vector.tensor_copy(cks0[:, P * j:P * j + P], s.ps[:, 3, 0:P]).then_inc(key_kept, 1)

            for kv in range(2):
                for b in range(B):
                    u = B * kv + b
                    if kv == 1 and b % 4 == 0:
                        dve.wait_ge(first_out, b // 4 + 1)
                    for half in range(2):
                        i = 2 * u + half
                        dve.wait_ge(turned, i + 1)
                        nc.vector.tensor_tensor(view(kcs[:, 0, NBP * b + 16 * half:NBP * b + 16 * half + 1], [1, 16], [NBS, CB]),
                                                view(s.ps[:, i % 3, 0:1], [CB, 16], [1, CB]),
                                                view(pet[:, kv, 0:1], [0, 16], [1, CB]), ALU.add).then_inc(evacuated, 1)
                    if kv == 1 and b == 1:
                        norm_keys()
            dve.wait_ge(first_out, 4)
            dve.wait_ge(key_high, 1)
            own.step(nc.vector.tensor_tensor(s.ck_l[:], view(s.ps[:, 3, 0:1], [P, HKV], [1, NBP]), f32(ckh[:]), ALU.subtract))
            own.step(nc.vector.tensor_copy(s.ck_h[:], f32(ckh[:])))
            dve.wait_ge(key_kept, 2)
            own.step(nc.vector.tensor_copy(s.cks[:], cks0[:]))
            own.sync()

        @block.tensor
        def _(pe):
            def turn(u):
                pe.wait_ge(raw_in[u % SLOTS], 16 * (PAGES - len(POOL_PAGES)) * (u // SLOTS + 1))
                pe.wait_ge(raw_in_pool[u % SLOTS], 16 * len(POOL_PAGES) * (u // SLOTS + 1))
                for half in range(2):
                    i = 2 * u + half
                    if i >= 3:
                        pe.wait_ge(evacuated, i - 2)
                    for j in range(4):
                        last = nc.tensor.transpose(s.ps[:, i % 3, P * j:P * j + P], raw[:, u % SLOTS, 4 * half + j, :], s.ident[:])
                    last.then_inc(turned, 1)

            def second(kv):
                for j, (c0, n) in enumerate(tiles):
                    pe.wait_ge(silu_out, (1 if j < 2 else 2) if kv == 0 else 3)
                    nc.tensor.matmul(s.ps[0:n, OUT_BANK[j], 0:KVW], hid[:, kv, c0:c0 + n], w2[:, kv, :], start=True, stop=True).then_inc(second_out, 1)

            def turn_keys(j):
                pe.wait_ge(normed, j + 1)
                if j == 1:
                    pe.wait_ge(key_kept, 1)
                if j < 2:
                    nc.tensor.transpose(s.ps[:, 3, 0:P], nat[:], s.ident[:]).then_inc(key_turned, 1)
                else:
                    pe.wait_ge(key_kept, 2)
                    for h in range(HKV):
                        last = nc.tensor.transpose(s.ps[:, 3, P * h:P * h + NBP], dup[0:NBP, h, :, :].rearrange("p a d -> p (a d)"), s.ident[0:NBP, 0:NBP])
                    last.then_inc(key_turned, 1)

            def first(kv, half):
                cols = slice(NBS // 2 * half, NBS // 2 * (half + 1))
                pe.wait_ge(evacuated, 2 * B * kv + B * (half + 1))
                for i in range(CB):
                    last = nc.tensor.matmul(s.ps[:, 4, cols], w1[:, kv, i, :], kcs[:, i, cols], start=(i == 0), stop=(i == CB - 1))
                last.then_inc(first_out, 1)

            for kv in range(2):
                for b in range(B):
                    turn(B * kv + b)
                    if b == 4:
                        if kv == 0:
                            pe.wait_ge(consts_in, 16 * 8)
                            for j in range(2):
                                for i in range(CB):
                                    last = nc.tensor.matmul(s.ps[:, 5, NBP * j:NBP * j + NBP], w1[:, j, i, :], s.kct[:, j, CB * i:CB * i + NBP],
                                                            start=(i == 0), stop=(i == CB - 1))
                            last.then_inc(prompt_out, 1)
                        else:
                            pe.wait_ge(silu_out, 2)
                        first(kv, 0)
                    if kv == 1 and b == 1:
                        for j in range(2):
                            turn_keys(j)
                        turn_keys(2)
                if kv == 1:
                    pe.wait_ge(silu_out, 2)
                    pe.wait_ge(normed, 3)
                first(kv, 1)
                second(kv)


R_ = B * H


def attend_sample(nc, s, io):
    m = Memory(nc, s.d_region)
    qb = m.put("q_by_row", [P, B, R_])
    ptw = m.put("pt_window", [P, 4, R_])
    assert m.at <= s.x_region
    m.at = s.x_region
    ktr = m.put("keys_turned", [P, 2, T + WIN])
    bias = m.put("bias_sample", [R_, L_SAMPLE])
    so = Memory(nc, m.at).put("s_out", [2, B * 4 * HD])
    sc = m.put("logits", [R_, max(T + B + WIN + B, B * 4 * HD)])
    pc = m.put("p_compressed", [R_, 4, NBP])
    own_mask = m.put("own_mask", [R_, B])
    newb = m.put("bias_new", [R_, B])
    sel = m.put("selection", [R_, 4, 16])
    groups = m.put("group_sum", [R_, R_])
    order = m.put("block_order", [R_, 16])
    stat = m.put("d_stats", [R_, 24])
    pts = m.put("pt_selected", [P, PAGES, R_])
    ptn = m.put("pt_new", [B, 2, R_])
    ptc = m.put("pt_compressed", [P, 2, G, H])
    ot = m.put("o_turned", [P, R_])
    on = m.put("o_natural", [R_, 2, HD])
    ys = m.put("y_rows", [B, 2, 512])
    rs = m.put("s_state", [P, B, 4, HD])
    vb = m.put("s_v_spread", [P, B, 4, HD])
    qk = m.put("s_qk", [P, 2, B * 4])
    yr = m.put("s_y", [B, 3, 512])
    rstat = m.put("s_stats", [B, 32])
    pages = m.put("page_row2", [1, B * PAGES], I32)
    assert m.at <= s.vs_region, m.at
    kraw, vs = s.kraw, s.vs
    pools = [c.rearrange("n t h d -> n t (h d)") for c in (io["cache_slc_k"], io["cache_slc_v"])]
    wins = [io["cache_win_k"], io["cache_win_v"]]
    with ExitStack() as ctx:
        sem = s.semaphore
        small_in, page_in = sem("d_small_in"), sem("page_table_in2")
        k_in = [sem(f"d_keys_in{b}") for b in range(2)]
        v_in = [sem(f"d_values_in{b}") for b in range(B)]
        bias_in = sem("bias_in")
        gates_out, gates_in, qb_ready = sem("gates_out"), sem("gates_in"), sem("qb_ready")
        turned, evac_v, evac_a, scored = sem("d_turned"), sem("d_evac_v"), sem("d_evac_a"), sem("d_scored")
        c_scored, c_max, c_exp, c_norm, c_grouped = sem("c_scored"), sem("c_max"), sem("c_exp"), sem("c_norm"), sem("c_grouped")
        s_max, s_exp, s_scaled, p_turned, p_kept, zero_c = (
            sem("s_max"), sem("s_exp"), sem("s_scaled"), sem("p_turned"), sem("p_kept"), sem("zero_c"))
        o_out, o_kept, o_turned, o_sel, o_stored, y_in, y_done, y_stored = (
            sem("o_out"), sem("o_kept"), sem("o_turned"), sem("o_sel"), sem("o_stored"), sem("y_in"), sem("y_done"), sem("y_stored"))
        r_in, st_ready, st_out, pq_ready, summed, so_kept, so_out, o_in, mean, root, yr_ready, yr_out = (
            sem("e_in"), sem("e_state"), sem("e_state_out"), sem("e_pq"), sem("e_summed"), sem("e_kept"), sem("e_stored"),
            sem("e_o_in"), sem("e_mean"), sem("e_root"), sem("e_y"), sem("e_y_out"))
        v_steps = sem("d_v_steps")
        block = ctx.enter_context(nc.Block())
        N1, W0 = T, T + B

        def load_keys(engine, b, some):
            engine.wait_ge(turned, 3 * (b - 1))
            for p in some:
                page = engine.value_load(pages[0:1, PAGES * b + p:PAGES * b + p + 1], min_val=0, max_val=N_PHYS - 1)
                engine.dma_start(kraw[:, b % 2, p, :], pools[0][bass.ds(page, 1), :, :].rearrange("a t c -> (a t) c")).then_inc(k_in[b % 2], 16)

        def load_values(engine, b):
            for p in range(PAGES):
                page = engine.value_load(pages[0:1, PAGES * b + p:PAGES * b + p + 1], min_val=0, max_val=N_PHYS - 1)
                engine.dma_start(vs[:, b, p, :], pools[1][bass.ds(page, 1), :, :].rearrange("a t c -> (a t) c")).then_inc(v_in[b], 16)
            engine.dma_start(vs[:, b, PAGES:PAGES + 4, :], wins[1][b].rearrange("(a t) c -> t a c", t=P)).then_inc(v_in[b], 16)

        @block.sync
        def _(sp):
            sp.dma_start(pages[:], io["page_table"].rearrange("(a b) p -> a (b p)", a=1)).then_inc(page_in, 16)
            sp.dma_start(dram(io["scratch"], 0, [24, B], [1, 24]), s.gates[0:B, TT, :]).then_inc(gates_out, 16)
            sp.wait_ge(page_in, 16)
            for b in range(2, B):
                if b == 3:
                    sp.dma_start(own_mask[:], io["c_own"]).then_inc(small_in, 16)
                    sp.dma_start(groups[:], io["c_group"]).then_inc(small_in, 16)
                    sp.dma_start(order[:], io["c_order"]).then_inc(small_in, 16)
                    for r in range(B):
                        sp.dma_start(bias[H * r:H * r + H, :], io["table"][:, O_SLC:O_SLC + L_SAMPLE]).then_inc(bias_in, 16)
                    sp.wait_ge(gates_out, 16)
                    sp.dma_start(stat[:, 0:3], dram(io["scratch"], 0, [3, R_], [1, 3])).then_inc(gates_in, 16)
                load_keys(sp, b, range(0, 4))
                sp.dma_start(kraw[:, b % 2, PAGES:PAGES + 4, :], wins[0][b].rearrange("(a t) c -> t a c", t=P)).then_inc(k_in[b % 2], 16)
            for b in (2, 3):
                load_values(sp, b)
            sp.dma_start(ys[:, 1, :], io["zn"][T:ROWS, :]).then_inc(y_in, 16)
            sp.wait_ge(o_sel, 1)
            sp.dma_start(dram(io["scratch"], 65536, [HD, R_], [1, HD]), on[:, 0, :]).then_inc(o_stored, 16)
            sp.wait_ge(o_stored, 16)
            sp.dma_start(ys[:, 0, :], dram(io["scratch"], 65536, [512, B], [1, 512])).then_inc(y_in, 16)
            sp.wait_ge(y_done, 1)
            sp.dma_start(io["y"][T:ROWS, 0:512], ys[:, 0, :]).then_inc(y_stored, 16)
            sp.wait_ge(y_stored, 16)

        @block.gpsimd
        def _(pool):
            nc.gpsimd.memset(qb[:], 0.0).then_inc(zero_c, 1)
            nc.gpsimd.memset(ptc[:], 0.0).then_inc(zero_c, 1)
            state = lambda a, e, j: dram(a, (2 * j + e) * HD * HD, [HD, HD], [H * HD * HD, B], [1, HD])
            for j in range(2):
                pool.dma_start(qk[:, j, :], dram(io["ret_rows"], j * B * 512, [1, P], [P, B * 4]), allow_slow_non_contiguous=True).then_inc(r_in, 16)
            for e in range(2):
                at = slice(HD * e, HD * e + HD)
                for j in range(4):
                    pool.dma_start(rs[at, :, j, :], state(io["state_ret"], e, j)).then_inc(r_in, 16)
                    pool.dma_start(vb[at, :, j, :], dram(io["ret_rows"], 2 * B * 512 + P * j + HD * e, [0, HD], [512, B], [1, HD])).then_inc(r_in, 16)
            pool.dma_start(yr[:, 1, :], io["y"][T:ROWS, 512:1024]).then_inc(r_in, 16)
            pool.wait_ge(page_in, 16)
            for b in (4, 5):
                load_values(pool, b)
            pool.wait_ge(st_ready, 1)
            for e in range(2):
                at = slice(HD * e, HD * e + HD)
                for j in range(4):
                    pool.dma_start(state(io["s_ret"], e, j), rs[at, :, j, :]).then_inc(st_out, 16)
            pool.wait_ge(so_kept, 4)
            pool.dma_start(dram(io["scratch"], 2 * 65536, [2048, 2], [1, 2048]), so[:]).then_inc(so_out, 16)
            pool.wait_ge(so_out, 16)
            for e in range(2):
                pool.dma_start(view(yr[:, 0, HD * e:HD * e + 1], [P, 4], [1, HD]), dram(io["scratch"], 2 * 65536 + 2048 * e, [256, B], [HD, 4], [1, HD])).then_inc(o_in, 16)
            pool.wait_ge(mean, 1)
            nc.gpsimd.tensor_tensor(rstat[:, 16:24], rstat[:, 16:24], view(s.small[0:B, S_HALF:S_HALF + 1], [0, H]), ALU.pow).then_inc(root, 1)
            pool.wait_ge(yr_ready, 1)
            pool.dma_start(io["y"][T:ROWS, 512:1024], yr[:, 0, :]).then_inc(yr_out, 16)
            pool.wait_ge(yr_out, 16)
            pool.wait_ge(st_out, 16 * 8)
            pool.wait_ge(zero_c, 2)

        @block.scalar
        def _(act):
            act.wait_ge(page_in, 16)
            for b in range(B):
                act.wait_ge(turned, 3 * b + 2)
                if b >= 2:
                    act.wait_ge(scored, b - 1)
                nc.scalar.activation(ktr[:, b % 2, 512:1024], s.ps[:, 5, :], ACT.Copy).then_inc(evac_a, 1)
                if b + 2 < B:
                    load_keys(act, b + 2, range(4, 8))
                if b in (3, 4):
                    load_values(act, b - 3)
                if b == 5:
                    act.wait_ge(c_max, 1)
                    nc.scalar.activation(pc[:, 0, :], pc[:, 0, :], ACT.Exp, bias=stat[:, 4:5], accum_out=stat[:, 5:6]).then_inc(c_exp, 1)
            for j, (a, z) in enumerate(((0, W0), (W0, W0 + WIN + B))):
                act.wait_ge(s_max, j + 1)
                nc.scalar.activation(sc[:, a:z], sc[:, a:z], ACT.Exp, bias=stat[:, 6 + j:7 + j], accum_out=stat[:, 8 + j:9 + j]).then_inc(s_exp, 1)

        @block.vector
        def _(dve):
            own = Chain(dve, v_steps)
            step, sync, tt, ts = own.step, own.sync, nc.vector.tensor_tensor, nc.vector.tensor_scalar

            def retain():
                every = lambda ap: view(ap, [256, B], [HD, 4], [1, HD])
                of_row = lambda j: view(qk[:, j, 0:1], [1, 32], [0, HD])
                rows = lambda ap: view(ap, [HD, 32], [1, HD])
                rs0, vb0 = rs[:, 0, 0, 0:1], vb[:, 0, 0, 0:1]
                dve.wait_ge(r_in, 16 * 19)
                step(ts(qk[:, 1, :], qk[:, 1, :], HD ** -0.5, None, ALU.mult))
                step(tt(every(rs0), every(rs0), view(s.small[:, S_GAM1:S_GAM1 + 1], [0, B], [1, 4], [0, HD]), ALU.mult))
                sync()
                step(tt(rows(vb0), rows(vb0), of_row(1), ALU.mult))
                sync()
                tt(rows(rs0), rows(rs0), rows(vb0), ALU.add).then_inc(st_ready, 1)
                dve.wait_ge(st_ready, 1)
                tt(rows(vb0), rows(rs0), of_row(0), ALU.mult).then_inc(pq_ready, 1)
                for j in range(4):
                    dve.wait_ge(summed, j + 1)
                    nc.vector.tensor_copy(so[:, 512 * j:512 * j + 512], s.ps[0:2, 7, :]).then_inc(so_kept, 1)

            def retained_norm():
                heads = lambda ap: view(ap, [HD, H], [1, HD])
                o = yr[:, 0, :]
                dve.wait_ge(o_in, 32)
                step(nc.vector.tensor_reduce(rstat[:, 0:8], heads(o), AX, ALU.add))
                sync()
                step(ts(rstat[:, 8:16], rstat[:, 0:8], 1.0 / HD, None, ALU.mult))
                sync()
                step(tt(heads(o), heads(o), view(rstat[:, 8:9], [1, H], [0, HD]), ALU.subtract))
                sync()
                step(tt(yr[:, 2, :], o, o, ALU.mult))
                sync()
                step(nc.vector.tensor_reduce(rstat[:, 0:8], heads(yr[:, 2, :]), AX, ALU.add))
                sync()
                ts(rstat[:, 16:24], rstat[:, 0:8], 1.0 / HD, EPS, ALU.mult, ALU.add).then_inc(mean, 1)
                dve.wait_ge(root, 1)
                step(tt(heads(o), heads(o), view(rstat[:, 16:17], [1, H], [0, HD]), ALU.mult))
                sync()
                tt(o, o, yr[:, 1, :], ALU.mult).then_inc(yr_ready, 1)
                dve.wait_ge(yr_ready, 1)

            def compressed():
                dve.wait_ge(bias_in, 128)
                dve.wait_ge(small_in, 48)
                dve.wait_ge(gates_in, 16)
                dve.wait_ge(c_scored, 1)
                step(tt(pc[:, 0, :], s.ps[0:R_, 3, 16:16 + NBP], bias[:, L_SLC + L_SWIN:L_SLC + L_SWIN + NBP], ALU.add))
                sync()
                step(nc.vector.tensor_reduce(stat[:, 3:4], pc[:, 0, :], AX, ALU.max))
                sync()
                ts(stat[:, 4:5], stat[:, 3:4], -1.0, None, ALU.mult).then_inc(c_max, 1)
                dve.wait_ge(c_exp, 1)
                step(nc.vector.reciprocal(stat[:, 10:11], stat[:, 5:6]))
                sync()
                step(ts(pc[:, 1, :], pc[:, 0, :], stat[:, 10:11], None, ALU.mult))
                sync()
                dve.sem_inc(c_norm, 1)
                step(ts(pc[:, 2, :], pc[:, 1, :], stat[:, 0:1], None, ALU.mult))
                sync()
                step(nc.vector.tensor_copy(pc[:, 0, :], pc[:, 2, :]))
                step(nc.vector.tensor_copy(pc[:, 3, :], pc[:, 2, :]))
                dve.wait_ge(c_grouped, 1)
                step(nc.vector.tensor_reduce(sel[:, 0, :], view(s.ps[0:R_, 3, 64:65], [2, 16], [1, 2]), AX, ALU.add))
                sync()
                step(nc.vector.tensor_copy(pc[:, 1, :], pc[:, 2, :]))
                step(nc.vector.tensor_reduce(stat[:, 11:12], sel[:, 0, 1:15], AX, ALU.min))
                sync()
                step(ts(sel[:, 1, 1:15], sel[:, 0, 1:15], stat[:, 11:12], None, ALU.is_equal))
                sync()
                step(tt(sel[:, 2, 1:15], sel[:, 1, 1:15], order[:, 1:15], ALU.mult))
                sync()
                step(nc.vector.tensor_reduce(stat[:, 12:13], sel[:, 2, 1:15], AX, ALU.max))
                sync()
                step(ts(sel[:, 3, :], order[:], stat[:, 12:13], MASK, ALU.is_equal, ALU.mult))

            dve.wait_ge(zero_c, 2)
            nc.vector.tensor_copy(view(qb[:, 0, 0:1], [R_ + H, B], [1, H]), s.qfull[:]).then_inc(qb_ready, 1)
            for b in range(B):
                dve.wait_ge(turned, 3 * b + 1)
                if b >= 2:
                    dve.wait_ge(scored, b - 1)
                nc.vector.tensor_copy(ktr[:, b % 2, 0:512], s.ps[:, 4, :]).then_inc(evac_v, 1)
                dve.wait_ge(turned, 3 * b + 3)
                nc.vector.tensor_copy(ktr[:, b % 2, 1024:1536], s.ps[:, 6, :]).then_inc(evac_v, 1)
                if b == 3:
                    retain()
                if b == 5:
                    compressed()
            retained_norm()
            step(ts(newb[:], own_mask[:], bias[:, L_SAMPLE - 1:L_SAMPLE], None, ALU.add))
            sync()
            dve.wait_ge(scored, B)
            for j in range(2):
                step(tt(sc[:, 512 * j:512 * j + 512], s.ps[0:R_, j, :], bias[:, 512 * j:512 * j + 512], ALU.add))
            step(tt(sc[:, W0:W0 + WIN], s.ps[0:R_, 2, :], bias[:, L_SLC:L_SLC + WIN], ALU.add))
            dve.wait_ge(c_scored, 2)
            step(tt(sc[:, N1:N1 + B], s.ps[0:R_, 3, 0:B], newb[:], ALU.add))
            step(tt(sc[:, W0 + WIN:W0 + WIN + B], s.ps[0:R_, 3, B:2 * B], newb[:], ALU.add))
            sync()
            step(tt(view(sc[:, 0:1], [64, 16], [1, 64]), view(sc[:, 0:1], [64, 16], [1, 64]), view(sel[:, 3, 0:1], [1, 16], [0, 64]), ALU.add))
            sync()
            for j, (a, z) in enumerate(((0, W0), (W0, W0 + WIN + B))):
                step(nc.vector.tensor_reduce(stat[:, 13 + j:14 + j], sc[:, a:z], AX, ALU.max))
                sync()
                ts(stat[:, 6 + j:7 + j], stat[:, 13 + j:14 + j], -1.0, None, ALU.mult).then_inc(s_max, 1)
            for j, (a, z) in enumerate(((0, W0), (W0, W0 + WIN + B))):
                dve.wait_ge(s_exp, j + 1)
                step(nc.vector.reciprocal(stat[:, 15 + j:16 + j], stat[:, 8 + j:9 + j]))
                sync()
                ts(sc[:, a:z], sc[:, a:z], stat[:, 15 + j:16 + j], stat[:, 1 + j:2 + j], ALU.mult, ALU.mult).then_inc(s_scaled, 1)
            dve.wait_ge(p_turned, 1)
            step(nc.vector.tensor_copy(pts[:], view(s.ps[:, 4, 0:1], [R_, PAGES], [1, R_])))
            dve.wait_ge(p_turned, 2)
            step(nc.vector.tensor_copy(ptw[:], view(s.ps[:, 5, 0:1], [R_, 4], [1, R_])))
            step(nc.vector.tensor_copy(ptn[:], view(s.ps[0:B, 5, 256:257], [R_, 2], [1, R_])))
            for r in range(G):
                at = slice(NBP * r, NBP * r + NBP)
                step(nc.vector.tensor_copy(ptc[at, :, r, :], view(s.ps[at, 5, 384 + H * r:385 + H * r], [32, 2], [1, H])))
            sync()
            dve.sem_inc(p_kept, 1)
            dve.wait_ge(o_out, 1)
            nc.vector.tensor_copy(ot[:], s.ps[:, 7, 0:R_]).then_inc(o_kept, 1)
            dve.wait_ge(o_turned, 1)
            step(ts(on[:, 1, :], s.ps[0:R_, 6, 0:HD], s.small[0:R_, S_SEL + 2:S_SEL + 3], None, ALU.mult))
            sync()
            nc.vector.scalar_tensor_tensor(on[:, 0, :], s.ps[0:R_, 6, HD:2 * HD], s.small[0:R_, S_SEL + 3:S_SEL + 4], on[:, 1, :],
                                           ALU.mult, ALU.add).then_inc(o_sel, 1)
            dve.wait_ge(y_in, 32)
            tt(ys[:, 0, :], ys[:, 0, :], ys[:, 1, :], ALU.mult).then_inc(y_done, 1)
            dve.wait_ge(y_done, 1)

        @block.tensor
        def _(pe):
            pe.wait_ge(zero_c, 2)
            pe.wait_ge(qb_ready, 1)
            for b in range(B):
                last = nc.tensor.matmul(s.ps[0:R_, 3, 16:16 + NBP], qb[:, b, :], s.cks[:, NBP * b:NBP * b + NBP], start=(b == 0), stop=(b == B - 1))
            last.then_inc(c_scored, 1)
            for j in range(2):
                last = nc.tensor.matmul(s.ps[0:R_, 3, B * j:B * j + B], s.qfull[:].rearrange("p b h -> p (b h)"), s.knew[:, j, :], start=True, stop=True)
            last.then_inc(c_scored, 1)

            def turn(b):
                if b >= 2:
                    pe.wait_ge(k_in[b % 2], 16 * (PAGES + 1) * (b // 2))
                for part in range(3):
                    if b:
                        pe.wait_ge(evac_a if part == 1 else evac_v, b if part == 1 else 2 * b - (1 if part == 0 else 0))
                    for j in range(4):
                        last = nc.tensor.transpose(s.ps[:, 4 + part, P * j:P * j + P], kraw[:, b % 2, 4 * part + j, :], s.ident[:])
                    last.then_inc(turned, 1)

            def score(b):
                pe.wait_ge(evac_a, b + 1)
                pe.wait_ge(evac_v, 2 * b + 2)
                for part in range(3):
                    last = nc.tensor.matmul(s.ps[0:R_, part, :], qb[:, b, :], ktr[:, b % 2, 512 * part:512 * part + 512],
                                            start=(b == 0), stop=(b == B - 1))
                last.then_inc(scored, 1)

            turn(0)
            for b in range(B):
                if b + 1 < B:
                    turn(b + 1)
                score(b)
                if b == 2:
                    pe.wait_ge(pq_ready, 1)
                    flat = vb[:].rearrange("p b j d -> p (b j d)")
                    for j in range(4):
                        if j:
                            pe.wait_ge(so_kept, j)
                        nc.tensor.matmul(s.ps[0:2, 7, :], s.small[:, S_SEL:S_SEL + 2], flat[:, 512 * j:512 * j + 512], start=True, stop=True).then_inc(summed, 1)
                if b == 5:
                    pe.wait_ge(c_norm, 1)
                    pe.wait_ge(small_in, 48)
                    nc.tensor.matmul(s.ps[0:R_, 3, 64:64 + NBP], groups[:], pc[:, 1, :], start=True, stop=True).then_inc(c_grouped, 1)
            pe.wait_ge(so_kept, 4)
            pe.wait_ge(s_scaled, 1)
            for j in range(PAGES):
                last = nc.tensor.transpose(s.ps[:, 4, R_ * j:R_ * j + R_], sc[:, P * j:P * j + P], s.ident[0:R_, 0:R_])
            last.then_inc(p_turned, 1)
            pe.wait_ge(s_scaled, 2)
            for j in range(4):
                nc.tensor.transpose(s.ps[:, 5, R_ * j:R_ * j + R_], sc[:, W0 + P * j:W0 + P * j + P], s.ident[0:R_, 0:R_])
            for j, a in enumerate((N1, W0 + WIN)):
                nc.tensor.transpose(s.ps[0:B, 5, 256 + R_ * j:256 + R_ * j + R_], sc[:, a:a + B], s.ident[0:R_, 0:R_])
            nc.tensor.transpose(s.ps[:, 5, 384:384 + R_], pc[:].rearrange("p a c -> p (a c)"), s.ident[0:R_, 0:R_]).then_inc(p_turned, 1)
            pe.wait_ge(p_kept, 1)
            for b in range(B):
                if b < B - 2:
                    pe.wait_ge(v_in[b], 16 * (PAGES + 1))
                cols = slice(H * b, H * b + H)
                out = s.ps[:, 7, cols]
                for j in range(PAGES):
                    nc.tensor.matmul(out, vs[:, b, j, :], pts[:, j, cols], start=(j == 0), stop=False)
                for j in range(4):
                    nc.tensor.matmul(out, vs[:, b, PAGES + j, :], ptw[:, j, cols], start=False, stop=False)
                for j in range(2):
                    nc.tensor.matmul(out, s.vnew[0:B, j, :], ptn[:, j, cols], start=False, stop=False)
                last = nc.tensor.matmul(out, s.cvs[:, b // G, :], ptc[:, b // G, b % G, :], start=False, stop=True)
            last.then_inc(o_out, 1)
            pe.wait_ge(o_kept, 1)
            nc.tensor.transpose(s.ps[0:R_, 6, 0:P], ot[:], s.ident[:]).then_inc(o_turned, 1)


def attend_prompt(nc, s, io):
    RL, RP = 5, 3
    m = Memory(nc, s.x_region)
    full = m.put("bias_full", [P, H, T])
    wide = m.put("bias_window", [P, H, WIN + P])
    short = m.put("bias_short", [P, H, 2 * NBP])
    lg = m.put("unit_logits", [P, RL, T])
    pt = m.put("unit_pt", [P, RP, T])
    yt = m.put("y_tile", [P, 2, 512])
    zt = m.put("z_tile", [P, 2, 512])
    parts = m.put("branch_tiles", [P, 2, 2, 512])
    st = m.put("a_stats", [P, 128])
    relx = m.put("rel_bias_masked2", [33, H])
    assert m.at <= 229368, m.at
    hot = Memory(nc, s.x_region + 4 * H * T + 4 * H * (WIN + P) + 4 * H * 2 * NBP).put("one_hot2", [33, NBP * P])
    units = []
    for t in range(TT):
        units.append((t, "c", 0, 2))
        for h in range(H):
            units += [(t, "f", h, t + 1), (t, "w", h, min(t, WIN // P) + 1)]
    n_u = len(units)
    per_tile = 1 + 2 * H
    chunks = []
    first_chunk = []
    for u, (_, _, _, n) in enumerate(units):
        first_chunk.append(len(chunks))
        chunks += [(u, b0, min(4, n - b0)) for b0 in range(0, n, 4)]
    first_chunk.append(len(chunks))
    by_act = [k % 2 == 0 for k in range(len(chunks))]
    n_by = lambda k, act: sum(1 for j in range(k) if by_act[j] == act)
    fulls = lambda u: u // per_tile
    HALF = T // 2
    LB, LE, LC, LT, LP = 1, 2, 3, 3, 5
    in_turn = lambda u: 0 <= u < n_u

    with ExitStack() as ctx:
        sem = s.semaphore
        small_in, near_in, short_out, short_kept = sem("a_small_in"), sem("near_in"), sem("short_out"), sem("short_kept")
        far_in, wide_ready = sem("far_in"), sem("wide_ready")
        z_in = [sem(f"z_in{b}") for b in range(2)]
        scored, biased, exped, c_ready = sem("scored"), sem("biased"), sem("exped"), sem("c_ready")
        turned, kept_v, kept_a = sem("a_turned"), sem("kept_v"), sem("kept_a")
        weighed, c_used, tile_used = sem("weighed"), sem("c_used"), sem("tile_used")
        y_added, y_ready = sem("a_y_added"), sem("a_y_ready")
        y_out = [sem(f"a_y_out{b}") for b in range(2)]
        v_steps = sem("a_v_steps")
        block = ctx.enter_context(nc.Block())
        S_MIN = 0
        S_FW, S_SCALE = 8, 80

        @block.sync
        def _(sp):
            sp.dma_start(relx[0:32, :], io["rel_bias"]).then_inc(small_in, 16)
            sp.dma_start(hot[:], io["c_hot_cmp"]).then_inc(small_in, 16)
            rows = lambda h, first: io["skew"][bass.ds(h, 1), first:first + P * L_FULL].rearrange("a (p c) -> (a p) c", c=L_FULL)
            with sp.Fori(0, H) as h:
                sp.dma_start(full[:, bass.ds(h, 1), HALF:T].rearrange("p a c -> p (a c)"), rows(h, P - 1 + HALF)[:, 0:HALF]).then_inc(near_in, 16)
            with sp.Fori(0, H) as h:
                sp.dma_start(full[:, bass.ds(h, 1), 0:HALF].rearrange("p a c -> p (a c)"), rows(h, P - 1)[:, 0:HALF]).then_inc(far_in, 16)
            for t in range(TT):
                if t >= 2:
                    sp.wait_ge(y_ready, t - 1)
                sp.dma_start(zt[:, t % 2, :], io["zn"][P * t:P * t + P, :]).then_inc(z_in[t % 2], 16)
                if t >= 1:
                    sp.wait_ge(y_ready, t)
                    sp.dma_start(io["y"][P * (t - 1):P * t, 0:512], yt[:, (t - 1) % 2, :]).then_inc(y_out[(t - 1) % 2], 16)
            sp.wait_ge(y_ready, TT)
            sp.dma_start(io["y"][T - P:T, 0:512], yt[:, (TT - 1) % 2, :]).then_inc(y_out[(TT - 1) % 2], 16)
            for b in range(2):
                sp.wait_ge(y_out[b], 16 * TT // 2)

        @block.gpsimd
        def _(pool):
            nc.gpsimd.memset(relx[32:33, :], MASK).then_inc(short_kept, 1)
            pool.wait_ge(short_kept, 1)
            nc.gpsimd.memset(short[:], MASK).then_inc(short_kept, 1)
            pool.wait_ge(short_kept, 2)
            pool.wait_ge(near_in, 16 * H)
            pool.wait_ge(far_in, 16 * H)
            nc.gpsimd.tensor_copy(wide[:], full[:, :, T - WIN - P:T]).then_inc(wide_ready, 1)
            pool.wait_ge(wide_ready, 1)
            nc.gpsimd.affine_select(out=wide[:, :, 0:P], in_=wide[:, :, 0:P], compare_op=ALU.is_gt, fill=MASK, base=0,
                                    pattern=[[0, H], [1, P]], channel_multiplier=-1).then_inc(wide_ready, 1)
            pool.wait_ge(wide_ready, 2)
            for t in range(TT):
                y = yt[:, t % 2, :]
                pool.wait_ge(c_used, t + 1)
                pool.wait_ge(tile_used, t + 1)
                for j in range(2):
                    nc.gpsimd.tensor_tensor(y, y, parts[:, t % 2, j, :], ALU.add).then_inc(y_added, 1)
                    pool.wait_ge(y_added, 2 * t + j + 1)
                pool.wait_ge(z_in[t % 2], 16 * (t // 2 + 1))
                nc.gpsimd.tensor_tensor(y, y, zt[:, t % 2, :], ALU.mult).then_inc(y_ready, 1)
                pool.wait_ge(y_ready, t + 1)

        def keep(k, engine_wait, copy, done):
            u, b0, n = chunks[k]
            engine_wait(turned, k + 1)
            if u >= RP:
                engine_wait(weighed, u - RP + 1)
            copy(pt[:, u % RP, P * b0:P * b0 + P * n], s.ps[:, 4 + k % 2, 0:P * n]).then_inc(done, 1)

        @block.scalar
        def _(act):
            def exp(u):
                t, br, h, n = units[u]
                if br == "c":
                    act.wait_ge(c_ready, fulls(u) + 1)
                    nc.scalar.activation(lg[:, u % RL, 0:H * NBP], lg[:, u % RL, 0:H * NBP], ACT.Exp, scale=-1.0).then_inc(exped, 1)
                else:
                    at = S_FW + 2 * H * (t % 2) + (0 if br == "f" else H) + h
                    act.wait_ge(biased, u + 1)
                    if t >= 2 and h == 0:
                        act.wait_ge(tile_used, t - 1)
                    nc.scalar.activation(lg[:, u % RL, 0:P * n], lg[:, u % RL, 0:P * n], ACT.Exp, scale=-1.0,
                                         bias=st[:, S_MIN + u % RL:S_MIN + u % RL + 1], accum_out=st[:, at:at + 1]).then_inc(exped, 1)

            for i in range(n_u + LP):
                if in_turn(i - LE):
                    exp(i - LE)
                if in_turn(i - LT):
                    for k in range(first_chunk[i - LT], first_chunk[i - LT + 1]):
                        if by_act[k]:
                            keep(k, act.wait_ge, lambda out, in_: nc.scalar.activation(out, in_, ACT.Copy), kept_a)

        @block.vector
        def _(dve):
            own = Chain(dve, v_steps)
            step, sync, tt, ts = own.step, own.sync, nc.vector.tensor_tensor, nc.vector.tensor_scalar
            blocks = lambda ap: view(ap, [NBP, H], [1, NBP])
            heads = lambda ap: view(ap, [HD, H], [1, HD])
            per_head = lambda c: view(st[:, c:c + 1], [1, H], [0, HD])
            gate = lambda t, j: view(s.gates[:, t, j:j + 1], [3, H])

            def bias(u):
                t, br, h, n = units[u]
                dve.wait_ge(scored, u + 1)
                if u >= RL:
                    dve.wait_ge(turned, first_chunk[u - RL + 1])
                pair = s.ps[:, 2 * (u % 2):2 * (u % 2) + 2, :].rearrange("p a c -> p (a c)")
                if br == "c":
                    v0 = 4 * (TT - 1 - t)
                    l = lg[:, u % RL, 0:H * NBP]
                    step(nc.vector.scalar_tensor_tensor(blocks(l), blocks(pair), -1.0, view(short[:, 0, v0:v0 + 1], [2 * NBP, H], [1, NBP]),
                                                        ALU.mult, ALU.subtract))
                    sync()
                    dve.sem_inc(biased, 1)
                    step(nc.vector.tensor_reduce(st[:, 48:56], blocks(l), AX, ALU.min))
                    sync()
                    step(ts(st[:, 56:64], st[:, 48:56], -FLOOR, None, ALU.min))
                    sync()
                    tt(blocks(l), blocks(l), view(st[:, 56:57], [1, H], [0, NBP]), ALU.subtract).then_inc(c_ready, 1)
                else:
                    if P * t == HALF and h == 0:
                        if br == "f":
                            dve.wait_ge(far_in, 16 * H)
                        else:
                            dve.wait_ge(wide_ready, 2)
                    strip = full[:, h, T - P * n:T] if br == "f" or P * n <= WIN else wide[:, h, :]
                    nc.vector.tensor_tensor_reduce(out=lg[:, u % RL, 0:P * n], in0=pair[:, 0:P * n], in1=strip, scale=-1.0, scalar=-FLOOR,
                                                   op0=ALU.add, op1=ALU.min, accum_out=st[:, S_MIN + u % RL:S_MIN + u % RL + 1]).then_inc(biased, 1)

            def c_sums(u):
                dve.wait_ge(exped, u + 1)
                step(nc.vector.tensor_reduce(st[:, 64:72], blocks(lg[:, u % RL, 0:H * NBP]), AX, ALU.add))
                sync()
                step(ts(st[:, 64:72], st[:, 64:72], 1e-30, None, ALU.max))
                sync()
                step(nc.vector.reciprocal(st[:, 72:80], st[:, 64:72]))
                sync()
                step(tt(st[:, 72:80], st[:, 72:80], gate(units[u][0], 0), ALU.mult))
                sync()

            def c_out(u):
                t = units[u][0]
                dve.wait_ge(weighed, u + 1)
                if t >= 2:
                    dve.wait_ge(y_out[t % 2], 16 * (t // 2))
                tt(heads(yt[:, t % 2, :]), heads(s.ps[:, 7, :]), per_head(72), ALU.mult).then_inc(c_used, 1)

            def tile_end(t):
                u_last = per_tile * (t + 1) - 1
                c, r = S_FW + 2 * H * (t % 2), S_SCALE + 2 * H * (t % 2)
                dve.wait_ge(exped, u_last + 1)
                if t >= 2:
                    dve.wait_ge(y_ready, t - 1)
                step(nc.vector.reciprocal(st[:, r:r + 2 * H], st[:, c:c + 2 * H]))
                sync()
                step(tt(view(st[:, r:r + 1], [H, 2], [1, H]), view(st[:, r:r + 1], [H, 2], [1, H]),
                        view(s.gates[:, t, 1:2], [1, 2], [3, H]), ALU.mult))
                sync()
                dve.wait_ge(weighed, u_last + 1)
                for j in range(2):
                    step(tt(heads(parts[:, t % 2, j, :]), heads(s.ps[:, 6 + j, :]), per_head(r + H * j), ALU.mult))
                sync()
                dve.sem_inc(tile_used, 1)

            dve.wait_ge(short_kept, 2)
            dve.wait_ge(short_out, 1)
            step(nc.vector.tensor_copy(short[:, :, 0:NBP], view(s.ps[:, 0, 0:1], [1, H], [H, NBP])))
            sync()
            dve.sem_inc(short_kept, 1)
            dve.wait_ge(near_in, 16 * H)
            for i in range(n_u + LP + 1):
                if in_turn(i - LB):
                    bias(i - LB)
                if in_turn(i - LC) and units[i - LC][1] == "c":
                    c_sums(i - LC)
                if in_turn(i - LT):
                    for k in range(first_chunk[i - LT], first_chunk[i - LT + 1]):
                        if not by_act[k]:
                            keep(k, dve.wait_ge, nc.vector.tensor_copy, kept_v)
                v = i - LP
                if in_turn(v) and units[v][1] == "c":
                    c_out(v)
                if in_turn(v) and v % per_tile == per_tile - 1:
                    tile_end(units[v][0])
            dve.wait_ge(y_ready, TT)

        @block.tensor
        def _(pe):
            def score(u):
                t, br, h, n = units[u]
                if u >= 2:
                    pe.wait_ge(biased, u - 1)
                q = lambda h: s.qs[:, h, P * t:P * t + P]
                b0 = 2 * (u % 2)
                if br == "c":
                    for h in range(H):
                        out = s.ps[:, b0, NBP * h:NBP * h + NBP]
                        nc.tensor.matmul(out, q(h), s.ck_h[:, h // G, :], start=True, stop=False)
                        last = nc.tensor.matmul(out, q(h), s.ck_l[:, h // G, :], start=False, stop=True)
                    last.then_inc(scored, 1)
                    return
                j, k0 = (0, 0) if br == "f" else (1, P * (t + 1 - n))
                for c in range(0, P * n, 512):
                    w = min(512, P * n - c)
                    out = s.ps[:, b0 + c // 512, 0:w]
                    nc.tensor.matmul(out, q(h), s.kh[:, j, h // G, k0 + c:k0 + c + w], start=True, stop=False)
                    last = nc.tensor.matmul(out, q(h), s.kl[:, j, h // G, k0 + c:k0 + c + w], start=False, stop=True)
                last.then_inc(scored, 1)

            def turn(u):
                pe.wait_ge(exped, u + 1)
                for k in range(first_chunk[u], first_chunk[u + 1]):
                    if k >= 2:
                        j = k - 2
                        pe.wait_ge(kept_a if by_act[j] else kept_v, n_by(j, by_act[j]) + 1)
                    _, b0, n = chunks[k]
                    for b in range(n):
                        last = nc.tensor.transpose(s.ps[:, 4 + k % 2, P * b:P * b + P], lg[:, u % RL, P * (b0 + b):P * (b0 + b) + P], s.ident[:])
                    last.then_inc(turned, 1)

            def weigh(u):
                t, br, h, n = units[u]
                k = first_chunk[u + 1]
                pe.wait_ge(kept_a, n_by(k, True))
                if n_by(k, False):
                    pe.wait_ge(kept_v, n_by(k, False))
                if br == "c":
                    if t >= 1:
                        pe.wait_ge(tile_used, t)
                    for kv in range(HKV):
                        last = nc.tensor.matmul(s.ps[:, 7, 256 * kv:256 * kv + 256], pt[:, u % RP, P * kv:P * kv + P],
                                                s.cv_bd[:, kv, :, :].rearrange("p g d -> p (g d)"), start=True, stop=True)
                    last.then_inc(weighed, 1)
                    return
                if br == "w" and h == 0:
                    pe.wait_ge(c_used, t + 1)
                j = 0 if br == "f" else 1
                for b in range(n):
                    last = nc.tensor.matmul(s.ps[:, 6 + j, HD * h:HD * h + HD], pt[:, u % RP, P * b:P * b + P],
                                            s.v[:, j, t + 1 - n + b, HD * (h // G):HD * (h // G) + HD], start=(b == 0), stop=(b == n - 1))
                last.then_inc(weighed, 1)

            pe.wait_ge(small_in, 32)
            pe.wait_ge(short_kept, 2)
            for v in range(NBP):
                last = nc.tensor.matmul(s.ps[:, 0, H * v:H * v + H], hot[:, P * v:P * v + P], relx[:], start=True, stop=True)
            last.then_inc(short_out, 1)
            pe.wait_ge(short_kept, 3)
            for i in range(n_u + LP):
                if in_turn(i):
                    score(i)
                if in_turn(i - LT):
                    turn(i - LT)
                if in_turn(i - LP):
                    weigh(i - LP)


def project_out(nc, s, io):
    m = Memory(nc, s.k_region)
    yt = m.put("y_rows_in", [P, 2, D])
    xr = m.put("x_rows", [P, 2, 512])
    out = m.put("out_rows", [P, 2, 512])
    n_idx = 2 * NT
    with ExitStack() as ctx:
        sem = s.semaphore
        y_in = [sem(f"o_y_in{b}") for b in range(2)]
        x_in = [sem(f"o_x_in{b}") for b in range(2)]
        w_in = [sem(f"o_w_in{k}") for k in range(KT)]
        turned, y_high, y_low, w_high, w_low, w_used = sem("y_turned"), sem("o_y_high"), sem("o_y_low"), sem("o_w_high"), sem("o_w_low"), sem("o_w_used")
        projected, added = sem("o_projected"), sem("o_added")
        stored = [sem(f"o_stored{b}") for b in range(2)]
        block = ctx.enter_context(nc.Block())
        yh, yl = s.xh, s.xl

        @block.sync
        def _(sp):
            def load_w(g, some=range(KT)):
                for k in some:
                    if g:
                        sp.wait_ge(w_low, k + 1)
                    sp.dma_start(s.wraw[:, k, :], io["w_out"][P * k:P * k + P, 512 * g:512 * g + 512]).then_inc(w_in[k], 16)
            def load_y(t):
                if t >= 2:
                    sp.wait_ge(turned, 2 * (t - 1))
                sp.dma_start(yt[0:rows_of(t), t % 2, :], io["y"][P * t:P * t + rows_of(t), :]).then_inc(y_in[t % 2], 16)

            load_y(0)
            load_y(1)
            load_w(0, range(0, KT, 2))
            for i in range(n_idx + 1):
                if i + 2 < NT:
                    load_y(i + 2)
                if i == 1:
                    load_w(1)
                if i < n_idx:
                    g, t = i // NT, i % NT
                    if i >= 2:
                        sp.wait_ge(added, i - 1)
                    src = io["xp"][P * t:P * t + P, :] if t < TT else io["xs"]
                    sp.dma_start(xr[0:rows_of(t), i % 2, :], src[:, 512 * g:512 * g + 512]).then_inc(x_in[i % 2], 16)
                if i >= 1:
                    g, t = (i - 1) // NT, (i - 1) % NT
                    sp.wait_ge(added, i)
                    to = io["yp"][P * t:P * t + P, :] if t < TT else io["ys"]
                    sp.dma_start(to[:, 512 * g:512 * g + 512], out[0:rows_of(t), (i - 1) % 2, :]).then_inc(stored[(i - 1) % 2], 16)
            for b in range(2):
                sp.wait_ge(stored[b], 16 * NT)

        @block.scalar
        def _(act):
            def split_w(g):
                for k in range(KT):
                    act.wait_ge(w_in[k], 16 * (g + 1))
                    if g:
                        act.wait_ge(w_used, k + 1)
                    nc.scalar.activation(s.wh[:, k, :], s.wraw[:, k, :], ACT.Copy).then_inc(w_high, 1)
            for k in range(1, KT, 2):
                act.dma_start(s.wraw[:, k, :], io["w_out"][P * k:P * k + P, 0:512]).then_inc(w_in[k], 16)
            split_w(0)
            for t in range(NT):
                n = rows_of(t)
                for half in range(2):
                    i = 2 * t + half
                    act.wait_ge(turned, i + 1)
                    nc.scalar.activation(yh[:, 4 * half:4 * half + 4, P * t:P * t + n],
                                         view(s.ps[:, 4 + i % 4, 0:1], [P, 4], [1, n]), ACT.Copy).then_inc(y_high, 1)
            split_w(1)

        @block.vector
        def _(dve):
            def split_w(g):
                for k in range(KT):
                    dve.wait_ge(w_high, KT * g + k + 1)
                    nc.vector.tensor_tensor(s.wl[:, k, :], s.wraw[:, k, :], f32(s.wh[:, k, :]), ALU.subtract).then_inc(w_low, 1)

            def add(i):
                n = rows_of(i % NT)
                dve.wait_ge(projected, i + 1)
                dve.wait_ge(x_in[i % 2], 16 * (i // 2 + 1))
                if i >= 2:
                    dve.wait_ge(stored[i % 2], 16 * (i // 2))
                nc.vector.tensor_tensor(out[0:n, i % 2, :], s.ps[0:n, i % 4, :], xr[0:n, i % 2, :], ALU.add).then_inc(added, 1)

            split_w(0)
            for t in range(NT):
                n = rows_of(t)
                for half in range(2):
                    i = 2 * t + half
                    dve.wait_ge(y_high, i + 1)
                    cols = (slice(None), slice(4 * half, 4 * half + 4), slice(P * t, P * t + n))
                    nc.vector.tensor_tensor(yl[cols], view(s.ps[:, 4 + i % 4, 0:1], [P, 4], [1, n]), f32(yh[cols]),
                                            ALU.subtract).then_inc(y_low, 1)
                if t >= 2:
                    add(t - 2)
            split_w(1)
            for i in range(NT - 2, n_idx):
                add(i)
            dve.wait_ge(added, n_idx)

        @block.tensor
        def _(pe):
            def turn(t):
                n = rows_of(t)
                pe.wait_ge(y_in[t % 2], 16 * (t // 2 + 1))
                for half in range(2):
                    i = 2 * t + half
                    if i >= 4:
                        pe.wait_ge(y_low, i - 3)
                    for j in range(4):
                        k = 4 * half + j
                        last = nc.tensor.transpose(s.ps[:, 4 + i % 4, P * j:P * j + n], yt[0:n, t % 2, P * k:P * k + P], s.ident[0:n, 0:n])
                    last.then_inc(turned, 1)

            def proj(i):
                g, t = i // NT, i % NT
                n = rows_of(t)
                if i >= 4:
                    pe.wait_ge(added, i - 3)
                if g == 0:
                    pe.wait_ge(y_low, 2 * (t + 1))
                for k in range(KT):
                    if t == 0:
                        pe.wait_ge(w_low, KT * g + k + 1)
                    rows = slice(P * t, P * t + n)
                    to = s.ps[0:n, i % 4, :]
                    nc.tensor.matmul(to, yh[:, k, rows], s.wh[:, k, :], start=(k == 0), stop=False)
                    nc.tensor.matmul(to, yh[:, k, rows], s.wl[:, k, :], start=False, stop=False)
                    ins = nc.tensor.matmul(to, yl[:, k, rows], s.wh[:, k, :], start=False, stop=(k == KT - 1))
                    if t == TT and g == 0:
                        ins.then_inc(w_used, 1)
                if t == TT and g == 0:
                    pe.wait_ge(w_used, KT)
                    pe.sem_inc(projected, 1)
                else:
                    ins.then_inc(projected, 1)

            turn(0)
            turn(1)
            for i in range(n_idx):
                if i + 2 < NT:
                    turn(i + 2)
                proj(i)


def build(nc, io):
    s = Shared(nc)
    layout(nc, s)
    persistent_compressed(nc, s)
    with nc.psum_tensor("ps", [P, 8, 512], F32) as ps:
        s.ps = ps
        normalise_x(nc, s, io)
        between(nc, s)
        project(nc, s, io)
        between(nc, s)
        compress(nc, s, io)
        between(nc, s)
        attend_sample(nc, s, io)
        between(nc, s)
        attend_prompt(nc, s, io)
        between(nc, s)
        project_out(nc, s, io)


def bucket_one_hot(dist, masked):
    n = np.maximum(dist, 0)
    ratio = np.log(np.maximum(n, 1).astype(np.float32) / np.float32(16)) / np.float32(math.log(64))
    large = np.minimum(16 + (ratio * np.float32(16)).astype(np.int32), 31)
    bucket = np.where(masked, 32, np.where(n < 16, n, large))
    return (np.arange(33)[:, None] == bucket.reshape(1, -1)).astype(np.float32)


def constants():
    c = {}
    half = HD // 2
    inv = np.float32(10000.0) ** (-np.arange(half, dtype=np.float32) / np.float32(half))
    pos = np.minimum(np.arange(NT * P).reshape(NT, P).T, T).astype(np.float32)
    ang = pos[:, :, None] * inv.astype(np.float32)
    cos, sin = np.cos(ang), np.sin(ang)
    c["c_rope"] = np.stack([np.concatenate([cos, cos], -1), np.concatenate([-sin, sin], -1)], 1).reshape(P, -1)
    log_g = np.log1p(-np.exp2(-5.0 - np.arange(H)))
    i = np.arange(P)
    diff = i[None, :] - i[:, None]
    scale = HD ** -0.5
    dec = np.where(diff >= 0, np.exp(np.maximum(diff, 0)[None] * log_g[:, None, None]), 0.0) * scale
    c["c_dec"] = dec.transpose(1, 0, 2).reshape(P, -1)
    part_head = 2 * np.arange(4)[None, :] + (i[:, None] // HD)
    c["c_qdec"] = np.exp((i[None, None, :] + 1.0) * log_g[part_head][:, :, None]).reshape(P, -1)
    small = np.zeros((P, S_WIDTH))
    small[:, S_KDEC:S_KDEC + 8] = np.exp((P - 1.0 - i)[:, None] * log_g[None, :]) * scale
    small[:, S_GAM128:S_GAM128 + 8] = np.exp(P * log_g)[None, :]
    small[:, S_GAM1:S_GAM1 + 4] = np.exp(log_g)[part_head]
    small[:, S_HALF] = -0.5
    small[:, S_SEL] = i < HD
    small[:, S_SEL + 1] = i >= HD
    small[:, S_SEL + 2] = (i % 8) < G
    small[:, S_SEL + 3] = (i % 8) >= G
    c["c_small"] = small
    k = np.arange
    dist = np.concatenate([1023 - k(L_FULL), T - k(L_SLC), WIN - k(L_SWIN), T - (CB - 1) - CB * k(L_SCMP), 0 * k(32)])
    masked = dist < 0
    masked[O_SWIN:O_SWIN + L_SWIN] |= dist[O_SWIN:O_SWIN + L_SWIN] >= WIN
    c["c_hot"] = bucket_one_hot(dist, masked)
    dist = k(P)[None, :] - (CB - 1) + CB * (28 - k(NBP)[:, None])
    c["c_hot_cmp"] = bucket_one_hot(dist, dist < 0)
    row = k(R_) // H
    c["c_own"] = np.where(row[:, None] == k(B)[None, :], 0.0, MASK)
    c["c_group"] = (k(R_)[:, None] // G == k(R_)[None, :] // G)
    c["c_order"] = np.broadcast_to(k(16) + 1.0, (R_, 16))
    return {k: np.ascontiguousarray(v, dtype=np.float32) for k, v in c.items()}


_INS = ["x_prompt", "x_sample", "cache_cmp_k", "cache_cmp_v", "cache_slc_k", "cache_slc_v", "cache_win_k", "cache_win_v",
        "state_ret", "page_table", "norm_g", "w_in", "q_norm_g", "k_norm_g", "cmp_pe_k", "cmp_w1_k", "cmp_w2_k",
        "cmp_pe_v", "cmp_w1_v", "cmp_w2_v", "rel_bias", "ret_gn_g", "w_out"]
_KV1, _KVS = (1, T, HKV, HD), (B, 1, HKV, HD)
_OUTS = [("y_prompt", (1, T, D)), ("y_sample", (B, 1, D)),
         ("p_cmp_k", _KV1), ("p_cmp_v", _KV1), ("p_slc_k", _KV1), ("p_slc_v", _KV1),
         ("p_win_k", (1, WIN, HKV, HD)), ("p_win_v", (1, WIN, HKV, HD)), ("p_ret", (1, H, HD, HD)),
         ("s_cmp_k", _KVS), ("s_cmp_v", _KVS), ("s_slc_k", _KVS), ("s_slc_v", _KVS),
         ("s_win_k", (B, WIN, HKV, HD)), ("s_win_v", (B, WIN, HKV, HD)), ("s_ret", (B, H, HD, HD))]


def flat_rows(io):
    io["xp"] = io["x_prompt"].rearrange("a t d -> (a t) d")
    io["xs"] = io["x_sample"].rearrange("b s d -> (b s) d")
    prompt = lambda a: a.rearrange("a t h d -> (a t) (h d)")
    sample = lambda a: a.rearrange("b s h d -> (b s) (h d)")
    io["yp"], io["ys"] = io["y_prompt"].rearrange("a t d -> (a t) d"), io["y_sample"].rearrange("b s d -> (b s) d")
    parts = ("cmp_k", "cmp_v", "slc_k", "slc_v")
    io["prompt_out"] = {n: prompt(io["p_" + n]) for n in parts}
    io["sample_out"] = {n: sample(io["s_" + n]) for n in parts}
    io["p_win_k"], io["p_win_v"] = prompt(io["p_win_k"]), prompt(io["p_win_v"])
    window = lambda a: a.rearrange("b t h d -> b t (h d)")
    io["s_win_k"], io["s_win_v"] = window(io["s_win_k"]), window(io["s_win_v"])
    io["cache_win_k"], io["cache_win_v"] = window(io["cache_win_k"]), window(io["cache_win_v"])


def kernel(**inputs):
    import numpy as _np
    import concourse.bacc as _bacc
    from concourse import mybir as _mybir
    from concourse.bass_utils import run_bass_kernel_spmd as _run

    nc = _bacc.Bacc("TRN2", target_bir_lowering=False, num_devices=1)
    arrays, io = {}, {}
    for name, a in [(n, inputs[n]) for n in _INS] + list(constants().items()):
        a = _np.ascontiguousarray(a)
        arrays[f"in_{name}"] = a
        io[name] = (nc.dram_tensor(f"in_{name}", a.shape, _mybir.dt.from_np(a.dtype), kind="ExternalInput").ap())
    for name, shape in _OUTS:
        io[name] = (nc.dram_tensor(f"out_{name}", list(shape), F32, kind="ExternalOutput").ap())
    for name, shape in (("y", (ROWS, D)), ("zn", (ROWS, 512)), ("ret_rows", (3, B, 512)), ("scratch", (8, 65536)), ("table", (H, L_TABLE)), ("skew", (H, L_SKEW))):
        io[name] = (nc.dram_tensor(f"tmp_{name}", list(shape), F32).ap())
    flat_rows(io)
    build(nc, io)
    r = _run(nc, [arrays], core_ids=[0])
    return tuple(r.results[0][f"out_{name}"] for name, _ in _OUTS)
```
